# Optimizing a Trainium2 kernel written in Bass

```python
import math
import jax, jax.numpy as jnp
from jax import lax
import numpy as np
import jax
import jax.numpy as jnp

D_MODEL = 1024
BATCH = 1
SEQ = 256
DEPTH = 2

GRID_W = 64
CTX_LEN = 256
N_MIXERS = 4
Q_BLOCK = 128
ROPE_BASE = 10000.0
EPS = 1e-6
ADA_CHUNKS = 6

RET_HEADS = 4
RET_DK = D_MODEL // RET_HEADS
RET_DV = 2 * RET_DK
RET_CHUNK = 128

DIFF_HEADS = 8
DIFF_DH = D_MODEL // (2 * DIFF_HEADS)
DIFF_DV = 2 * DIFF_DH

NA_HEADS = 16
NA_DH = D_MODEL // NA_HEADS
NA_WIN_H = 8
NA_WIN_W = 16

MLA_HEADS = 16
MLA_Q_RANK = 256
MLA_KV_RANK = 128
MLA_NOPE = 64
MLA_ROPE = 32
MLA_V = 64
MLA_QK = MLA_NOPE + MLA_ROPE

FFN_HIDDEN = -(-8 * D_MODEL // (3 * 256)) * 256


def rms_norm(x):
    xf = x.astype(jnp.float32)
    return (xf * lax.rsqrt(jnp.mean(xf * xf, axis=-1, keepdims=True) + EPS)).astype(x.dtype)

def rms_norm_gain(x, g):
    return rms_norm(x) * g.astype(x.dtype)

def modulate(x, shift, scale):
    return rms_norm(x) * (1.0 + scale) + shift

def swiglu(h, w_in, w_out):
    a, g = jnp.split(h @ w_in, 2, axis=-1)
    return (jax.nn.silu(a) * g) @ w_out

def rope_2d(x):
    n, d = x.shape[1], x.shape[-1]
    half = d // 2
    quarter = half // 2
    pos = jnp.arange(n)
    row = (pos // GRID_W).astype(jnp.float32)
    col = (pos % GRID_W).astype(jnp.float32)
    inv_freq = jnp.power(ROPE_BASE, -jnp.arange(quarter, dtype=jnp.float32) / quarter)
    bshape = (n,) + (1,) * (x.ndim - 3) + (quarter,)

    def rot(t, p):
        ang = (p[:, None] * inv_freq[None, :]).reshape(bshape)
        cos, sin = jnp.cos(ang).astype(t.dtype), jnp.sin(ang).astype(t.dtype)
        t1, t2 = t[..., :quarter], t[..., quarter:]
        return jnp.concatenate([t1 * cos - t2 * sin, t2 * cos + t1 * sin], axis=-1)

    return jnp.concatenate([rot(x[..., :half], row), rot(x[..., half:], col)], axis=-1)

def map_query_blocks(fn, q):
    b, n = q.shape[0], q.shape[1]
    qb = jnp.moveaxis(q.reshape((b, n // Q_BLOCK, Q_BLOCK) + q.shape[2:]), 1, 0)
    out = jnp.moveaxis(lax.map(fn, qb), 0, 1)
    return out.reshape((b, n) + out.shape[3:])

def softmax_attend(q, k, v, scale):
    s = jnp.einsum('bqhd,bkhd->bhqk', q, k).astype(jnp.float32) * scale
    p = jax.nn.softmax(s, axis=-1).astype(v.dtype)
    return jnp.einsum('bhqk,bkhv->bqhv', p, v)

def chunk_retention(q, k, v, log_gamma, s0):
    b, n, h, _ = q.shape
    dv = v.shape[-1]
    nc = n // RET_CHUNK
    f32 = jnp.float32

    def chunks(t):
        return jnp.moveaxis(t.astype(f32).reshape(b, nc, RET_CHUNK, h, t.shape[-1]), 1, 0)

    idx = jnp.arange(RET_CHUNK, dtype=f32)
    rel = idx[:, None] - idx[None, :]
    d_intra = jnp.where(rel >= 0, jnp.exp(jnp.maximum(rel, 0.0) * log_gamma[:, None, None]), 0.0)
    d_cross = jnp.exp((idx + 1.0)[None, :] * log_gamma[:, None]).T[None, :, :, None]
    d_state = jnp.exp((RET_CHUNK - 1.0 - idx)[None, :] * log_gamma[:, None]).T[None, :, :, None]
    d_chunk = jnp.exp(RET_CHUNK * log_gamma)[None, :, None, None]

    def step(s, qkv):
        qc, kc, vc = qkv
        att = jnp.einsum('bihd,bjhd->bhij', qc, kc) * d_intra
        o = jnp.einsum('bhij,bjhv->bihv', att, vc) + jnp.einsum('bihd,bhdv->bihv', qc, s) * d_cross
        s = s * d_chunk + jnp.einsum('bjhd,bjhv->bhdv', kc * d_state, vc)
        return s, o

    _, o = lax.scan(step, s0.astype(f32), (chunks(q), chunks(k), chunks(v)))
    return jnp.moveaxis(o, 0, 1).reshape(b, n, h, dv)

def retention_output(o, g, norm_g, w_out):
    b, n, h, dv = o.shape
    of = o.astype(jnp.float32)
    mu = jnp.mean(of, axis=-1, keepdims=True)
    var = jnp.mean(jnp.square(of - mu), axis=-1, keepdims=True)
    on = ((of - mu) * lax.rsqrt(var + EPS)).astype(g.dtype).reshape(b, n, h * dv) * norm_g
    return (on * jax.nn.silu(g)) @ w_out

def retention_mixer(h_ctx, h_lat, w_in, decay_logit, norm_g, w_out, need_ctx):
    f32 = jnp.float32
    nqk = RET_HEADS * RET_DK
    splits = [nqk, 2 * nqk, 2 * nqk + RET_HEADS * RET_DV]

    def proj(h):
        b, n, _ = h.shape
        q, k, v, g = jnp.split(h @ w_in, splits, axis=-1)
        return (q.reshape(b, n, RET_HEADS, RET_DK),
                k.reshape(b, n, RET_HEADS, RET_DK) * (RET_DK ** -0.5),
                v.reshape(b, n, RET_HEADS, RET_DV), g)

    qc, kc, vc, gc = proj(h_ctx)
    ql, kl, vl, gl = proj(h_lat)
    ql, kl = rope_2d(ql), rope_2d(kl)
    log_gamma = jax.nn.log_sigmoid(decay_logit.astype(f32))
    lf, lb = log_gamma[0], log_gamma[1]
    n_ctx = h_ctx.shape[1]
    pos = jnp.arange(n_ctx, dtype=f32)
    kcf, vcf = kc.astype(f32), vc.astype(f32)
    w_f = jnp.exp((n_ctx - 1.0 - pos)[:, None] * lf[None, :])[None, :, :, None]
    w_b = jnp.exp(pos[:, None] * lb[None, :])[None, :, :, None]
    s_f = jnp.einsum('blhk,blhv->bhkv', kcf * w_f, vcf)
    s_b = jnp.einsum('blhk,blhv->bhkv', kcf * w_b, vcf)
    o_lat = (chunk_retention(ql, kl, vl, lf, s_f)
             + chunk_retention(ql[:, ::-1], kl[:, ::-1], vl[:, ::-1], lb, s_b)[:, ::-1])
    y_lat = retention_output(o_lat, gl, norm_g, w_out)
    if not need_ctx:
        return None, y_lat
    rel = pos[:, None] - pos[None, :]
    d_bi = (jnp.where(rel >= 0, jnp.exp(jnp.maximum(rel, 0.0) * lf[:, None, None]), 0.0)
            + jnp.where(rel <= 0, jnp.exp(jnp.maximum(-rel, 0.0) * lb[:, None, None]), 0.0))
    att = jnp.einsum('bihd,bjhd->bhij', qc.astype(f32), kcf) * d_bi
    o_ctx = jnp.einsum('bhij,bjhv->bihv', att, vcf)
    return retention_output(o_ctx, gc, norm_g, w_out), y_lat

def diff_attend(q, k, v, lam, scale):
    s = jnp.einsum('bqhmd,bkhmd->bhmqk', q, k).astype(jnp.float32) * scale
    p = jax.nn.softmax(s, axis=-1)
    p = p[:, :, 0] - lam * p[:, :, 1]
    return jnp.einsum('bhqk,bkhv->bqhv', p.astype(v.dtype), v)

def diff_attention_mixer(h_ctx, h_lat, w_in, q_norm_g, k_norm_g, lam_vecs, subln_g, w_out,
                         lambda_init, need_ctx):
    nq = DIFF_HEADS * 2 * DIFF_DH

    def proj(h):
        b, n, _ = h.shape
        q, k, v = jnp.split(h @ w_in, [nq, 2 * nq], axis=-1)
        q = rms_norm_gain(q.reshape(b, n, DIFF_HEADS, 2, DIFF_DH), q_norm_g)
        k = rms_norm_gain(k.reshape(b, n, DIFF_HEADS, 2, DIFF_DH), k_norm_g)
        return q, k, v.reshape(b, n, DIFF_HEADS, DIFF_DV)

    qc, kc, vc = proj(h_ctx)
    ql, kl, vl = proj(h_lat)
    ql, kl = rope_2d(ql), rope_2d(kl)
    lv = lam_vecs.astype(jnp.float32)
    lam = jnp.exp(jnp.sum(lv[0] * lv[1])) - jnp.exp(jnp.sum(lv[2] * lv[3])) + lambda_init
    scale = DIFF_DH ** -0.5

    def out(o):
        b, n = o.shape[0], o.shape[1]
        o = rms_norm_gain(o, subln_g) * (1.0 - lambda_init)
        return o.reshape(b, n, DIFF_HEADS * DIFF_DV) @ w_out

    k_all = jnp.concatenate([kc, kl], axis=1)
    v_all = jnp.concatenate([vc, vl], axis=1)
    y_lat = out(map_query_blocks(lambda qb: diff_attend(qb, k_all, v_all, lam, scale), ql))
    if not need_ctx:
        return None, y_lat
    return out(diff_attend(qc, kc, vc, lam, scale)), y_lat

def neighborhood_mixer(h_ctx, h_lat, w_in, q_norm_g, k_norm_g, rel_bias, w_out, need_ctx):
    def proj(h):
        b, n, _ = h.shape
        q, k, v = jnp.split(h @ w_in, 3, axis=-1)
        q = rms_norm_gain(q.reshape(b, n, NA_HEADS, NA_DH), q_norm_g)
        k = rms_norm_gain(k.reshape(b, n, NA_HEADS, NA_DH), k_norm_g)
        return q, k, v.reshape(b, n, NA_HEADS, NA_DH)

    qc, kc, vc = proj(h_ctx)
    ql, kl, vl = proj(h_lat)
    scale = NA_DH ** -0.5
    b, n = ql.shape[0], ql.shape[1]
    rows = n // GRID_W
    wh = min(NA_WIN_H, rows)
    n_loc = wh * NA_WIN_W

    def grid(t):
        return t.reshape(b, rows, GRID_W, NA_HEADS, NA_DH)

    kg, vg = grid(kl), grid(vl)
    col = np.arange(GRID_W)
    col_start = np.clip(col - NA_WIN_W // 2, 0, GRID_W - NA_WIN_W)
    col_idx = col_start[:, None] + np.arange(NA_WIN_W)[None, :]
    dc_idx = col_idx - col[:, None] + (NA_WIN_W - 1)

    def row_block(args):
        r, q_row = args
        r0 = jnp.clip(r - NA_WIN_H // 2, 0, rows - wh)
        k_win = lax.dynamic_slice_in_dim(kg, r0, wh, axis=1)[:, :, col_idx]
        v_win = lax.dynamic_slice_in_dim(vg, r0, wh, axis=1)[:, :, col_idx]
        dr_idx = r0 + jnp.arange(wh) - r + (NA_WIN_H - 1)
        bias = rel_bias[:, dr_idx[:, None, None], dc_idx[None, :, :]].transpose(0, 2, 1, 3)
        s_loc = (jnp.einsum('bqhd,brqwhd->bhqrw', q_row, k_win).astype(jnp.float32) * scale
                 + bias.astype(jnp.float32))
        s_ctx = jnp.einsum('bqhd,bkhd->bhqk', q_row, kc).astype(jnp.float32) * scale
        s = jnp.concatenate([s_loc.reshape(b, NA_HEADS, GRID_W, n_loc), s_ctx], axis=-1)
        p = jax.nn.softmax(s, axis=-1).astype(v_win.dtype)
        p_loc = p[..., :n_loc].reshape(b, NA_HEADS, GRID_W, wh, NA_WIN_W)
        return (jnp.einsum('bhqrw,brqwhv->bqhv', p_loc, v_win)
                + jnp.einsum('bhqk,bkhv->bqhv', p[..., n_loc:], vc))

    o = lax.map(row_block, (jnp.arange(rows), jnp.moveaxis(grid(ql), 1, 0)))
    y_lat = jnp.moveaxis(o, 0, 1).reshape(b, n, NA_HEADS * NA_DH) @ w_out
    if not need_ctx:
        return None, y_lat
    y_ctx = softmax_attend(qc, kc, vc, scale).reshape(b, -1, NA_HEADS * NA_DH) @ w_out
    return y_ctx, y_lat

def split_qk_norm(t, g):
    return jnp.concatenate([rms_norm(t[..., :MLA_NOPE]), rms_norm(t[..., MLA_NOPE:])], axis=-1) * g.astype(t.dtype)

def rotate_rope_part(t):
    return jnp.concatenate([t[..., :MLA_NOPE], rope_2d(t[..., MLA_NOPE:])], axis=-1)

def mla_mixer(h_ctx, h_lat, w_down, q_norm_g, kv_norm_g, w_uq, w_ukv, qk_norm_q, qk_norm_k,
              w_out, need_ctx):
    def keys_values(z, rotate):
        b, n, _ = z.shape
        c_kv = z[..., MLA_Q_RANK:MLA_Q_RANK + MLA_KV_RANK]
        k_rope = z[..., MLA_Q_RANK + MLA_KV_RANK:]
        kv = (rms_norm_gain(c_kv, kv_norm_g) @ w_ukv).reshape(b, n, MLA_HEADS, MLA_NOPE + MLA_V)
        k_rope = jnp.broadcast_to(k_rope[:, :, None, :], (b, n, MLA_HEADS, MLA_ROPE))
        k = split_qk_norm(jnp.concatenate([kv[..., :MLA_NOPE], k_rope], axis=-1), qk_norm_k)
        return (rotate_rope_part(k) if rotate else k), kv[..., MLA_NOPE:]

    def queries(z, rotate):
        b, n, _ = z.shape
        q = (rms_norm_gain(z[..., :MLA_Q_RANK], q_norm_g) @ w_uq).reshape(b, n, MLA_HEADS, MLA_QK)
        q = split_qk_norm(q, qk_norm_q)
        return rotate_rope_part(q) if rotate else q

    scale = MLA_QK ** -0.5
    z_ctx = h_ctx @ w_down
    z_lat = h_lat @ w_down
    kc, vc = keys_values(z_ctx, False)
    kl, vl = keys_values(z_lat, True)
    ql = queries(z_lat, True)
    k_all = jnp.concatenate([kc, kl], axis=1)
    v_all = jnp.concatenate([vc, vl], axis=1)
    b, n = ql.shape[0], ql.shape[1]
    o = map_query_blocks(lambda qb: softmax_attend(qb, k_all, v_all, scale), ql)
    y_lat = o.reshape(b, n, MLA_HEADS * MLA_V) @ w_out
    if not need_ctx:
        return None, y_lat
    o_ctx = softmax_attend(queries(z_ctx, False), kc, vc, scale)
    return o_ctx.reshape(b, -1, MLA_HEADS * MLA_V) @ w_out, y_lat

def first_inputs(seed: int = 0) -> dict:
    key = jax.random.key(seed)
    keys = iter(jax.random.split(key, 40))
    f32 = jnp.float32

    def normal(shape, scale):
        return jax.random.normal(next(keys), shape, f32) * scale

    def gain(shape):
        return 1.0 + normal(shape, 0.02)

    d = D_MODEL
    n_ret, n_diff, n_na, n_mla = [len(range(m, DEPTH, N_MIXERS)) for m in range(N_MIXERS)]
    gam = 1.0 - 2.0 ** (-5.0 - np.arange(RET_HEADS, dtype=np.float32))
    decay_logit0 = jnp.asarray(np.log(gam / (1.0 - gam)), f32)
    ret_cols = 2 * RET_HEADS * RET_DK + 2 * RET_HEADS * RET_DV
    diff_cols = 2 * DIFF_HEADS * 2 * DIFF_DH + DIFF_HEADS * DIFF_DV
    mla_down_cols = MLA_Q_RANK + MLA_KV_RANK + MLA_ROPE
    return {
        'x': normal((BATCH, SEQ, d), 1.0),
        'c': normal((BATCH, d), 1.0),
        'ctx': normal((BATCH, CTX_LEN, d), 1.0),
        'c_ctx': normal((d,), 1.0),
        'ada_w': normal((DEPTH, d, ADA_CHUNKS * d), 0.5 * d ** -0.5),
        'ada_b': normal((DEPTH, ADA_CHUNKS * d), 0.02),
        'ret_w_in': normal((n_ret, d, ret_cols), d ** -0.5),
        'ret_decay_logit': decay_logit0 + normal((n_ret, 2, RET_HEADS), 0.1),
        'ret_norm_g': gain((n_ret, RET_HEADS * RET_DV)),
        'ret_w_out': normal((n_ret, RET_HEADS * RET_DV, d), (RET_HEADS * RET_DV) ** -0.5),
        'diff_w_in': normal((n_diff, d, diff_cols), d ** -0.5),
        'diff_q_norm_g': gain((n_diff, DIFF_DH)),
        'diff_k_norm_g': gain((n_diff, DIFF_DH)),
        'diff_lambda': normal((n_diff, 4, DIFF_DH), 0.1),
        'diff_subln_g': gain((n_diff, DIFF_DV)),
        'diff_w_out': normal((n_diff, DIFF_HEADS * DIFF_DV, d), (DIFF_HEADS * DIFF_DV) ** -0.5),
        'na_w_in': normal((n_na, d, 3 * NA_HEADS * NA_DH), d ** -0.5),
        'na_q_norm_g': gain((n_na, NA_DH)),
        'na_k_norm_g': gain((n_na, NA_DH)),
        'na_rel_bias': normal((n_na, NA_HEADS, 2 * NA_WIN_H - 1, 2 * NA_WIN_W - 1), 0.1),
        'na_w_out': normal((n_na, NA_HEADS * NA_DH, d), (NA_HEADS * NA_DH) ** -0.5),
        'mla_w_down': normal((n_mla, d, mla_down_cols), d ** -0.5),
        'mla_q_norm_g': gain((n_mla, MLA_Q_RANK)),
        'mla_kv_norm_g': gain((n_mla, MLA_KV_RANK)),
        'mla_w_uq': normal((n_mla, MLA_Q_RANK, MLA_HEADS * MLA_QK), MLA_Q_RANK ** -0.5),
        'mla_w_ukv': normal((n_mla, MLA_KV_RANK, MLA_HEADS * (MLA_NOPE + MLA_V)), MLA_KV_RANK ** -0.5),
        'mla_qk_norm_q': gain((n_mla, MLA_QK)),
        'mla_qk_norm_k': gain((n_mla, MLA_QK)),
        'mla_w_out': normal((n_mla, MLA_HEADS * MLA_V, d), (MLA_HEADS * MLA_V) ** -0.5),
        'ffn_w_in': normal((DEPTH, d, 2 * FFN_HIDDEN), d ** -0.5),
        'ffn_w_out': normal((DEPTH, FFN_HIDDEN, d), FFN_HIDDEN ** -0.5),
    }

def first_block(x, c, ctx, c_ctx, ada_w, ada_b,
              ret_w_in, ret_decay_logit, ret_norm_g, ret_w_out,
              diff_w_in, diff_q_norm_g, diff_k_norm_g, diff_lambda, diff_subln_g, diff_w_out,
              na_w_in, na_q_norm_g, na_k_norm_g, na_rel_bias, na_w_out,
              mla_w_down, mla_q_norm_g, mla_kv_norm_g, mla_w_uq, mla_w_ukv,
              mla_qk_norm_q, mla_qk_norm_k, mla_w_out,
              ffn_w_in, ffn_w_out):
    s_lat = jax.nn.silu(c)[:, None, :]
    s_ctx = jax.nn.silu(c_ctx)[None, None, :]
    x_lat, x_ctx = x, ctx
    for i in range(DEPTH):
        need_ctx = i < DEPTH - 1
        mod_l = jnp.split(s_lat @ ada_w[i] + ada_b[i], ADA_CHUNKS, axis=-1)
        mod_c = jnp.split(s_ctx @ ada_w[i] + ada_b[i], ADA_CHUNKS, axis=-1)
        h_lat = modulate(x_lat, mod_l[0], mod_l[1])
        h_ctx = modulate(x_ctx, mod_c[0], mod_c[1])
        kind, j = i % N_MIXERS, i // N_MIXERS
        if kind == 0:
            y_ctx, y_lat = retention_mixer(h_ctx, h_lat, ret_w_in[j], ret_decay_logit[j],
                                           ret_norm_g[j], ret_w_out[j], need_ctx)
        elif kind == 1:
            lambda_init = 0.8 - 0.6 * math.exp(-0.3 * i)
            y_ctx, y_lat = diff_attention_mixer(h_ctx, h_lat, diff_w_in[j], diff_q_norm_g[j],
                                                diff_k_norm_g[j], diff_lambda[j], diff_subln_g[j],
                                                diff_w_out[j], lambda_init, need_ctx)
        elif kind == 2:
            y_ctx, y_lat = neighborhood_mixer(h_ctx, h_lat, na_w_in[j], na_q_norm_g[j],
                                              na_k_norm_g[j], na_rel_bias[j], na_w_out[j], need_ctx)
        else:
            y_ctx, y_lat = mla_mixer(h_ctx, h_lat, mla_w_down[j], mla_q_norm_g[j], mla_kv_norm_g[j],
                                     mla_w_uq[j], mla_w_ukv[j], mla_qk_norm_q[j], mla_qk_norm_k[j],
                                     mla_w_out[j], need_ctx)
        x_lat = x_lat + mod_l[2] * y_lat
        x_lat = x_lat + mod_l[5] * swiglu(modulate(x_lat, mod_l[3], mod_l[4]), ffn_w_in[i], ffn_w_out[i])
        if need_ctx:
            x_ctx = x_ctx + mod_c[2] * y_ctx
            x_ctx = x_ctx + mod_c[5] * swiglu(modulate(x_ctx, mod_c[3], mod_c[4]), ffn_w_in[i], ffn_w_out[i])
    return x_lat


CHUNK = 64
D_FF = 4096
LN_EPS = 1e-5
NORM_EPS = 1e-6
H_A = 4
DK_A = 128
DV_A = 128
CONV_K = 4
A_QK = H_A * DK_A
A_V = H_A * DV_A
H_B = 4
D_B = 128
B_PREV = 8
REL_CLIP = 128
B_W = H_B * D_B
H_C = 8
HKV_C = 2
G_C = H_C // HKV_C
D_C = 64
WINDOW = 128
C_PREV = WINDOW // CHUNK
C_Q = H_C * D_C
C_KV = HKV_C * D_C
N_BRANCH = 3
IN_SPLITS = (A_QK, A_QK, A_V, H_A, H_A, A_V, B_W, B_W, B_W, C_Q, C_KV, C_KV)
D_IN = sum(IN_SPLITS)


def layer_norm(x, g, b):
    xf = x.astype(jnp.float32)
    mu = jnp.mean(xf, -1, keepdims=True)
    xc = xf - mu
    var = jnp.mean(xc * xc, -1, keepdims=True)
    return (xc * lax.rsqrt(var + LN_EPS) * g.astype(jnp.float32) + b.astype(jnp.float32)).astype(x.dtype)

def swiglu_2(x, w_in, w_out):
    gate, up = jnp.split(x @ w_in, 2, axis=-1)
    return (jax.nn.silu(gate) * up) @ w_out

def causal_depthwise_conv(x, w):
    k = w.shape[0]
    return lax.conv_general_dilated(x, w[:, None, :], window_strides=(1,), padding=[(k - 1, 0)],
                                    dimension_numbers=('NWC', 'WIO', 'NWC'),
                                    feature_group_count=x.shape[-1])

def l2_normalize(x):
    return x * lax.rsqrt(jnp.sum(x * x, -1, keepdims=True) + NORM_EPS)

def to_chunks(a):
    b, t, h = a.shape[:3]
    a = a.reshape(b, t // CHUNK, CHUNK, h, *a.shape[3:])
    return jnp.moveaxis(a, (1, 3), (0, 2))

def chunk_gated_delta_rule(q, k, v, g, beta):
    b, t, h, dk = q.shape
    dv = v.shape[-1]
    q = to_chunks(q) * (dk ** -0.5)
    k = to_chunks(k)
    v = to_chunks(v)
    g = to_chunks(g)
    beta = to_chunks(beta)
    g_cum = jnp.cumsum(g, axis=-1)
    idx = jnp.arange(CHUNK)
    causal = idx[:, None] >= idx[None, :]
    strict = idx[:, None] > idx[None, :]
    decay = jnp.exp(jnp.where(causal, g_cum[..., :, None] - g_cum[..., None, :], -jnp.inf))
    k_beta = k * beta[..., None]
    lower = jnp.where(strict, jnp.einsum('nbhid,nbhjd->nbhij', k_beta, k) * decay, 0.0)
    eye = jnp.eye(CHUNK, dtype=jnp.float32)
    rhs = jnp.concatenate([v * beta[..., None], k_beta * jnp.exp(g_cum)[..., None]], axis=-1)
    uw = lax.linalg.triangular_solve(eye + lower, rhs, left_side=True, lower=True, unit_diagonal=True)
    u, w = uw[..., :dv], uw[..., dv:]
    attn = jnp.einsum('nbhid,nbhjd->nbhij', q, k) * decay
    q_dec = q * jnp.exp(g_cum)[..., None]
    g_last = g_cum[..., -1]
    k_dec = k * jnp.exp(g_last[..., None] - g_cum)[..., None]

    def step(state, inp):
        q_c, k_c, u_c, w_c, a_c, gl_c = inp
        v_new = u_c - jnp.einsum('bhcd,bhdv->bhcv', w_c, state)
        o_c = jnp.einsum('bhcd,bhdv->bhcv', q_c, state) + jnp.einsum('bhij,bhjv->bhiv', a_c, v_new)
        state = state * jnp.exp(gl_c)[..., None, None] + jnp.einsum('bhcd,bhcv->bhdv', k_c, v_new)
        return state, o_c

    s0 = jnp.zeros((b, h, dk, dv), jnp.float32)
    _, o = lax.scan(step, s0, (q_dec, k_dec, u, w, attn, g_last))
    o = jnp.moveaxis(o, (0, 2), (1, 3))
    return o.reshape(b, t, h, dv)

def gated_deltanet(qa, ka, va, beta_raw, a_raw, za, conv_w, a_log, dt_bias, norm_g):
    b, t, _ = qa.shape
    f32 = jnp.float32
    qkv = jax.nn.silu(causal_depthwise_conv(jnp.concatenate([qa, ka, va], -1), conv_w)).astype(f32)
    q, k, v = jnp.split(qkv, [A_QK, 2 * A_QK], axis=-1)
    q = l2_normalize(q.reshape(b, t, H_A, DK_A))
    k = l2_normalize(k.reshape(b, t, H_A, DK_A))
    v = v.reshape(b, t, H_A, DV_A)
    beta = jax.nn.sigmoid(beta_raw.astype(f32))
    g = -jnp.exp(a_log.astype(f32)) * jax.nn.softplus(a_raw.astype(f32) + dt_bias.astype(f32))
    o = chunk_gated_delta_rule(q, k, v, g, beta)
    z = za.reshape(b, t, H_A, DV_A).astype(f32)
    o = o * lax.rsqrt(jnp.mean(o * o, -1, keepdims=True) + NORM_EPS) * norm_g.astype(f32) * jax.nn.silu(z)
    return o.reshape(b, t, A_V).astype(qa.dtype)

def chunk_band(a, n_prev):
    b, t = a.shape[:2]
    n = t // CHUNK
    pad = [(0, 0), (n_prev * CHUNK, 0)] + [(0, 0)] * (a.ndim - 2)
    ap = jnp.pad(a, pad).reshape(b, n + n_prev, CHUNK, *a.shape[2:])
    band = jnp.stack([ap[:, j:j + n] for j in range(n_prev + 1)], axis=2)
    return band.reshape(b, n, (n_prev + 1) * CHUNK, *a.shape[2:])

def band_geometry(n, n_prev):
    i = jnp.arange(CHUNK)
    j = jnp.arange((n_prev + 1) * CHUNK)
    dist = n_prev * CHUNK + i[:, None] - j[None, :]
    valid = (jnp.arange(n)[:, None] - n_prev + j[None, :] // CHUNK) >= 0
    return dist, valid

def alibi_slopes(n):
    return 2.0 ** (-8.0 * jnp.arange(1, n + 1, dtype=jnp.float32) / n)

def chunk_relpos_attention(q, k, v, rel_bias):
    b, t, _ = q.shape
    n = t // CHUNK
    q = q.reshape(b, n, CHUNK, H_B, D_B)
    kb = chunk_band(k.reshape(b, t, H_B, D_B), B_PREV)
    vb = chunk_band(v.reshape(b, t, H_B, D_B), B_PREV)
    s = jnp.einsum('bnqhd,bnkhd->bnhqk', q, kb).astype(jnp.float32) * (D_B ** -0.5)
    dist, valid = band_geometry(n, B_PREV)
    rel_idx = jnp.clip(dist, -(CHUNK - 1), REL_CLIP) + (CHUNK - 1)
    bias = rel_bias.astype(jnp.float32)[:, rel_idx]
    s = jnp.where(valid[None, :, None, None, :], s + bias, -jnp.inf)
    p = jax.nn.softmax(s, axis=-1).astype(v.dtype)
    o = jnp.einsum('bnhqk,bnkhd->bnqhd', p, vb)
    return o.reshape(b, t, B_W)

def swa_sink_attention(q, k, v, sinks):
    b, t, _ = q.shape
    n = t // CHUNK
    q = q.reshape(b, n, CHUNK, HKV_C, G_C, D_C)
    kb = chunk_band(k.reshape(b, t, HKV_C, D_C), C_PREV)
    vb = chunk_band(v.reshape(b, t, HKV_C, D_C), C_PREV)
    s = jnp.einsum('bnqhgd,bnkhd->bnhgqk', q, kb).astype(jnp.float32) * (D_C ** -0.5)
    dist, valid = band_geometry(n, C_PREV)
    slopes = alibi_slopes(H_C).reshape(HKV_C, G_C)
    s = s - slopes[:, :, None, None] * jnp.abs(dist).astype(jnp.float32)
    s = jnp.where(valid[None, :, None, None, None, :], s, -jnp.inf)
    sink = jnp.broadcast_to(sinks.astype(jnp.float32).reshape(HKV_C, G_C)[:, :, None, None], s.shape[:-1] + (1,))
    p = jax.nn.softmax(jnp.concatenate([s, sink], axis=-1), axis=-1)[..., :-1].astype(v.dtype)
    o = jnp.einsum('bnhgqk,bnkhd->bnqhgd', p, vb)
    return o.reshape(b, t, C_Q)

def hybrid_mixer(x, w_in, b_in, conv_w, a_log, dt_bias, gdn_norm_g, rel_bias, sinks,
                 w_gate, b_gate, w_br_a, w_br_b, w_br_c, w_out):
    b, t, d = x.shape
    proj = x @ w_in + b_in
    split_at = np.cumsum(IN_SPLITS)[:-1].tolist()
    (qa, ka, va, beta_raw, a_raw, za, qb, kb, vb, qc, kc, vc) = jnp.split(proj, split_at, axis=-1)
    o_a = gated_deltanet(qa, ka, va, beta_raw, a_raw, za, conv_w, a_log, dt_bias, gdn_norm_g)
    o_b = chunk_relpos_attention(qb, kb, vb, rel_bias)
    o_c = swa_sink_attention(qc, kc, vc, sinks)
    gates = jax.nn.sigmoid(x @ w_gate + b_gate).reshape(b, t, N_BRANCH, d)
    merged = (gates[:, :, 0] * (o_a @ w_br_a) + gates[:, :, 1] * (o_b @ w_br_b)
              + gates[:, :, 2] * (o_c @ w_br_c))
    return merged @ w_out

def second_inputs(seed: int = 0) -> dict:
    key = jax.random.key(seed)
    keys = list(jax.random.split(key, 32))
    f32 = jnp.float32
    L, D = DEPTH, D_MODEL
    sub_scale = (8.0 * DEPTH) ** -0.25

    def nrm(shape, scale):
        return jax.random.normal(keys.pop(), shape, f32) * scale

    def gain(shape):
        return 1.0 + nrm(shape, 0.02)

    x = nrm((BATCH, SEQ, D), 1.0)
    ln1_g = gain((L, D))
    ln1_b = nrm((L, D), 0.02)
    w_ff1_in = nrm((L, D, 2 * D_FF), D ** -0.5)
    w_ff1_out = nrm((L, D_FF, D), D_FF ** -0.5 * sub_scale)
    w_in = nrm((L, D, D_IN), D ** -0.5)
    b_in = nrm((L, D_IN), 0.02)
    conv_w = nrm((L, CONV_K, 2 * A_QK + A_V), CONV_K ** -0.5)
    a_log = jnp.log(jax.random.uniform(keys.pop(), (L, H_A), f32, 1.0, 16.0))
    dt = jnp.exp(jax.random.uniform(keys.pop(), (L, H_A), f32, math.log(1e-3), math.log(1e-1)))
    dt_bias = dt + jnp.log(-jnp.expm1(-dt))
    gdn_norm_g = gain((L, DV_A))
    rel_bias = nrm((L, H_B, CHUNK + REL_CLIP), 0.1)
    sinks = nrm((L, H_C), 0.5)
    w_gate = nrm((L, D, N_BRANCH * D), D ** -0.5)
    b_gate = nrm((L, N_BRANCH * D), 0.02)
    w_br_a = nrm((L, A_V, D), A_V ** -0.5 * sub_scale)
    w_br_b = nrm((L, B_W, D), B_W ** -0.5 * sub_scale)
    w_br_c = nrm((L, C_Q, D), C_Q ** -0.5 * sub_scale)
    w_out = nrm((L, D, D), D ** -0.5 * sub_scale)
    ln2_g = gain((L, D))
    ln2_b = nrm((L, D), 0.02)
    w_ff2_in = nrm((L, D, 2 * D_FF), D ** -0.5)
    w_ff2_out = nrm((L, D_FF, D), D_FF ** -0.5 * sub_scale)
    ln3_g = gain((L, D))
    ln3_b = nrm((L, D), 0.02)
    return {'x': x, 'ln1_g': ln1_g, 'ln1_b': ln1_b, 'w_ff1_in': w_ff1_in, 'w_ff1_out': w_ff1_out,
            'w_in': w_in, 'b_in': b_in, 'conv_w': conv_w, 'a_log': a_log, 'dt_bias': dt_bias,
            'gdn_norm_g': gdn_norm_g, 'rel_bias': rel_bias, 'sinks': sinks, 'w_gate': w_gate,
            'b_gate': b_gate, 'w_br_a': w_br_a, 'w_br_b': w_br_b, 'w_br_c': w_br_c, 'w_out': w_out,
            'ln2_g': ln2_g, 'ln2_b': ln2_b, 'w_ff2_in': w_ff2_in, 'w_ff2_out': w_ff2_out,
            'ln3_g': ln3_g, 'ln3_b': ln3_b}

def second_block(x, ln1_g, ln1_b, w_ff1_in, w_ff1_out, w_in, b_in, conv_w, a_log, dt_bias,
              gdn_norm_g, rel_bias, sinks, w_gate, b_gate, w_br_a, w_br_b, w_br_c, w_out,
              ln2_g, ln2_b, w_ff2_in, w_ff2_out, ln3_g, ln3_b):
    alpha = (2.0 * DEPTH) ** 0.25
    for l in range(DEPTH):
        x = layer_norm(alpha * x + 0.5 * swiglu_2(x, w_ff1_in[l], w_ff1_out[l]), ln1_g[l], ln1_b[l])
        mix = hybrid_mixer(x, w_in[l], b_in[l], conv_w[l], a_log[l], dt_bias[l], gdn_norm_g[l],
                           rel_bias[l], sinks[l], w_gate[l], b_gate[l], w_br_a[l], w_br_b[l],
                           w_br_c[l], w_out[l])
        x = layer_norm(alpha * x + mix, ln2_g[l], ln2_b[l])
        x = layer_norm(alpha * x + 0.5 * swiglu_2(x, w_ff2_in[l], w_ff2_out[l]), ln3_g[l], ln3_b[l])
    return x


def setup_inputs(seed=0):
    out = dict(first_inputs(seed))
    for name, value in second_inputs(seed + 1).items():
        if name != "x":
            out[name + "_2"] = value
    return out


def reference(
    x, c, ctx, c_ctx, ada_w, ada_b, ret_w_in, ret_decay_logit, ret_norm_g, ret_w_out, diff_w_in,
    diff_q_norm_g, diff_k_norm_g, diff_lambda, diff_subln_g, diff_w_out, na_w_in, na_q_norm_g,
    na_k_norm_g, na_rel_bias, na_w_out, mla_w_down, mla_q_norm_g, mla_kv_norm_g, mla_w_uq,
    mla_w_ukv, mla_qk_norm_q, mla_qk_norm_k, mla_w_out, ffn_w_in, ffn_w_out, ln1_g_2, ln1_b_2,
    w_ff1_in_2, w_ff1_out_2, w_in_2, b_in_2, conv_w_2, a_log_2, dt_bias_2, gdn_norm_g_2,
    rel_bias_2, sinks_2, w_gate_2, b_gate_2, w_br_a_2, w_br_b_2, w_br_c_2, w_out_2, ln2_g_2,
    ln2_b_2, w_ff2_in_2, w_ff2_out_2, ln3_g_2, ln3_b_2,
):
    x = first_block(
        x, c, ctx, c_ctx, ada_w, ada_b, ret_w_in, ret_decay_logit, ret_norm_g, ret_w_out,
        diff_w_in, diff_q_norm_g, diff_k_norm_g, diff_lambda, diff_subln_g, diff_w_out, na_w_in,
        na_q_norm_g, na_k_norm_g, na_rel_bias, na_w_out, mla_w_down, mla_q_norm_g,
        mla_kv_norm_g, mla_w_uq, mla_w_ukv, mla_qk_norm_q, mla_qk_norm_k, mla_w_out, ffn_w_in,
        ffn_w_out,
    )
    return second_block(
        x, ln1_g_2, ln1_b_2, w_ff1_in_2, w_ff1_out_2, w_in_2, b_in_2, conv_w_2, a_log_2,
        dt_bias_2, gdn_norm_g_2, rel_bias_2, sinks_2, w_gate_2, b_gate_2, w_br_a_2, w_br_b_2,
        w_br_c_2, w_out_2, ln2_g_2, ln2_b_2, w_ff2_in_2, w_ff2_out_2, ln3_g_2, ln3_b_2,
    )


_drawn_inputs = setup_inputs


def setup_inputs(seed=0):
    import zlib

    import numpy as np

    out = dict(_drawn_inputs(seed))
    spreads = {}
    factors = {'ret_norm_g': 8.0,
     'diff_q_norm_g': 8.0,
     'diff_k_norm_g': 8.0,
     'diff_lambda': 8.0,
     'diff_subln_g': 25.116,
     'b_in_2': 8.0,
     'a_log_2': 4.779,
     'gdn_norm_g_2': 44.279,
     'rel_bias_2': 29.55,
     'sinks_2': 30.62,
     'b_gate_2': 8.0}
    for name, (base, spread) in spreads.items():
        noise = np.random.default_rng([zlib.crc32(name.encode()), seed]).standard_normal(out[name].shape)
        drawn = base * np.exp(spread * noise) if base else spread * noise
        out[name] = jnp.asarray(drawn.astype(out[name].dtype))
    for name, factor in factors.items():
        out[name] = (out[name] * factor).astype(out[name].dtype)
    return out
```

```python
import math
from contextlib import ExitStack

import numpy as np

import concourse.bass as bass
from concourse import mybir

F32 = mybir.dt.float32
F32R = mybir.dt.float32r
ALU = mybir.AluOpType
ACT = mybir.ActivationFunctionType
AX = mybir.AxisListType.X

P = 128
D = 1024
DC = D // P
T = 256
TT = 2 * T
CTX, LAT = slice(0, T), slice(T, TT)
EPS = 1e-6
LN_EPS = 1e-5
RET_H, RET_VB = 4, 4
FFN_B = 22
FF_B = 32
LAMBDA_INIT = 0.8 - 0.6 * math.exp(-0.3)
ALPHA = 4.0 ** 0.25
LAYERS2 = 2
CH = 64
RAW, SPLIT = 4, 2

ADA_TILES = 48
FIRST = [("ret_qkv", 16, 16), ("ret_g", 8, 8), ("ret_out", 8, 4), ("ffn_in0", 22, 22), ("ffn_out0", 11, 2),
         ("diff_in", 12, 12), ("diff_out", 4, 4), ("ffn_in1", 22, 22), ("ffn_out1", 11, 2)]
LAYER = [("ff1_in", 32, 32), ("ff1_out", 16, 4), ("w_in", 18, 18), ("w_gate", 12, 12), ("w_br", 6, 6),
         ("w_out", 4, 4), ("ff2_in", 32, 32), ("ff2_out", 16, 4)]
N1 = sum(t for _, t, _ in FIRST)
G1 = sum(g for _, _, g in FIRST)
NL = sum(t for _, t, _ in LAYER)
GL = sum(g for _, _, g in LAYER)
NORMS = 4 + 3 * LAYERS2
TILES = N1 + LAYERS2 * NL + SPLIT
assert NL % 4 == 0 and GL % 2 == 0 and G1 % 2 == 0 and TILES % 4 == 0 and ADA_TILES % 4 == 0


def starts(phases, n, g):
    out = {}
    for name, tiles, groups in phases:
        out[name] = (n, g, tiles)
        n, g = n + tiles, g + groups
    return out


PH = {**starts(FIRST, 0, 0), **starts(LAYER, N1, G1)}

C_ADAB, C_RETG, C_DQG, C_DKG, C_SUB, C_COND = 0, 96, 112, 113, 114, 115
NCOL1 = 131
C_LN = [(0, 8), (16, 24), (32, 40)]
C_BIN, C_BG, C_CONV, C_GDN = 48, 77, 101, 149
NCOL2 = 150
R_VB, R_VC, R_BETA, R_A, R_ALOG, R_DT, R_SINK = 0, 512, 640, 644, 648, 652, 656
NROW2 = 664


def build(nc, ada, ws, xt, col1, row1, col2, row2, relb, cst, ret_cst, ret_dist, c64, out):
    KB = 1024
    base = -(-nc.sbuf_base // 64) * 64

    def at(name, shape, kb, dtype=F32):
        return nc.alloc_sbuf_tensor_at(name, shape, dtype, offset=base + int(kb * KB) // 32 * 32)

    raw = at("raw", [P, RAW, 16, P], 0)
    w_lo = at("w_lo", [P, RAW, 16, P], 0, F32R)
    w_hi = at("w_hi", [P, SPLIT, 16, P], 32, F32R)
    X = at("X", [P, DC, TT], 48)
    h_hi = at("h_hi", [P, DC, TT], 64, F32R)
    h_lo = at("h_lo", [P, DC, TT], 80, F32R)
    l_hi = at("l_hi", [P, DC, T], 64, F32R)
    l_lo = at("l_lo", [P, DC, T], 72, F32R)
    relB = at("relB", [P, 4, 2, T], 80)
    rows2 = at("rows2", [P, NROW2], 88)
    bandB = at("bandB", [P, 2, T], 91)
    bandC = at("bandC", [P, 2, T], 93)
    cs = at("cs", [P, 6, P], 96)
    ident, ones, ones64, rot_ret, rot_diff, swap64 = (cs[:, i, :] for i in range(6))
    rope_d = at("rope_d", [P, 2, T], 99)
    mod = at("mod", [P, 2, 48, 2], 101)
    cols1 = at("cols1", [P, NCOL1], 101.8)
    cols2 = at("cols2", [P, NCOL2], 102.4)
    silu_c = at("silu_c", [P, DC, 2], 103.1)
    lgam = at("lgam", [P, 8], 103.2)
    lam = at("lam", [P, 4], 103.3)
    small = at("small", [P, 16], 103.4)
    softx = at("softx", [P, 2, 16], 103.5)
    rr = at("rr", [P, TT], 104)
    ada_row = at("ada_row", [2, 2, T], 104)
    AR = 106
    SQ = at("SQ", [P, DC, TT], AR)
    QK = at("QK", [P, 16, TT], AR)
    V = at("V", [P, RET_H, 4, TT], AR + 32)
    DM = at("DM", [P, RET_H, 4, T], AR + 64)
    rope_r = at("rope_r", [P, 2, 2, T], AR + 80)
    dist = at("dist", [P, 4, 4, T], AR + 32)
    expd = at("expd", [P, 2, 4, T], AR + 48)
    rtmp = at("rtmp", [P, 2, 2, T], AR + 84)
    att = at("att", [P, 6, T], AR + 84)
    sqh = at("sqh", [P, 4, TT], AR + 90)
    y_hi = at("y_hi", [P, 16, TT], AR + 32, F32R)
    y_lo = at("y_lo", [P, 16, TT], AR, F32R)
    gs = at("gs", [P, 2, TT], AR + 84)
    gp = at("gp", [P, 2, TT], AR + 90)
    hid_hi = at("hid_hi", [P, FFN_B, TT], AR, F32R)
    hid_lo = at("hid_lo", [P, FFN_B, TT], AR + 44, F32R)
    fs = at("fs", [P, 2, TT], AR + 88)
    fp = at("fp", [P, 2, TT], AR + 92)
    QK1 = at("QK1", [P, 12, TT], AR)
    V1 = at("V1", [P, 4, D], AR + 24)
    R1 = at("R1", [P, 12, TT], AR + 40)
    SQ1 = at("SQ1", [P, 12, TT], AR + 64)
    lamv = at("lamv", [P, 4, 64], AR + 100)
    E1 = at("E1", [P, 2, 2, TT], AR + 40)
    P1 = at("P1", [P, 2, TT], AR + 48)
    PT1 = at("PT1", [P, 2, 4, T], AR + 52)
    O1 = at("O1", [P, 8, T], AR + 64)
    SO1 = at("SO1", [P, 8, T], AR + 72)
    RO1 = at("RO1", [P, 8, T], AR + 80)
    d_hi = at("d_hi", [P, DC, T], AR, F32R)
    d_lo = at("d_lo", [P, DC, T], AR + 8, F32R)
    fh_hi = at("fh_hi", [P, FF_B, T], AR, F32R)
    fh_lo = at("fh_lo", [P, FF_B, T], AR + 32, F32R)
    gs2 = at("gs2", [P, 2, T], AR + 88)
    gp2 = at("gp2", [P, 2, T], AR + 92)
    gate = at("gate", [P, 24, T], AR)
    o_hi = at("o_hi", [P, 12, T], AR + 24, F32R)
    o_lo = at("o_lo", [P, 12, T], AR + 36, F32R)
    CV = at("CV", [P, 12, T], AR + 48)
    za = at("za", [P, 4, T], AR + 60)
    QKVp = at("QKVp", [P, 12, T + 3], AR + 64)
    qkb = at("qkb", [P, 8, T], AR + 76.5)
    vb = at("vb", [P, 2, 512], AR + 84.5)
    qc = at("qc", [P, 4, T], AR + 88.5)
    kc = at("kc", [P, 2, T], AR + 92.5)
    vc = at("vc", [P, 2, 2, P], AR + 94.5)
    ba = at("ba", [64, 4, 8], AR + 96.5)
    beta = at("beta", [64, 4, 4], AR + 96.75)
    gdec = at("gdec", [64, 4, 4], AR + 97)
    gcum = at("gcum", [64, 4, 4], AR + 97.25)
    gsuf = at("gsuf", [64, 4, 4], AR + 97.5)
    gexp = at("gexp", [64, 4, 4], AR + 97.75)
    bt = at("bt", [64, 8, 16], AR + 98)
    m64 = at("m64", [64, 9, CH], AR + 99.5)
    NSQ = at("NSQ", [P, 4, T], AR + 64)
    NR = at("NR", [P, 4, T], AR + 68)
    TT2 = at("TT2", [P, 2, 2, T], AR + 64)
    PT2 = at("PT2", [P, 2, 2, T], AR + 68)
    kT = at("kT", [64, 8, P], AR + 64)
    vT = at("vT", [64, 8, P], AR + 68)
    kbg = at("kbg", [64, 8, P], AR + 72)
    kdec = at("kdec", [64, 8, P], AR + 76)
    DT = at("DT", [64, 8, CH], AR + 80)
    LT = at("LT", [64, 8, CH], AR + 82)
    qkT = at("qkT", [64, 8, CH], AR + 84)
    Tm = at("Tm", [64, 8, CH], AR + 86)
    Um = at("Um", [64, 8, CH], AR + 88)
    Pm = at("Pm", [64, 8, CH], AR + 90)
    Mm = at("Mm", [64, 8, CH], AR + 92)
    gcb = at("gcb", [P, 8, CH], AR + 94)
    uu = at("uu", [64, 8, P], AR + 64)
    wT = at("wT", [P, 8, CH], AR + 90)
    qdec = at("qdec", [P, 8, CH], AR + 82)
    vnew = at("vnew", [64, 2, P], AR + 92)
    Sst = at("Sst", [P, 2, P], AR + 86)
    oA = at("oA", [P, 2, T], AR + 72)
    osq = at("osq", [P, 2, T], AR + 74)
    mrg = at("mrg", [P, DC, T], AR + 64)
    mrt = at("mrt", [P, 4, T], AR + 72)
    m_hi = at("m_hi", [P, DC, T], AR + 76, F32R)
    m_lo = at("m_lo", [P, DC, T], AR + 84, F32R)

    with ExitStack() as ctx:
        ps = ctx.enter_context(nc.psum_tensor("ps", [P, 8, 512], F32))

        def sem(name):
            return ctx.enter_context(nc.semaphore(name))

        raw_full = [sem(f"raw_full{s}") for s in range(RAW)]
        (hi_done, lo_done, tile_used, sums_taken, mod_ready, tables_in, params_in, layer_used,
         x_in, silu_c_ready, operand_ready, silu_ready, gate_ready) = map(sem, (
            "hi_done", "lo_done", "tile_used", "sums_taken", "mod_ready", "tables_in", "params_in",
            "layer_used", "x_in", "silu_c_ready", "operand_ready", "silu_ready", "gate_ready"))
        (x_ready, mean_ready, sq_ready, square_sum, var_ready, std_ready, scaled, normed, lgam_exp, lgam_one,
         lgam_ln, decays_exp, decays_ready, lgam_ready) = map(sem, (
            "x_ready", "mean_ready", "sq_ready", "square_sum", "var_ready", "std_ready", "scaled", "normed",
            "lgam_exp", "lgam_one", "lgam_ln", "decays_exp", "decays_ready", "lgam_ready"))
        (rot_in, rot_ready, rot_taken, att_ready, att_decayed, ho_ready, ho_taken, ho_mean, ho_centred, ho_sq,
         ho_sqsum, ho_var, ho_std, heads_done) = map(sem, (
            "rot_in", "rot_ready", "rot_taken", "att_ready", "att_decayed", "ho_ready", "ho_taken", "ho_mean",
            "ho_centred", "ho_sq", "ho_sqsum", "ho_var", "ho_std", "heads_done"))
        (lam_dot, lam_exp, qk_ready, qk_sq, qk_sums, qk_sums_taken, qk_std, drot_in, drot_ready, drot_taken,
         s_ready, s_max, s_exp, s_prob, s_turned, s_copied, so_ready, so_taken, so_sq, so_sum, so_var,
         so_std) = map(sem, (
            "lam_dot", "lam_exp", "qk_ready", "qk_sq", "qk_sums", "qk_sums_taken", "qk_std", "drot_in",
            "drot_ready", "drot_taken", "s_ready", "s_max", "s_exp", "s_prob", "s_turned", "s_copied", "so_ready",
            "so_taken", "so_sq", "so_sum", "so_var", "so_std"))
        (m_in, kswap_ready, kswap_taken, conv_done, conv_silu, n_sq, n_sum, n_var, n_std, n_done, ba_ready,
         a_in, a_out, b_s, b_max, b_exp, b_prob, b_turned, b_copied, b_o, b_taken, bias_ready) = map(sem, (
            "m_in", "kswap_ready", "kswap_taken", "conv_done", "conv_silu", "n_sq", "n_sum", "n_var", "n_std",
            "n_done", "ba_ready", "a_in", "a_out", "b_s", "b_max", "b_exp", "b_prob", "b_turned", "b_copied",
            "b_o", "b_taken", "bias_ready"))
        (g_mid, g_lin, g_exp, g_ln, g_rate, gd_ready, gd_sums, gd_taken, gd_exp, gd_turn_k, gd_turned,
         gd_diff, gd_decay, gd_kk, gd_sys, inv_mask, inv_p, inv_pc, inv_done, inv_next, rhs_ready, uw_ready,
         uw_taken, sc_w, sc_v, sc_s, sc_next, go_sq, go_sum, go_var, go_std, out_done) = map(sem, (
            "g_mid", "g_lin", "g_exp", "g_ln", "g_rate", "gd_ready", "gd_sums", "gd_taken", "gd_exp",
            "gd_turn_k", "gd_turned", "gd_diff", "gd_decay", "gd_kk", "gd_sys", "inv_mask", "inv_p", "inv_pc",
            "inv_done", "inv_next", "rhs_ready", "uw_ready", "uw_taken", "sc_w", "sc_v", "sc_s", "sc_next",
            "go_sq", "go_sum", "go_var", "go_std", "out_done"))

        waits_passed, ada_copied, ada_turned = map(sem, ("waits_passed", "ada_copied", "ada_turned"))
        go_copied = sem("go_copied")
        (logit_in, dist_in, lam_in, band_in, ada_ready, mod_scaled, lgam_abs, qk_in, za_ready, centred) = map(sem, (
            "logit_in", "dist_in", "lam_in", "band_in", "ada_ready", "mod_scaled", "lgam_abs", "qk_in", "za_ready",
            "centred"))

        block = ctx.enter_context(nc.Block())

        def tiles(phase, layer, eng, body, first=0, count=None, per=4):
            n0, _, total = PH[phase]
            count = total - first if count is None else count
            turns = count // per
            done = 0
            if turns > 1:
                with eng.Fori(0, turns) as i:
                    for u in range(per):
                        body(i, u, n0 + first + u, i * (per // 4) + layer * (NL // 4))
                done = turns * per
            for u in range(done, count):
                body(0, u, n0 + first + u, layer * (NL // 4))

        def group(phase, layer, g):
            return layer * GL + g + PH[phase][1]

        def raw_slot(s):
            return (s + ADA_TILES) % RAW

        def pair(phase, g):
            return 2 * ((PH[phase][1] + g) % 2)

        def bank(phase, g):
            g += PH[phase][1]
            return 2 * (g % 2) + g // 2 % 2

        @block.sync
        def _(sp):
            sp.dma_start(cols1[:], col1).then_inc(x_in, 16)
            sp.dma_start(X[:], xt).then_inc(x_in, 16)
            for n in range(RAW):
                sp.dma_start(raw[:, n], ada[n]).then_inc(raw_full[n], 16)
            with sp.Fori(0, ADA_TILES // 4 - 1) as i:
                for u in range(4):
                    sp.wait_ge(ada_copied, i * 4 + u + 1)
                    sp.dma_start(raw[:, u], ada[bass.ds(i * 4 + u + 4, 1)].rearrange("a p b c -> (a p) b c")
                                 ).then_inc(raw_full[u], 16)
            for u in range(4):
                sp.wait_ge(ada_copied, ADA_TILES - 3 + u)
                sp.dma_start(raw[:, u], ws[u]).then_inc(raw_full[u], 16)
            with sp.Fori(0, TILES // 4 - 1) as i:
                for u in range(4):
                    sp.wait_ge(tile_used, i * 4 + u + 1 + SPLIT)
                    sp.dma_start(raw[:, u], ws[bass.ds(i * 4 + u + 4, 1)].rearrange("a p b c -> (a p) b c")
                                 ).then_inc(raw_full[u], 16)
            sp.wait_ge(normed, DC * NORMS)
            sp.dma_start(out, X[:, :, LAT]).then_inc(out_done, 16)
            sp.wait_ge(out_done, 16)

        @block.gpsimd
        def _(pool):
            pool.dma_start(lgam[:], row1[:, 0:8]).then_inc(logit_in, 16)
            pool.dma_start(dist[:], ret_dist).then_inc(dist_in, 16)
            pool.dma_start(rope_r[:], ret_cst).then_inc(tables_in, 16)
            pool.dma_start(cs[:], cst[:, 0:768].rearrange("p (a b) -> p a b", b=P)).then_inc(tables_in, 16)
            pool.dma_start(rope_d[:], cst[:, 768:1280].rearrange("p (a b) -> p a b", b=T)).then_inc(tables_in, 16)
            for h in range(RET_H):
                pool.wait_ge(decays_exp, 2 * h + 2)
                pool.wait_ge(dist_in, 16)
                nc.gpsimd.tensor_tensor(expd[:], expd[:], dist[:, 2:4], ALU.mult)
                pool.drain()
                nc.gpsimd.tensor_tensor(DM[:, h], expd[:, 0], expd[:, 1], ALU.add).then_inc(decays_ready, 1)
            pool.wait_ge(sums_taken, group("ffn_out0", 0, 2) + 2)
            pool.dma_start(lamv[:], row1[:, 8:264].rearrange("p (a b) -> p a b", b=64)).then_inc(lam_in, 16)
            pool.wait_ge(sums_taken, group("ffn_out1", 0, 2) + 2)
            pool.dma_start(bandB[:], cst[:, 1280:1792].rearrange("p (a b) -> p a b", b=T)).then_inc(band_in, 16)
            pool.dma_start(bandC[:], cst[:, 1792:2304].rearrange("p (a b) -> p a b", b=T)).then_inc(band_in, 16)
            pool.dma_start(m64[:], c64).then_inc(band_in, 16)
            pool.wait_ge(band_in, 48)
            with pool.Fori(0, LAYERS2) as layer:
                pool.wait_ge(layer_used, layer + 1)
                pool.dma_start(cols2[:], col2[bass.ds(layer, 1)].rearrange("a p c -> (a p) c")
                               ).then_inc(params_in, 16)
                pool.dma_start(rows2[:], row2[bass.ds(layer, 1)].rearrange("a p c -> (a p) c")
                               ).then_inc(params_in, 16)
                pool.dma_start(relB[:], relb[bass.ds(layer, 1)].rearrange("a p h b k -> (a p) h b k")
                               ).then_inc(params_in, 16)
                pool.wait_ge(params_in, layer * 48 + 48)
                for h in range(4):
                    ins = nc.gpsimd.tensor_tensor(relB[:, h], relB[:, h], bandB[:], ALU.add)
                ins.then_inc(bias_ready, 1)

        @block.tensor
        def _(pe):
            mm = nc.tensor.matmul

            def pass_wait():
                pe.sem_inc(waits_passed)

            def product(out_, blk, s, rhs_hi, rhs_lo, start, stop):
                mm(out_, w_hi[:, s % SPLIT, blk], rhs_hi, start=start, stop=False)
                mm(out_, w_hi[:, s % SPLIT, blk], rhs_lo, start=False, stop=False)
                return mm(out_, w_lo[:, raw_slot(s), blk], rhs_hi, start=False, stop=stop)

            def product_rows(out_, blk, s, x_hi, x_lo, start, stop):
                mm(out_, x_hi, w_hi[:, s % SPLIT, blk], start=start, stop=False)
                mm(out_, x_hi, w_lo[:, raw_slot(s), blk], start=False, stop=False)
                return mm(out_, x_lo, w_hi[:, s % SPLIT, blk], start=False, stop=stop)

            def wait_tile(s, turn):
                pe.wait_ge(lo_done, turn * 4 + s + 1)

            def wide(phase, layer, rhs_hi, rhs_lo, width, first=0, count=None):
                if width == T:
                    pe.wait_ge(sums_taken, group(phase, layer, first + 2))
                    pass_wait()

                def body(i, u, s, turn):
                    wait_tile(s, turn)
                    ahead = 1 if width == TT else -1
                    pe.wait_ge(sums_taken, group(phase, layer, i * 4 + first + u + ahead))
                    b = pair(phase, first + u) if width == TT else bank(phase, first + u)
                    for mi in range(2):
                        o = ps[:, b + mi, 0:TT] if width == TT else ps[:, b, mi * T:(mi + 1) * T]
                        for c in range(DC):
                            ins = product(o, mi * DC + c, s, rhs_hi[:, c, :], rhs_lo[:, c, :], c == 0, c == DC - 1)
                    ins.then_inc(tile_used, 1)
                tiles(phase, layer, pe, body, first, count)

            def values(phase, layer, x_hi, x_lo, nblk, first, count):
                def body(i, u, s, turn):
                    wait_tile(s, turn)
                    pe.wait_ge(sums_taken, group(phase, layer, i * 4 + first + u + (1 if nblk == 4 else -1)))
                    b = pair(phase, first + u) if nblk == 4 else bank(phase, first + u)
                    for kb in range(nblk):
                        o = ps[:, b + kb // 2, (kb % 2) * T:(kb % 2 + 1) * T].rearrange("p (a b) -> p a b", b=P)
                        for c in range(DC):
                            tok = slice(kb * P, kb * P + P)
                            ins = product_rows(o, slice(c, 16, DC), s, x_hi[:, c, tok], x_lo[:, c, tok],
                                               c == 0, c == DC - 1)
                    ins.then_inc(tile_used, 1)
                tiles(phase, layer, pe, body, first, count)

            def deep(phase, layer, rhs_hi, rhs_lo, width, parts):
                def body(i, u, s, turn):
                    wait_tile(s, turn)
                    q = u % parts
                    if q == 0:
                        pe.wait_ge(sums_taken, group(phase, layer, i * 2 + u // parts + 1))
                    b = pair(phase, u // parts)
                    for mi in range(2):
                        for c in range(DC):
                            ins = product(ps[:, b + mi, 0:width], mi * DC + c, s, rhs_hi[:, q * DC + c, :],
                                          rhs_lo[:, q * DC + c, :], q == 0 and c == 0, q == parts - 1 and c == DC - 1)
                    ins.then_inc(tile_used, 1)
                tiles(phase, layer, pe, body, per=2 * parts)

            def ffn_out(phase, cols):
                width = cols.stop - cols.start
                pe.wait_ge(sums_taken, group(phase, 0, 2))

                def body(first, last):
                    def run(i, u, s, turn):
                        wait_tile(s, turn)
                        for ci in range(2):
                            blk = bass.ds(i * 8 + 2 * (u + first) + ci, 1)
                            for m in range(DC):
                                ins = product(ps[:, m, 0:width], ci * DC + m, s,
                                              hid_hi[:, blk, cols], hid_lo[:, blk, cols],
                                              first == 0 and ci == 0, last and ci == 1)
                        ins.then_inc(tile_used, 1)
                    return run
                tiles(phase, 0, pe, body(0, False), 0, 1)
                tiles(phase, 0, pe, body(1, False), 1, 8)
                tiles(phase, 0, pe, body(9, False), 9, 1)
                tiles(phase, 0, pe, body(10, True), 10, 1)

            def norm(q, cols, mean=None):
                width = cols.stop - cols.start
                if mean is not None:
                    pe.wait_ge(x_ready, q)
                    for c in range(DC):
                        ins = mm(ps[:, 4, 0:width], ones, X[:, c, cols], start=c == 0, stop=c == DC - 1)
                    ins.then_inc(mean_ready, 1)
                for c in range(DC):
                    pe.wait_ge(sq_ready, q * DC + c + 1)
                    ins = mm(ps[:, 5, 0:width], ones, SQ[:, c, 0:width], start=c == 0, stop=c == DC - 1)
                ins.then_inc(square_sum, 1)

            pe.sem_inc(tile_used, SPLIT)
            pe.wait_ge(silu_c_ready, 1)

            def ada_tile(turn, u):
                pe.wait_ge(raw_full[u], turn * 16 + 16)
                for c in range(DC):
                    ins = mm(ps[0:2, 4 + u % 2, 0:T].rearrange("p (a b) -> p a b", b=P), silu_c[:, c, :],
                             raw[:, u, c:16:DC, :], start=c == 0, stop=c == DC - 1)
                ins.then_inc(ada_ready, 1)

            def ada_turn(t, u):
                pe.wait_ge(ada_copied, t + 1)
                for mi in range(2):
                    ins = mm(ps[:, 6 + u % 2, 2 * mi:2 * mi + 2], ada_row[:, u % 2, mi * P:mi * P + P],
                             ident[0:2, 0:2], start=True, stop=True)
                ins.then_inc(ada_turned, 1)
            pe.wait_ge(tables_in, 48)
            for u in range(4):
                ada_tile(0, u)
                if u:
                    ada_turn(u - 1, u - 1)
            with pe.Fori(1, ADA_TILES // 4) as i:
                for u in range(4):
                    ada_tile(i, u)
                    ada_turn(i * 4 + u - 1, (u - 1) % 4)
            ada_turn(ADA_TILES - 1, 3)
            pe.wait_ge(mod_ready, ADA_TILES)

            norm(0, slice(0, TT))
            pe.wait_ge(operand_ready, 1)
            wide("ret_qkv", 0, h_hi, h_lo, TT, 0, 8)
            values("ret_qkv", 0, h_hi, h_lo, 4, 8, 8)
            pe.wait_ge(sums_taken, group("ret_qkv", 0, 16) + 2)
            for r in range(8):
                if r >= 4:
                    pe.wait_ge(rot_taken, r - 3)
                mm(ps[:, 4 + r % 4, :].rearrange("p (a b) -> p a b", b=T), rot_ret, QK[:, 2 * r:2 * r + 2, LAT],
                   start=True, stop=True).then_inc(rot_ready, 1)
            pe.wait_ge(rot_taken, 8)
            for h in range(RET_H):
                if h:
                    pe.wait_ge(ho_var, h)
                for kb in range(4):
                    for c in range(2):
                        mm(ps[:, 4 + kb // 2, (kb % 2) * T:(kb % 2 + 1) * T], QK[:, 8 + 2 * h + c, kb * P:kb * P + P],
                           QK[:, 2 * h + c, LAT], start=c == 0, stop=c == 1)
                for kb in range(2):
                    for c in range(2):
                        ins = mm(ps[:, 6, kb * T:kb * T + T], QK[:, 8 + 2 * h + c, kb * P:kb * P + P],
                                 QK[:, 2 * h + c, CTX], start=c == 0, stop=c == 1)
                ins.then_inc(att_ready, 1)
                pe.wait_ge(att_decayed, h + 1)
                for b in range(4):
                    for kb in range(2):
                        mm(ps[:, b, CTX], V[:, h, kb, b * P:b * P + P], att[:, 4 + kb, :], start=kb == 0, stop=kb == 1)
                    for kb in range(4):
                        ins = mm(ps[:, b, LAT], V[:, h, kb, b * P:b * P + P], att[:, kb, :],
                                 start=kb == 0, stop=kb == 3)
                ins.then_inc(ho_ready, 1)
                pe.wait_ge(ho_taken, h + 1)
                for b in range(4):
                    ins = mm(ps[:, 7, :], ones, V[:, h, b, :], start=b == 0, stop=b == 3)
                ins.then_inc(ho_mean, 1)
                pe.wait_ge(ho_sq, h + 1)
                for b in range(4):
                    ins = mm(ps[:, 4, :], ones, sqh[:, b, :], start=b == 0, stop=b == 3)
                ins.then_inc(ho_sqsum, 1)
            wide("ret_g", 0, h_hi, h_lo, TT)
            pe.wait_ge(operand_ready, 2)
            deep("ret_out", 0, y_hi, y_lo, TT, 2)
            norm(1, slice(0, TT))
            pe.wait_ge(operand_ready, 3)
            wide("ffn_in0", 0, h_hi, h_lo, TT)
            pe.wait_ge(operand_ready, 4)
            ffn_out("ffn_out0", slice(0, TT))

            norm(2, slice(0, TT))
            pe.wait_ge(operand_ready, 5)
            wide("diff_in", 0, h_hi[:, :, LAT], h_lo[:, :, LAT], T, 0, 4)
            wide("diff_in", 0, h_hi, h_lo, TT, 4, 4)
            values("diff_in", 0, h_hi, h_lo, 4, 8, 4)
            for r in range(12):
                pe.wait_ge(qk_sq, r // 4 + 1)
                if r >= 4:
                    pe.wait_ge(qk_sums_taken, r - 3)
                mm(ps[:, 4 + r % 4, :], ones64, SQ1[:, r, :], start=True, stop=True).then_inc(qk_sums, 1)
            for r in range(8):
                pe.wait_ge(qk_ready, 1 if r < 4 else 2 if r < 6 else 3)
                pe.wait_ge(qk_sums_taken, 12) if r < 4 else pe.wait_ge(drot_taken, r - 3)
                src = (QK1[:, r, :].rearrange("p (a b) -> p a b", b=T) if r < 4
                       else QK1[:, 4 + 2 * (r - 4):6 + 2 * (r - 4), LAT])
                mm(ps[:, 4 + r % 4, :].rearrange("p (a b) -> p a b", b=T), rot_diff, src,
                   start=True, stop=True).then_inc(drot_ready, 1)
            pe.wait_ge(drot_taken, 8)
            pe.wait_ge(sums_taken, group("diff_in", 0, 12) + 2)

            def diff_scores(r):
                h, qb = r // 2, r % 2
                if r >= 2:
                    pe.wait_ge(s_exp, r - 1)
                for m in range(2):
                    rows = slice(64 * m, 64 * m + 64)
                    off = (h % 2) * T + qb * P
                    ins = mm(ps[:, 4 + 2 * (r % 2) + m, :], QK1[rows, h // 2, off:off + P], QK1[rows, 4 + h, :],
                             start=True, stop=True)
                ins.then_inc(s_ready, 1)

            def diff_turn(r):
                pe.wait_ge(s_prob, r + 1)
                if r >= 2:
                    pe.wait_ge(s_copied, r - 1)
                for kb in range(4):
                    ins = nc.tensor.transpose(ps[:, r % 2, kb * P:kb * P + P], P1[:, r % 2, kb * P:kb * P + P], ident)
                ins.then_inc(s_turned, 1)

            def diff_values(h):
                pe.wait_ge(s_copied, 2 * h + 2)
                if h >= 2:
                    pe.wait_ge(so_taken, h - 1)
                for kb in range(4):
                    ins = mm(ps[:, 2 + h % 2, 0:T], V1[:, kb, h * P:h * P + P], PT1[:, h % 2, kb, :],
                             start=kb == 0, stop=kb == 3)
                ins.then_inc(so_ready, 1)
            diff_scores(0)
            for r in range(18):
                if r < 15:
                    diff_scores(r + 1)
                if 1 <= r < 17:
                    diff_turn(r - 1)
                if r >= 3 and r % 2 == 1:
                    diff_values(r // 2 - 1)
            pe.wait_ge(so_sq, 1)
            for r in range(4):
                ins = mm(ps[:, 4 + r, :], ones, SO1[:, 2 * r:2 * r + 2, :], start=True, stop=True)
            ins.then_inc(so_sum, 1)
            pe.wait_ge(operand_ready, 6)
            wide("diff_out", 0, d_hi, d_lo, T)
            norm(3, LAT)
            pe.wait_ge(operand_ready, 7)
            wide("ffn_in1", 0, h_hi[:, :, LAT], h_lo[:, :, LAT], T)
            pe.wait_ge(operand_ready, 8)
            ffn_out("ffn_out1", slice(0, T))

            with pe.Fori(0, LAYERS2) as layer:
                def have(k):
                    pe.wait_ge(operand_ready, layer * 7 + 9 + k)
                    pass_wait()
                have(0)
                wide("ff1_in", layer, l_hi, l_lo, T)
                have(1)
                deep("ff1_out", layer, fh_hi, fh_lo, T, 4)
                norm(layer * 3 + 4, LAT, 0)
                have(2)
                wide("w_in", layer, l_hi, l_lo, T, 0, 12)
                values("w_in", layer, l_hi, l_lo, 2, 12, 2)
                wide("w_in", layer, l_hi, l_lo, T, 14, 2)

                def key_value(i, u, s, turn):
                    wait_tile(s, turn)
                    pe.wait_ge(sums_taken, group("w_in", layer, 15))
                    b = bank("w_in", 16)
                    for c in range(DC):
                        product(ps[:, b, 0:T], c, s, l_hi[:, c, :], l_lo[:, c, :], c == 0, c == DC - 1)
                    for kb in range(2):
                        for c in range(DC):
                            tok = slice(kb * P, kb * P + P)
                            ins = product_rows(ps[:, b, T + kb * P:T + kb * P + P], DC + c, s, l_hi[:, c, tok],
                                               l_lo[:, c, tok], c == 0, c == DC - 1)
                    ins.then_inc(tile_used, 1)
                tiles("w_in", layer, pe, key_value, 16, 1)

                def rates(i, u, s, turn):
                    wait_tile(s, turn)
                    pe.wait_ge(sums_taken, group("w_in", layer, 16))
                    b = bank("w_in", 17)
                    for n in range(4):
                        tok = slice(n * CH, n * CH + CH)
                        o = ps[0:64, b, n * 8:n * 8 + 8]
                        for c in range(DC):
                            mm(o, l_hi[:, c, tok], w_hi[:, s % SPLIT, c, 0:8], start=c == 0, stop=False)
                            mm(o, l_hi[:, c, tok], w_lo[:, raw_slot(s), c, 0:8], start=False, stop=False)
                            ins = mm(o, l_lo[:, c, tok], w_hi[:, s % SPLIT, c, 0:8], start=False, stop=c == DC - 1)
                    ins.then_inc(tile_used, 1)
                tiles("w_in", layer, pe, rates, 17, 1)
                wide("w_gate", layer, l_hi, l_lo, T)

                pe.wait_ge(m_in, layer + 1)
                pe.wait_ge(sums_taken, group("w_gate", layer, 12) + 2)
                mm(ps[:, 4, 0:T], swap64, kc[:, 0, :], start=True, stop=True).then_inc(kswap_ready, 1)
                for r in range(2):
                    pe.wait_ge(n_sq, layer * 2 + r + 1)
                    for j in range(2):
                        ins = mm(ps[:, 5 + j, :], ones, NSQ[:, 2 * j:2 * j + 2, :], start=True, stop=True)
                    ins.then_inc(n_sum, 1)
                pe.wait_ge(kswap_taken, layer + 1)
                pe.wait_ge(n_var, layer * 2 + 2)

                def scores(r):
                    if r >= 2:
                        pe.wait_ge(b_max, layer * 12 + r - 1)
                    for qb in range(2):
                        if r < 4:
                            q, k = qkb[:, r, qb * P:qb * P + P], qkb[:, 4 + r, :]
                        else:
                            h = r - 4
                            rows = slice(64 * (h % 2), 64 * (h % 2) + 64)
                            kv = h // 4
                            q, k = qc[rows, h // 2, qb * P:qb * P + P], kc[rows, 0 if kv == h % 2 else 1, :]
                        ins = mm(ps[:, 4 + r % 2, qb * T:qb * T + T], q, k, start=True, stop=True)
                    ins.then_inc(b_s, 1)

                def turn(r):
                    pe.wait_ge(b_prob, layer * 12 + r + 1)
                    if r >= 2:
                        pe.wait_ge(b_copied, layer * 12 + r - 1)
                    for kb in range(2):
                        for qb in range(2):
                            ins = nc.tensor.transpose(ps[:, 6 + r % 2, kb * T + qb * P:kb * T + qb * P + P],
                                                      TT2[:, r % 2, qb, kb * P:kb * P + P], ident)
                    ins.then_inc(b_turned, 1)

                def mix(r):
                    pe.wait_ge(b_copied, layer * 12 + r + 1)
                    if r >= 2:
                        pe.wait_ge(b_taken, layer * 12 + r - 1)
                    for kb in range(2):
                        if r < 4:
                            v = vb[:, kb, r * P:r * P + P]
                        else:
                            h = r - 4
                            v = vc[:, kb, 0 if h // 4 == h % 2 else 1, :]
                        ins = mm(ps[:, r % 2, 0:T], v, PT2[:, r % 2, kb, :], start=kb == 0, stop=kb == 1)
                    ins.then_inc(b_o, 1)
                scores(0)
                for r in range(14):
                    if r < 11:
                        scores(r + 1)
                    if 1 <= r < 13:
                        turn(r - 1)
                    if r >= 2:
                        mix(r - 2)
                pe.wait_ge(b_taken, layer * 12 + 12)
                pe.wait_ge(b_copied, layer * 12 + 12)

                pe.wait_ge(g_rate, layer + 1)
                pass_wait()
                mm(ps[0:64, 4, 0:16], m64[:, 0, :], gdec[:], start=True, stop=True)
                mm(ps[0:64, 4, 16:32], m64[:, 1, :], gdec[:], start=True, stop=True).then_inc(gd_sums, 1)
                for hp in range(2):
                    w = layer * 2 + hp
                    pe.wait_ge(gd_ready, w + 1)
                    mm(ps[:, 4, :], ones[0:64, :], Tm[:], start=True, stop=True)
                    mm(ps[0:64, 5, :], ones[0:64, 0:64], Um[:], start=True, stop=True)
                    for y in range(8):
                        h, n = 2 * hp + y // 4, y % 4
                        q, k, v = (CV[:, 4 * j + h, n * CH:n * CH + CH] for j in range(3))
                        mm(ps[0:64, 6, y * CH:y * CH + CH], k, k, start=True, stop=True)
                        mm(ps[0:64, 7, y * CH:y * CH + CH], k, q, start=True, stop=True)
                        nc.tensor.transpose(ps[0:64, y // 4, (y % 4) * P:(y % 4) * P + P], k, ident)
                        ins = nc.tensor.transpose(ps[0:64, 2 + y // 4, (y % 4) * P:(y % 4) * P + P], v, ident)
                    ins.then_inc(gd_kk, 1)
                    for lv in range(6):
                        x = w * 6 + lv
                        pe.wait_ge(inv_mask, x + 1)
                        pass_wait()
                        for y in range(8):
                            ins = mm(ps[0:64, 4, y * CH:y * CH + CH], Mm[:, y, :], Tm[:, y, :], start=True, stop=True)
                        ins.then_inc(inv_p, 1)
                        pe.wait_ge(inv_pc, x + 1)
                        pass_wait()
                        for y in range(8):
                            mm(ps[0:64, 5, y * CH:y * CH + CH], Um[:, y, :], Pm[:, y, :], start=True, stop=True)
                            ins = mm(ps[0:64, 6, y * CH:y * CH + CH], Pm[:, y, :], Um[:, y, :], start=True, stop=True)
                        ins.then_inc(inv_done, 1)
                    pe.wait_ge(inv_next, w + 1)
                    pass_wait()
                    for y in range(8):
                        mm(ps[0:64, y // 4, (y % 4) * P:(y % 4) * P + P], Um[:, y, :], vT[:, y, :], start=True, stop=True)
                        ins = mm(ps[:, 4, y * CH:y * CH + CH], kbg[:, y, :], Um[:, y, :], start=True, stop=True)
                    ins.then_inc(uw_ready, 1)
                    pe.wait_ge(uw_taken, w + 1)
                    for n in range(4):
                        x = w * 4 + n
                        if n:
                            pe.wait_ge(sc_next, w * 3 + n)
                            for j in range(2):
                                ins = mm(ps[0:64, 5, j * P:j * P + P], wT[:, 4 * j + n, :], Sst[:, j, :],
                                         start=True, stop=True)
                            ins.then_inc(sc_w, 1)
                        pe.wait_ge(sc_v, x + 1)
                        for j in range(2):
                            o = ps[:, 6, j * T + n * CH:j * T + n * CH + CH]
                            if n:
                                mm(o, Sst[:, j, :], qdec[:, 4 * j + n, :], start=True, stop=False)
                            ins = mm(o, vnew[:, j, :], qkT[:, 4 * j + n, :], start=n == 0, stop=True)
                        if n < 3:
                            for j in range(2):
                                ins = mm(ps[:, 7, j * P:j * P + P], kdec[:, 4 * j + n, :], vnew[:, j, :],
                                         start=True, stop=True)
                        ins.then_inc(sc_s, 1)
                    pe.wait_ge(go_sq, w + 1)
                    mm(ps[:, 4, :], ones, osq[:], start=True, stop=True).then_inc(go_sum, 1)

                have(3)

                def branch(i, u, s, turn):
                    wait_tile(s, turn)
                    pe.wait_ge(sums_taken, group("w_br", layer, u + 1))
                    b = pair("w_br", u)
                    for mi in range(4):
                        for c in range(4):
                            ins = product(ps[:, b + mi // 2, (mi % 2) * T:(mi % 2 + 1) * T], mi * 4 + c, s,
                                          o_hi[:, 4 * (u // 2) + c, :], o_lo[:, 4 * (u // 2) + c, :], c == 0, c == 3)
                    ins.then_inc(tile_used, 1)
                tiles("w_br", layer, pe, branch, per=8)
                have(4)
                wide("w_out", layer, m_hi, m_lo, T)
                norm(layer * 3 + 5, LAT, 1)
                have(5)
                wide("ff2_in", layer, l_hi, l_lo, T)
                have(6)
                deep("ff2_out", layer, fh_hi, fh_lo, T, 4)
                norm(layer * 3 + 6, LAT, 2)

        @block.scalar
        def _(act):
            fn = nc.scalar.activation

            def split_hi(s, turn):
                act.wait_ge(raw_full[raw_slot(s)], turn * 16 + 16 * ((s + ADA_TILES) // 4 + 1))
                act.wait_ge(tile_used, turn * 4 + s + 1)
                nc.scalar.copy(w_hi[:, s % SPLIT], raw[:, raw_slot(s)]).then_inc(hi_done, 1)

            def only_split(phase, layer, first=0, count=None, per=4):
                tiles(phase, layer, act, lambda i, u, s, turn: split_hi(s + SPLIT, turn), first, count, per)

            def norm(q, cols, gains, mean=None):
                width = cols.stop - cols.start
                if mean is not None:
                    act.wait_ge(centred, mean + 1)
                elif q:
                    act.wait_ge(x_ready, q)
                for c in range(DC):
                    fn(SQ[:, c, 0:width], X[:, c, cols], ACT.Square).then_inc(sq_ready, 1)
                act.wait_ge(var_ready, q + 1)
                fn(rr[:, 0:width], rr[:, 0:width], ACT.Sqrt).then_inc(std_ready, 1)
                for c in range(DC):
                    act.wait_ge(scaled, q * DC + c + 1)
                    v = SQ[:, c, 0:width] if mean is None else X[:, c, cols]
                    for part, (gain, shift) in gains(c):
                        ins = fn(v[:, part], v[:, part], ACT.Identity, bias=shift, scale=gain)
                    ins.then_inc(normed, 1)

            def ada_gains(layer, which, parts):
                def of(c):
                    return [(part, (mod[:, layer, 8 * (which + 1) + c, j:j + 1], mod[:, layer, 8 * which + c, j:j + 1]))
                            for part, j in parts]
                return of

            def ln_gains(j):
                def of(c):
                    g, b = C_LN[j]
                    return [(slice(0, T), (cols2[:, g + c:g + c + 1], cols2[:, b + c:b + c + 1]))]
                return of

            def swiglu(phase, layer, dst, width, number):
                def body(i, u, s, turn):
                    split_hi(s + SPLIT, turn)
                    b = pair(phase, u) if width == TT else bank(phase, u)
                    act.wait_ge(tile_used, turn * 4 + s + 1 + SPLIT)
                    act.wait_ge(sums_taken, group(phase, layer, i * 4 + u + 1))
                    fn(dst[:, u % 2, 0:width], ps[:, b, 0:width], ACT.Silu).then_inc(silu_ready, 1)
                tiles(phase, layer, act, body)

            both = [(CTX, 0), (LAT, 1)]
            act.wait_ge(x_in, 32)
            fn(silu_c[:], cols1[:, C_COND:C_COND + 16].rearrange("p (a b) -> p a b", b=2), ACT.Silu
               ).then_inc(silu_c_ready, 1)
            act.wait_ge(lgam_abs, 1)
            fn(small[:, 0:8], small[:, 0:8], ACT.Exp).then_inc(lgam_exp, 1)
            act.wait_ge(lgam_one, 1)
            fn(small[:, 8:16], rr[:, 0:8], ACT.Ln).then_inc(lgam_ln, 1)
            act.wait_ge(lgam_ready, 1)
            act.wait_ge(dist_in, 16)
            for h in range(RET_H):
                if h:
                    act.wait_ge(decays_ready, h)
                for d in range(2):
                    fn(expd[:, d], dist[:, d], ACT.Exp, scale=lgam[:, 4 * d + h:4 * d + h + 1]).then_inc(decays_exp, 1)
            split_hi(0, 0)
            split_hi(1, 0)
            act.wait_ge(mod_scaled, 1)
            norm(0, slice(0, TT), ada_gains(0, 0, both))
            only_split("ret_qkv", 0)
            for h in range(RET_H):
                act.wait_ge(ho_centred, h + 1)
                fn(sqh[:], V[:, h], ACT.Square).then_inc(ho_sq, 1)
                act.wait_ge(ho_var, h + 1)
                fn(rr[:], rr[:], ACT.Sqrt).then_inc(ho_std, 1)

            def gate_silu(i, u, s, turn):
                split_hi(s + SPLIT, turn)
                b = pair("ret_g", u)
                act.wait_ge(tile_used, turn * 4 + s + 1 + SPLIT)
                act.wait_ge(sums_taken, group("ret_g", 0, i * 4 + u + 2))
                fn(gs[:], ps[:, b:b + 2, :], ACT.Silu).then_inc(silu_ready, 1)
            tiles("ret_g", 0, act, gate_silu)
            only_split("ret_out", 0)
            norm(1, slice(0, TT), ada_gains(0, 3, both))
            swiglu("ffn_in0", 0, fs, TT, 8)
            only_split("ffn_out0", 0, 0, 11)
            norm(2, slice(0, TT), ada_gains(1, 0, both))
            only_split("diff_in", 0)
            act.wait_ge(lam_dot, 1)
            fn(lam[:, 0:2], lam[:, 0:2], ACT.Exp).then_inc(lam_exp, 1)
            act.wait_ge(qk_in, 1)
            for j in range(3):
                fn(SQ1[:, 4 * j:4 * j + 4], QK1[:, 4 * j:4 * j + 4], ACT.Square).then_inc(qk_sq, 1)
            for j in range(3):
                act.wait_ge(qk_sums_taken, 4 * j + 4)
                fn(R1[:, 4 * j:4 * j + 4], R1[:, 4 * j:4 * j + 4], ACT.Sqrt).then_inc(qk_std, 1)

            def diff_copy(r):
                h, qb = r // 2, r % 2
                act.wait_ge(s_turned, r + 1)
                if h >= 2:
                    act.wait_ge(so_ready, h - 1)
                nc.scalar.copy(PT1[:, h % 2, :, qb * P:qb * P + P], ps[:, r % 2, :].rearrange("p (a b) -> p a b", b=P)
                               ).then_inc(s_copied, 1)
            for r in range(16):
                act.wait_ge(s_max, r + 1)
                for m in range(2):
                    ins = fn(E1[:, r % 2, m], ps[:, 4 + 2 * (r % 2) + m, :], ACT.Exp, bias=softx[:, r % 2, 2 + m:3 + m],
                             scale=0.125, accum_out=softx[:, r % 2, 4 + m:5 + m])
                ins.then_inc(s_exp, 1)
                if r:
                    diff_copy(r - 1)
            diff_copy(15)
            act.wait_ge(so_taken, 8)
            fn(SO1[:], O1[:], ACT.Square).then_inc(so_sq, 1)
            act.wait_ge(so_var, 1)
            fn(RO1[:], RO1[:], ACT.Sqrt).then_inc(so_std, 1)
            only_split("diff_out", 0)
            norm(3, LAT, ada_gains(1, 3, [(slice(0, T), 1)]))
            swiglu("ffn_in1", 0, fs, T, 30)
            only_split("ffn_out1", 0, 0, 11)

            with act.Fori(0, LAYERS2) as layer:
                swiglu("ff1_in", layer, gs2, T, 52)
                only_split("ff1_out", layer)
                act.wait_ge(params_in, layer * 48 + 48)
                norm(layer * 3 + 4, LAT, ln_gains(0), layer * 3)
                only_split("w_in", layer)

                def gates(i, u, s, turn):
                    split_hi(s + SPLIT, turn)
                    b = bank("w_gate", u)
                    act.wait_ge(tile_used, turn * 4 + s + 1 + SPLIT)
                    act.wait_ge(sums_taken, group("w_gate", layer, u + 2))
                    for mi in range(2):
                        blk = 2 * u + mi
                        ins = fn(gate[:, blk, :], ps[:, b, mi * T:mi * T + T], ACT.Sigmoid,
                                 bias=cols2[:, C_BG + blk:C_BG + blk + 1])
                    ins.then_inc(sums_taken, 1)
                tiles("w_gate", layer, act, gates, per=16)

                act.wait_ge(m_in, layer + 1)
                fn(za[:], za[:], ACT.Silu).then_inc(za_ready, 1)
                act.wait_ge(conv_done, layer + 1)
                fn(CV[:], CV[:], ACT.Silu).then_inc(conv_silu, 1)
                act.drain()
                for r in range(2):
                    if r:
                        act.wait_ge(n_done, layer * 2 + r)
                    fn(NSQ[:], CV[:, 4 * r:4 * r + 4], ACT.Square).then_inc(n_sq, 1)
                    act.wait_ge(n_var, layer * 2 + r + 1)
                    fn(NR[:], NR[:], ACT.Sqrt).then_inc(n_std, 1)

                def turned_copy(r):
                    act.wait_ge(b_turned, layer * 12 + r + 1)
                    if r >= 2:
                        act.wait_ge(b_o, layer * 12 + r - 1)
                    nc.scalar.copy(PT2[:, r % 2], ps[:, 6 + r % 2, :].rearrange("p (a c) -> p a c", c=T)
                                   ).then_inc(b_copied, 1)
                for r in range(12):
                    act.wait_ge(b_max, layer * 12 + r + 1)
                    for qb in range(2):
                        ins = fn(TT2[:, r % 2, qb], TT2[:, r % 2, qb], ACT.Exp, bias=softx[:, r % 2, 2 + qb:3 + qb],
                                 scale=1.0 if r < 4 else 0.125, accum_out=softx[:, r % 2, 4 + qb:5 + qb])
                    if r >= 4:
                        ins = fn(softx[:, r % 2, 8:10], softx[:, r % 2, 8:10], ACT.Exp)
                    ins.then_inc(b_exp, 1)
                    if r:
                        turned_copy(r - 1)
                turned_copy(11)
                act.wait_ge(g_lin, layer + 1)
                fn(bt[:, 2], bt[:, 2], ACT.Exp)
                fn(bt[:, 3, 0:4], rows2[0:64, R_ALOG:R_ALOG + 4], ACT.Exp).then_inc(g_exp, 1)
                act.wait_ge(g_mid, layer + 1)
                fn(bt[:, 5], bt[:, 4], ACT.Ln)
                fn(bt[:, 0], bt[:, 0], ACT.Exp, scale=-1.0).then_inc(g_ln, 1)
                act.wait_ge(gd_taken, layer + 1)
                fn(gexp[:], gcum[:], ACT.Exp)
                fn(gsuf[:], gsuf[:], ACT.Exp).then_inc(gd_exp, 1)
                for hp in range(2):
                    w = layer * 2 + hp
                    act.wait_ge(gd_kk, w + 1)
                    act.wait_ge(gd_diff, w + 1)
                    fn(gcb[:], ps[:, 4, :].rearrange("p (a b) -> p a b", b=CH), ACT.Exp)
                    fn(DT[:], DT[:], ACT.Exp).then_inc(gd_decay, 1)
                    act.wait_ge(go_copied, w + 1)
                    fn(osq[:], oA[:], ACT.Square).then_inc(go_sq, 1)
                    act.wait_ge(go_var, w + 1)
                    fn(rr[:], rr[:], ACT.Sqrt).then_inc(go_std, 1)
                only_split("w_br", layer)
                only_split("w_out", layer)
                norm(layer * 3 + 5, LAT, ln_gains(1), layer * 3 + 1)
                swiglu("ff2_in", layer, gs2, T, 84)
                only_split("ff2_out", layer)
                norm(layer * 3 + 6, LAT, ln_gains(2), layer * 3 + 2)

        @block.vector
        def _(dve):
            tt, ts, stt, copy = (nc.vector.tensor_tensor, nc.vector.tensor_scalar, nc.vector.scalar_tensor_tensor,
                                 nc.vector.tensor_copy)

            def split_lo(s, turn):
                dve.wait_ge(hi_done, turn * 4 + s + 1)
                tt(w_lo[:, raw_slot(s)], raw[:, raw_slot(s)], w_hi[:, s % SPLIT].bitcast(F32), ALU.subtract
                   ).then_inc(lo_done, 1)

            def each(phase, layer, take, first=0, count=None, per=4):
                def body(i, u, s, turn):
                    split_lo(s + SPLIT, turn)
                    dve.wait_ge(tile_used, turn * 4 + s + 1 + SPLIT)
                    take(i, u)
                tiles(phase, layer, dve, body, first, count, per)

            def halves(hi, lo, src):
                copy(hi, src)
                dve.drain()
                return tt(lo, src, hi.bitcast(F32), ALU.subtract)

            def norm(q, cols, hi, lo, mean=None, eps=EPS):
                width = cols.stop - cols.start
                r = rr[:, 0:width]
                if mean is not None:
                    dve.wait_ge(mean_ready, mean + 1)
                    ts(r, ps[:, 4, 0:width], 1.0 / D, None, ALU.mult)
                    dve.drain()
                    tt(X[:, :, cols], X[:, :, cols], r.unsqueeze(1).to_broadcast([P, DC, width]), ALU.subtract
                       ).then_inc(centred, 1)
                dve.wait_ge(square_sum, q + 1)
                ts(r, ps[:, 5, 0:width], 1.0 / D, eps, ALU.mult, ALU.add).then_inc(var_ready, 1)
                dve.wait_ge(std_ready, q + 1)
                nc.vector.reciprocal(r, r)
                dve.drain()
                for c in range(DC):
                    v = SQ[:, c, 0:width] if mean is None else X[:, c, cols]
                    tt(v, X[:, c, cols], r, ALU.mult).then_inc(scaled, 1)
                v = SQ[:, :, 0:width] if mean is None else X[:, :, cols]
                for c in range(DC):
                    dve.wait_ge(normed, q * DC + c + 1)
                    copy(hi[:, c, :], v[:, c, :])
                dve.drain()
                tt(lo, v, hi.bitcast(F32), ALU.subtract).then_inc(operand_ready, 1)

            def swiglu(phase, layer, gates, prods, hi, lo, width, number):
                def take(i, u):
                    b = pair(phase, u) if width == TT else bank(phase, u)
                    up = ps[:, b + 1, 0:TT] if width == TT else ps[:, b, T:TT]
                    dve.wait_ge(silu_ready, layer * 64 + i * 4 + u + number + 1)
                    tt(prods[:, u % 2, 0:width], gates[:, u % 2, 0:width], up, ALU.mult)
                    dve.drain()
                    blk = bass.ds(i * 4 + u, 1)
                    halves(hi[:, blk, 0:width], lo[:, blk, 0:width], prods[:, u % 2:u % 2 + 1, 0:width]
                           ).then_inc(sums_taken, 1)
                each(phase, layer, take)
                dve.drain()
                copy(small[:, 15:16], small[:, 14:15]).then_inc(operand_ready, 1)

            dve.sem_inc(sums_taken, 2)
            dve.sem_inc(layer_used, 1)
            nc.vector.memset(small[:], 0.0)
            dve.wait_ge(logit_in, 16)
            dve.drain()
            stt(small[:, 0:8], lgam[:], -1.0, lgam[:], ALU.mult, ALU.min).then_inc(lgam_abs, 1)
            dve.wait_ge(lgam_exp, 1)
            ts(rr[:, 0:8], small[:, 0:8], 1.0, None, ALU.add).then_inc(lgam_one, 1)
            dve.wait_ge(lgam_ln, 1)
            ts(rr[:, 8:16], rr[:, 0:8], -1.0, 1e-30, ALU.add, ALU.max)
            dve.drain()
            nc.vector.reciprocal(rr[:, 8:16], rr[:, 8:16])
            dve.drain()
            tt(rr[:, 8:16], rr[:, 8:16], small[:, 0:8], ALU.mult)
            dve.drain()
            tt(small[:, 8:16], small[:, 8:16], rr[:, 8:16], ALU.mult)
            dve.drain()
            stt(lgam[:], lgam[:], 0.0, small[:, 8:16], ALU.min, ALU.subtract).then_inc(lgam_ready, 1)
            dve.wait_ge(x_in, 32)

            def ada_copy(t, u):
                dve.wait_ge(ada_ready, t + 1)
                copy(ada_row[:, u % 2], ps[0:2, 4 + u % 2, 0:T]).then_inc(ada_copied, 1)

            def ada_add(t, u):
                dve.wait_ge(ada_turned, t + 1)
                tt(mod[:].rearrange("p l c v -> p (l c) v")[:, bass.ds(t * 2, 2), :],
                   ps[:, 6 + u % 2, 0:4].rearrange("p (a b) -> p a b", b=2),
                   cols1[:, bass.ds(t * 2, 2)].unsqueeze(2).to_broadcast([P, 2, 2]), ALU.add).then_inc(mod_ready, 1)
            for u in range(4):
                ada_copy(u, u)
                if u:
                    ada_add(u - 1, u - 1)
            with dve.Fori(1, ADA_TILES // 4) as i:
                for u in range(4):
                    ada_copy(i * 4 + u, u)
                    ada_add(i * 4 + u - 1, (u - 1) % 4)
            ada_add(ADA_TILES - 1, 3)
            dve.drain()
            for l in range(2):
                for w in (1, 4):
                    ins = ts(mod[:, l, 8 * w:8 * w + 8, :], mod[:, l, 8 * w:8 * w + 8, :], 1.0, None, ALU.add)
            ins.then_inc(mod_scaled, 1)
            split_lo(0, 0)
            split_lo(1, 0)

            norm(0, slice(0, TT), h_hi[:], h_lo[:])
            dve.wait_ge(decays_ready, RET_H)

            def take_qk(i, u):
                b = pair("ret_qkv", u)
                copy(QK[:, bass.ds(i * 8 + 2 * u, 2), :], ps[:, b:b + 2, :]).then_inc(sums_taken, 1)

            def take_v(i, u):
                b = pair("ret_qkv", u)
                dst = V[:, bass.ds(i * 2 + u // 2, 1), :, (u % 2) * T:(u % 2 + 1) * T]
                copy(dst.rearrange("p a b c -> p (a b) c"), ps[:, b:b + 2, :].rearrange("p b (a c) -> p (b a) c", c=T)
                     ).then_inc(sums_taken, 1)
            each("ret_qkv", 0, take_qk, 0, 8)
            each("ret_qkv", 0, take_v, 8, 8)
            dve.drain()

            def rotate(x, sums, cos, sin, tmp):
                tt(tmp[:, 0], x, cos, ALU.mult)
                tt(tmp[:, 1], sums, sin, ALU.mult)
                dve.drain()
                return tt(x, tmp[:, 0], tmp[:, 1], ALU.add)
            dve.wait_ge(tables_in, 48)
            for r in range(8):
                dve.wait_ge(rot_ready, r + 1)
                rotate(QK[:, 2 * r:2 * r + 2, LAT], ps[:, 4 + r % 4, :].rearrange("p (a b) -> p a b", b=T),
                       rope_r[:, 0], rope_r[:, 1], rtmp).then_inc(rot_taken, 1)
                dve.drain()
            for h in range(RET_H):
                dve.wait_ge(att_ready, h + 1)
                stt(att[:, 0:4, :], ps[:, 4:6, :].rearrange("p b (a c) -> p (b a) c", c=T), 0.0625, DM[:, h],
                    ALU.mult, ALU.mult)
                stt(att[:, 4:6, :], ps[:, 6, :].rearrange("p (a c) -> p a c", c=T), 0.0625, DM[:, h, 2:4],
                    ALU.mult, ALU.mult).then_inc(att_decayed, 1)
                dve.wait_ge(ho_ready, h + 1)
                copy(V[:, h], ps[:, 0:4, :]).then_inc(ho_taken, 1)
                dve.wait_ge(ho_mean, h + 1)
                ts(rr[:], ps[:, 7, :], 1.0 / TT, None, ALU.mult)
                dve.drain()
                tt(V[:, h], V[:, h], rr[:].unsqueeze(1).to_broadcast([P, 4, TT]), ALU.subtract).then_inc(ho_centred, 1)
                dve.wait_ge(ho_sqsum, h + 1)
                ts(rr[:], ps[:, 4, :], 1.0 / TT, EPS, ALU.mult, ALU.add).then_inc(ho_var, 1)
                dve.wait_ge(ho_std, h + 1)
                nc.vector.reciprocal(rr[:], rr[:])
                dve.drain()
                tt(V[:, h], V[:, h], rr[:].unsqueeze(1).to_broadcast([P, 4, TT]), ALU.mult)
                dve.drain()
            Vb = V[:].rearrange("p h b t -> p (h b) t")

            def take_g(i, u):
                dve.wait_ge(silu_ready, i * 4 + u + 1)
                for mi in range(2):
                    blk = i * 8 + 2 * u + mi
                    stt(gp[:, mi:mi + 1, :], Vb[:, bass.ds(blk, 1), :], cols1[:, bass.ds(blk + C_RETG, 1)],
                        gs[:, mi:mi + 1, :], ALU.mult, ALU.mult)
                dve.drain()
                two = bass.ds(i * 8 + 2 * u, 2)
                halves(y_hi[:, two, :], y_lo[:, two, :], gp[:]).then_inc(sums_taken, 1)
            each("ret_g", 0, take_g)
            dve.drain()
            copy(small[:, 15:16], small[:, 14:15]).then_inc(operand_ready, 1)

            def add_gated(layer, which, m, sums, parts):
                for part, cols, j in parts:
                    ins = stt(X[:, m, cols], sums[:, part], mod[:, layer, 8 * which + m, j:j + 1], X[:, m, cols],
                              ALU.mult, ALU.add)
                return ins
            both = [(CTX, CTX, 0), (LAT, LAT, 1)]
            lat = [(slice(0, T), LAT, 1)]

            def take_ret_out(i, u):
                if u % 2:
                    b = pair("ret_out", u // 2)
                    for mi in range(2):
                        ins = add_gated(0, 2, 2 * (u // 2) + mi, ps[:, b + mi, :], both)
                    ins.then_inc(sums_taken, 1)
            each("ret_out", 0, take_ret_out, per=16)
            dve.drain()
            copy(small[:, 15:16], small[:, 14:15]).then_inc(x_ready, 1)
            norm(1, slice(0, TT), h_hi[:], h_lo[:])
            swiglu("ffn_in0", 0, fs, fp, hid_hi, hid_lo, TT, 8)

            def ffn_out(phase, layer, parts):
                each(phase, 0, lambda i, u: None, 0, 11)
                for m in range(DC):
                    ins = add_gated(layer, 5, m, ps[:, m, :], parts)
                    if m >= DC - 2:
                        ins.then_inc(sums_taken, 1)
                dve.drain()
            ffn_out("ffn_out0", 0, both)
            copy(small[:, 15:16], small[:, 14:15]).then_inc(x_ready, 1)

            norm(2, slice(0, TT), h_hi[:], h_lo[:])

            def take_diff(i, u):
                b = pair("diff_in", u) if u >= 4 else bank("diff_in", u)
                if u < 4:
                    ins = copy(QK1[:, u, :], ps[:, b, :])
                elif u < 8:
                    ins = copy(QK1[:, 4 + 2 * (u - 4):6 + 2 * (u - 4), :], ps[:, b:b + 2, :])
                else:
                    ins = copy(V1[:, :, (u - 8) * T:(u - 7) * T], ps[:, b:b + 2, :].rearrange("p b (a c) -> p (b a) c", c=T))
                ins.then_inc(sums_taken, 1)
            each("diff_in", 0, take_diff, per=16)
            dve.wait_ge(lam_in, 16)
            tt(lamv[:, 0:4:2], lamv[:, 0:4:2], lamv[:, 1:4:2], ALU.mult)
            dve.drain()
            nc.vector.tensor_reduce(lam[:, 0:2], lamv[:, 0:4:2], AX, ALU.add).then_inc(lam_dot, 1)
            dve.drain()
            copy(small[:, 15:16], small[:, 14:15]).then_inc(qk_in, 1)
            dve.wait_ge(lam_exp, 1)
            stt(lam[:, 2:3], lam[:, 1:2], -LAMBDA_INIT, lam[:, 0:1], ALU.add, ALU.subtract)
            for j in range(4):
                if j < 3:
                    for r in range(4 * j, 4 * j + 4):
                        dve.wait_ge(qk_sums, r + 1)
                        ts(R1[:, r], ps[:, 4 + r % 4, :], 1.0 / 64, EPS, ALU.mult, ALU.add).then_inc(qk_sums_taken, 1)
                if j:
                    some, gain = slice(4 * j - 4, 4 * j), C_DQG if j == 1 else C_DKG
                    dve.wait_ge(qk_std, j)
                    nc.vector.reciprocal(R1[:, some], R1[:, some])
                    dve.drain()
                    stt(QK1[:, some], QK1[:, some], cols1[:, gain:gain + 1], R1[:, some], ALU.mult, ALU.mult
                        ).then_inc(qk_ready, 1)
            dtmp = SQ1[:, 0:2, :].rearrange("p t (a b) -> p t a b", b=T)
            dve.drain()
            for r in range(8):
                dve.wait_ge(drot_ready, r + 1)
                x = (QK1[:, r, :].rearrange("p (a b) -> p a b", b=T) if r < 4
                     else QK1[:, 4 + 2 * (r - 4):6 + 2 * (r - 4), LAT])
                cos, sin = (rope_d[:, j].unsqueeze(1).to_broadcast([P, 2, T]) for j in range(2))
                rotate(x, ps[:, 4 + r % 4, :].rearrange("p (a b) -> p a b", b=T), cos, sin, dtmp).then_inc(drot_taken, 1)
                dve.drain()

            def diff_max(r):
                dve.wait_ge(s_ready, r + 1)
                b = 4 + 2 * (r % 2)
                nc.vector.tensor_reduce(softx[:, r % 2, 0:2], ps[:, b:b + 2, :], AX, ALU.max)
                dve.drain()
                ts(softx[:, r % 2, 2:4], softx[:, r % 2, 0:2], -0.125, None, ALU.mult).then_inc(s_max, 1)

            def diff_prob(r):
                dve.wait_ge(s_exp, r + 1)
                sx = softx[:, r % 2]
                nc.vector.reciprocal(sx[:, 6:8], sx[:, 4:6])
                dve.drain()
                tt(sx[:, 7:8], sx[:, 7:8], lam[:, 2:3], ALU.mult)
                if r >= 2:
                    dve.wait_ge(s_turned, r - 1)
                ts(P1[:, r % 2], E1[:, r % 2, 0], sx[:, 6:7], None, ALU.mult)
                dve.drain()
                stt(P1[:, r % 2], E1[:, r % 2, 1], sx[:, 7:8], P1[:, r % 2], ALU.mult, ALU.add).then_inc(s_prob, 1)

            def diff_out_head(h):
                dve.wait_ge(so_ready, h + 1)
                copy(O1[:, h, :], ps[:, 2 + h % 2, 0:T]).then_inc(so_taken, 1)
            for r in range(20):
                if r < 16:
                    diff_max(r)
                if 1 <= r < 17:
                    diff_prob(r - 1)
                if r >= 5 and r % 2 == 1:
                    diff_out_head((r - 5) // 2)
            dve.wait_ge(so_sum, 1)
            for r in range(4):
                ins = ts(RO1[:, 2 * r:2 * r + 2, :], ps[:, 4 + r, :].rearrange("p (a b) -> p a b", b=T), 1.0 / P, EPS,
                         ALU.mult, ALU.add)
            ins.then_inc(so_var, 1)
            dve.wait_ge(so_std, 1)
            nc.vector.reciprocal(RO1[:], RO1[:])
            dve.drain()
            tt(O1[:], O1[:], RO1[:], ALU.mult)
            dve.drain()
            ts(O1[:], O1[:], cols1[:, C_SUB:C_SUB + 1], 1.0 - LAMBDA_INIT, ALU.mult, ALU.mult)
            dve.drain()
            halves(d_hi[:], d_lo[:], O1[:]).then_inc(operand_ready, 1)

            def take_diff_out(i, u):
                b = bank("diff_out", u)
                for mi in range(2):
                    ins = add_gated(1, 2, 2 * u + mi, ps[:, b, mi * T:mi * T + T], lat)
                ins.then_inc(sums_taken, 1)
            each("diff_out", 0, take_diff_out, per=8)
            dve.drain()
            copy(small[:, 15:16], small[:, 14:15]).then_inc(x_ready, 1)
            norm(3, LAT, h_hi[:, :, LAT], h_lo[:, :, LAT])
            swiglu("ffn_in1", 0, fs, fp, hid_hi, hid_lo, T, 30)
            ffn_out("ffn_out1", 1, lat)
            halves(l_hi[:], l_lo[:], X[:, :, LAT]).then_inc(operand_ready, 1)

            with dve.Fori(0, LAYERS2) as layer:
                def scaled_sum(phase, width_pair, factor):
                    def take(m, b):
                        x = X[:, m, LAT]
                        ts(x, x, ALPHA, None, ALU.mult)
                        dve.drain()
                        sums = (ps[:, b:b + 2, 0:T] if width_pair else ps[:, b, :].rearrange("p (a c) -> p a c", c=T))
                        stt(x, sums, factor, x, ALU.mult, ALU.add).then_inc(sums_taken, 1)
                    return take

                def ff_out(phase):
                    add = scaled_sum(phase, True, 0.5)

                    def take(i, u):
                        if u % 4 == 3:
                            add(bass.ds(i * 4 + 2 * (u // 4), 2), pair(phase, u // 4))
                    each(phase, layer, take, per=8)
                    dve.drain()
                    copy(small[:, 15:16], small[:, 14:15]).then_inc(x_ready, 1)

                swiglu("ff1_in", layer, gs2, gp2, fh_hi, fh_lo, T, 52)
                ff_out("ff1_out")
                norm(layer * 3 + 4, LAT, l_hi[:], l_lo[:], layer * 3, LN_EPS)

                def take_in(i, u):
                    b = bank("w_in", u)

                    def fm(dst, col):
                        for mi in range(2):
                            ins = ts(dst[mi], ps[:, b, mi * T:mi * T + T], cols2[:, C_BIN + col + mi:C_BIN + col + mi + 1],
                                     None, ALU.add)
                        return ins
                    if u < 6:
                        ins = fm([QKVp[:, 2 * u + mi, 3:T + 3] for mi in range(2)], 2 * u)
                    elif u < 8:
                        ins = fm([za[:, 2 * (u - 6) + mi, :] for mi in range(2)], 2 * u)
                    elif u < 12:
                        ins = fm([qkb[:, 2 * (u - 8) + mi, :] for mi in range(2)], 2 * u)
                    elif u < 14:
                        c0 = (u - 12) * T
                        ins = tt(vb[:, :, c0:c0 + T], ps[:, b, :].rearrange("p (a c) -> p a c", c=T),
                                 rows2[:, R_VB + c0:R_VB + c0 + T].unsqueeze(1).to_broadcast([P, 2, T]), ALU.add)
                    elif u < 16:
                        ins = fm([qc[:, 2 * (u - 14) + mi, :] for mi in range(2)], 24 + 2 * (u - 14))
                    elif u == 16:
                        ts(kc[:, 0, :], ps[:, b, 0:T], cols2[:, C_BIN + 28:C_BIN + 29], None, ALU.add)
                        vv = ps[:, b, T:TT].rearrange("p (a c) -> p a c", c=P)
                        bias = rows2[:, R_VC:R_VC + P].unsqueeze(1).to_broadcast([P, 2, P])
                        tt(vc[:, :, 0, :], vv, bias, ALU.add)
                        tt(vc[:, :, 1, 0:64], vv[:, :, 64:128], bias[:, :, 64:128], ALU.add)
                        ins = tt(vc[:, :, 1, 64:128], vv[:, :, 0:64], bias[:, :, 0:64], ALU.add)
                    else:
                        ins = tt(ba[:], ps[0:64, b, 0:32].rearrange("p (a c) -> p a c", c=8),
                                 rows2[0:64, R_BETA:R_BETA + 8].unsqueeze(1).to_broadcast([64, 4, 8]), ALU.add)
                    ins.then_inc(sums_taken, 1)
                each("w_in", layer, take_in, per=32)
                nc.vector.memset(QKVp[:, :, 0:3], 0.0)
                dve.drain()
                copy(small[:, 15:16], small[:, 14:15]).then_inc(m_in, 1)
                tiles("w_gate", layer, dve, lambda i, u, s, turn: split_lo(s + SPLIT, turn), per=16)

                for tap in range(4):
                    for blk in range(12):
                        w = cols2[:, C_CONV + tap * 12 + blk:C_CONV + tap * 12 + blk + 1]
                        x = QKVp[:, blk, tap:tap + T]
                        if tap == 0:
                            ins = ts(CV[:, blk, :], x, w, None, ALU.mult)
                        else:
                            ins = stt(CV[:, blk, :], x, w, CV[:, blk, :], ALU.mult, ALU.add)
                    if tap == 3:
                        ins.then_inc(conv_done, 1)
                    else:
                        dve.drain()
                dve.wait_ge(kswap_ready, layer + 1)
                copy(kc[:, 1, :], ps[:, 4, 0:T]).then_inc(kswap_taken, 1)
                dve.wait_ge(conv_silu, layer + 1)
                for r in range(2):
                    dve.wait_ge(n_sum, layer * 2 + r + 1)
                    ts(NR[:], ps[:, 5:7, :].rearrange("p b (a c) -> p (b a) c", c=T), 1.0, EPS, ALU.mult, ALU.add
                       ).then_inc(n_var, 1)
                    dve.wait_ge(n_std, layer * 2 + r + 1)
                    nc.vector.reciprocal(NR[:], NR[:])
                    dve.drain()
                    x = CV[:, 4 * r:4 * r + 4]
                    stt(x, x, P ** -0.5 if r == 0 else 1.0, NR[:], ALU.mult, ALU.mult).then_inc(n_done, 1)
                dve.drain()

                dve.wait_ge(bias_ready, layer + 1)
                dve.wait_ge(band_in, 48)

                def soft_max(r):
                    dve.wait_ge(b_s, layer * 12 + r + 1)
                    if r >= 2:
                        dve.wait_ge(b_turned, layer * 12 + r - 1)
                    sx = softx[:, r % 2]
                    s = ps[:, 4 + r % 2, :].rearrange("p (a c) -> p a c", c=T)
                    if r < 4:
                        stt(TT2[:, r % 2], s, P ** -0.5, relB[:, r], ALU.mult, ALU.add)
                    else:
                        stt(TT2[:, r % 2], bandC[:], 8.0 * 2.0 ** -(r - 3), s, ALU.mult, ALU.add)
                    dve.drain()
                    nc.vector.tensor_reduce(sx[:, 0:2], TT2[:, r % 2], AX, ALU.max)
                    dve.drain()
                    if r < 4:
                        ins = ts(sx[:, 2:4], sx[:, 0:2], -1.0, None, ALU.mult)
                    else:
                        sink = rows2[:, R_SINK + r - 4:R_SINK + r - 3]
                        ts(sx[:, 0:2], sx[:, 0:2], 0.125, sink, ALU.mult, ALU.max)
                        dve.drain()
                        ts(sx[:, 2:4], sx[:, 0:2], -1.0, None, ALU.mult)
                        dve.drain()
                        ins = ts(sx[:, 8:10], sx[:, 2:4], sink, None, ALU.add)
                    ins.then_inc(b_max, 1)

                def soft_prob(r):
                    dve.wait_ge(b_exp, layer * 12 + r + 1)
                    sx = softx[:, r % 2]
                    if r >= 4:
                        tt(sx[:, 4:6], sx[:, 4:6], sx[:, 8:10], ALU.add)
                        dve.drain()
                    nc.vector.reciprocal(sx[:, 6:8], sx[:, 4:6])
                    dve.drain()
                    for qb in range(2):
                        ins = ts(TT2[:, r % 2, qb], TT2[:, r % 2, qb], sx[:, 6 + qb:7 + qb], None, ALU.mult)
                    ins.then_inc(b_prob, 1)

                def soft_out(r):
                    dve.wait_ge(b_o, layer * 12 + r + 1)
                    if r < 4:
                        rows, blk = slice(0, P), 4 + r
                    else:
                        h = r - 4
                        rows, blk = slice(64 * (h % 2), 64 * (h % 2) + 64), 8 + h // 2
                    halves(o_hi[rows, blk, :], o_lo[rows, blk, :], ps[rows, r % 2, 0:T]).then_inc(b_taken, 1)
                for r in range(15):
                    if r < 12:
                        soft_max(r)
                    if 1 <= r < 13:
                        soft_prob(r - 1)
                    if r >= 3:
                        soft_out(r - 3)
                dve.drain()

                bh = ba[:, :, 0:4].rearrange("p n h -> p h n")
                ah = ba[:, :, 4:8].rearrange("p n h -> p h n")
                b4 = [bt[:, j, :].rearrange("p (h n) -> p h n", n=4) for j in range(8)]
                copy(b4[0], bh)
                tt(b4[1], ah, rows2[0:64, R_DT:R_DT + 4].unsqueeze(2).to_broadcast([64, 4, 4]), ALU.add)
                dve.drain()
                stt(bt[:, 2], bt[:, 1], -1.0, bt[:, 1], ALU.mult, ALU.min).then_inc(g_lin, 1)
                dve.wait_ge(g_exp, layer + 1)
                ts(bt[:, 4], bt[:, 2], 1.0, None, ALU.add).then_inc(g_mid, 1)
                dve.drain()
                ts(bt[:, 6], bt[:, 4], -1.0, 1e-30, ALU.add, ALU.max)
                dve.drain()
                nc.vector.reciprocal(bt[:, 6], bt[:, 6])
                dve.drain()
                tt(bt[:, 6], bt[:, 6], bt[:, 2], ALU.mult)
                ts(bt[:, 1], bt[:, 1], 0.0, None, ALU.max)
                dve.drain()
                dve.wait_ge(g_ln, layer + 1)
                tt(bt[:, 6], bt[:, 6], bt[:, 5], ALU.mult)
                ts(bt[:, 0], bt[:, 0], 1.0, None, ALU.add)
                dve.drain()
                tt(bt[:, 6], bt[:, 6], bt[:, 1], ALU.add)
                nc.vector.reciprocal(beta[:], b4[0])
                dve.drain()
                stt(gdec[:], b4[6], -1.0, bt[:, 3, 0:4].unsqueeze(2).to_broadcast([64, 4, 4]), ALU.mult, ALU.mult
                    ).then_inc(g_rate, 1)
                dve.wait_ge(gd_sums, layer + 1)
                copy(gcum[:], ps[0:64, 4, 0:16].rearrange("p (a b) -> p a b", b=4))
                copy(gsuf[:], ps[0:64, 4, 16:32].rearrange("p (a b) -> p a b", b=4)).then_inc(gd_taken, 1)
                dve.wait_ge(gd_exp, layer + 1)
                tt(gexp[:], gexp[:], beta[:], ALU.mult)
                dve.drain()
                dve.wait_ge(za_ready, layer + 1)

                def over_systems(m):
                    return m.unsqueeze(1).to_broadcast([64, 8, CH])

                def per_token(t, hp, width):
                    v = t[:, 2 * hp:2 * hp + 2, :].rearrange("p h n -> p (h n)")
                    return v.unsqueeze(2).to_broadcast([64, 8, width])
                for hp in range(2):
                    w = layer * 2 + hp
                    tt(Tm[:], over_systems(m64[:, 0, :]), per_token(gdec, hp, CH), ALU.mult)
                    tt(Um[:], over_systems(ident[0:64, 0:64]), per_token(beta, hp, CH), ALU.mult).then_inc(gd_ready, 1)
                    dve.wait_ge(gd_kk, w + 1)

                    def sums64(b):
                        return ps[0:64, b, :].rearrange("p (a c) -> p a c", c=CH)
                    tt(DT[:], sums64(4), per_token(gcum, hp, CH), ALU.subtract)
                    dve.drain()
                    ts(DT[:], DT[:], 0.0, None, ALU.min).then_inc(gd_diff, 1)
                    copy(kT[:], ps[0:64, 0:2, :].rearrange("p b (a c) -> p (b a) c", c=P))
                    tt(vT[:], ps[0:64, 2:4, :].rearrange("p b (a c) -> p (b a) c", c=P), per_token(beta, hp, P), ALU.mult)
                    dve.drain()
                    tt(kbg[:], kT[:], per_token(gexp, hp, P), ALU.mult)
                    tt(kdec[:], kT[:], per_token(gsuf, hp, P), ALU.mult)
                    dve.wait_ge(gd_decay, w + 1)
                    tt(DT[:], DT[:], over_systems(m64[:, 0, :]), ALU.mult)
                    dve.drain()
                    tt(qkT[:], sums64(7), DT[:], ALU.mult)
                    tt(LT[:], sums64(6), DT[:], ALU.mult)
                    dve.drain()
                    tt(LT[:], LT[:], over_systems(m64[:, 2, :]), ALU.mult)
                    dve.drain()
                    tt(LT[:], sums64(5), LT[:], ALU.mult)
                    copy(Tm[:], over_systems(ident[0:64, 0:64]))
                    copy(Um[:], over_systems(ident[0:64, 0:64]))
                    for lv in range(6):
                        x = w * 6 + lv
                        dve.drain()
                        tt(Mm[:], LT[:], over_systems(m64[:, 3 + lv, :]), ALU.mult).then_inc(inv_mask, 1)
                        dve.wait_ge(inv_p, x + 1)
                        copy(Pm[:], sums64(4)).then_inc(inv_pc, 1)
                        dve.wait_ge(inv_done, x + 1)
                        tt(Tm[:], Tm[:], sums64(5), ALU.subtract)
                        ins = tt(Um[:], Um[:], sums64(6), ALU.subtract)
                    ins.then_inc(inv_next, 1)
                    dve.wait_ge(uw_ready, w + 1)
                    copy(uu[:], ps[0:64, 0:2, :].rearrange("p b (a c) -> p (b a) c", c=P))
                    copy(wT[:], ps[:, 4, :].rearrange("p (a c) -> p a c", c=CH))
                    tt(qdec[:], CV[:, 2 * hp:2 * hp + 2, :].rearrange("p h (n c) -> p (h n) c", c=CH), gcb[:],
                       ALU.mult).then_inc(uw_taken, 1)
                    dve.drain()
                    for n in range(4):
                        u_n = uu[:, n:8:4, :]
                        if n:
                            dve.wait_ge(sc_w, w * 3 + n)
                            tt(vnew[:], u_n, ps[0:64, 5, 0:T].rearrange("p (a c) -> p a c", c=P), ALU.subtract
                               ).then_inc(sc_v, 1)
                        else:
                            copy(vnew[:], u_n).then_inc(sc_v, 1)
                        dve.wait_ge(sc_s, w * 4 + n + 1)
                        if n < 3:
                            for j in range(2):
                                new = ps[:, 7, j * P:j * P + P]
                                if n:
                                    ins = stt(Sst[:, j, :], Sst[:, j, :], gcb[:, 4 * j + n, CH - 1:CH], new,
                                              ALU.mult, ALU.add)
                                else:
                                    ins = copy(Sst[:, j, :], new)
                            ins.then_inc(sc_next, 1)
                            dve.drain()
                    copy(oA[:], ps[:, 6, :].rearrange("p (a b) -> p a b", b=T)).then_inc(go_copied, 1)
                    dve.wait_ge(go_sum, w + 1)
                    ts(rr[:], ps[:, 4, :], 1.0 / P, EPS, ALU.mult, ALU.add).then_inc(go_var, 1)
                    dve.wait_ge(go_std, w + 1)
                    nc.vector.reciprocal(rr[:], rr[:])
                    dve.drain()
                    tt(oA[:], oA[:], rr[:].rearrange("p (a b) -> p a b", b=T), ALU.mult)
                    dve.drain()
                    stt(oA[:], oA[:], cols2[:, C_GDN:C_GDN + 1], za[:, 2 * hp:2 * hp + 2, :], ALU.mult, ALU.mult)
                    dve.drain()
                    ins = halves(o_hi[:, 2 * hp:2 * hp + 2, :], o_lo[:, 2 * hp:2 * hp + 2, :], oA[:])
                    dve.drain()
                ins.then_inc(operand_ready, 1)

                def take_branch(i, u):
                    b = pair("w_br", u)
                    br, m0 = u // 2, 4 * (u % 2)
                    if u == 0:
                        dve.wait_ge(sums_taken, group("w_gate", layer, 12) + 2)
                    sums = ps[:, b:b + 2, :].rearrange("p b (a c) -> p (b a) c", c=T)
                    g = gate[:, 8 * br + m0:8 * br + m0 + 4, :]
                    if br == 0:
                        tt(mrg[:, m0:m0 + 4, :], g, sums, ALU.mult).then_inc(sums_taken, 1)
                    else:
                        tt(mrt[:], g, sums, ALU.mult).then_inc(sums_taken, 1)
                        dve.drain()
                        tt(mrg[:, m0:m0 + 4, :], mrg[:, m0:m0 + 4, :], mrt[:], ALU.add)
                    dve.drain()
                each("w_br", layer, take_branch, per=8)
                dve.drain()
                halves(m_hi[:], m_lo[:], mrg[:]).then_inc(operand_ready, 1)
                add_mix = scaled_sum("w_out", False, 1.0)
                each("w_out", layer, lambda i, u: add_mix(slice(2 * u, 2 * u + 2), bank("w_out", u)), per=8)
                dve.drain()
                copy(small[:, 15:16], small[:, 14:15]).then_inc(x_ready, 1)
                norm(layer * 3 + 5, LAT, l_hi[:], l_lo[:], layer * 3 + 1, LN_EPS)
                swiglu("ff2_in", layer, gs2, gp2, fh_hi, fh_lo, T, 84)
                ff_out("ff2_out")
                norm(layer * 3 + 6, LAT, l_hi[:], l_lo[:], layer * 3 + 2, LN_EPS)
                dve.drain()
                copy(small[:, 15:16], small[:, 14:15]).then_inc(layer_used, 1)


def blocks1024(w):
    return w.reshape(8, P, -1, 2, P).transpose(2, 1, 3, 0, 4).reshape(-1, P, 16, P)


def pairs1024(a, b):
    both = np.stack([a.reshape(8, P, -1, P), b.reshape(8, P, -1, P)], 0)
    return both.transpose(3, 2, 0, 1, 4).reshape(-1, P, 16, P)


def deep_blocks(w):
    return w.reshape(-1, 8, P, 4, 2, P).transpose(3, 0, 2, 4, 1, 5).reshape(-1, P, 16, P)


def ffn_out_blocks(w):
    return w.reshape(-1, 2, P, 8, P).transpose(0, 2, 1, 3, 4).reshape(-1, P, 16, P)


def branch_blocks(w):
    return w.reshape(4, P, 2, 4, P).transpose(2, 1, 3, 0, 4).reshape(-1, P, 16, P)


def columns(v):
    return v.reshape(-1, P).T


def spread(v):
    return np.broadcast_to(v.reshape(1, -1), (P, v.size))


def constants():
    i = np.arange(P)
    ident = np.eye(P)
    ones = np.ones((P, P))
    ones64 = (i[:, None] // 64 == i[None] // 64) * 1.0

    def partner(size):
        half = size // 2
        r = np.zeros((P, P))
        for m in range(P):
            if m % size < half:
                r[m + half, m] = -1.0
            else:
                r[m - half, m] = 1.0
        return r
    swap = np.zeros((P, P))
    swap[(i + 64) % P, i] = 1.0
    t = np.arange(T)
    row, col = t // 64, t % 64
    f = 10000.0 ** -((i % 16) / 16.0)
    pos = np.where((i[:, None] % 64) < 32, row[None], col[None])
    ang = pos * f[:, None]
    q, k = t[:, None], t[None]
    bandB = np.where(k // CH <= q // CH, 0.0, -1e30)
    inside = (k // CH <= q // CH) & (k // CH >= q // CH - 2)
    bandC = np.where(inside, -np.abs(q - k), -1e30)

    def rows(m):
        return m.reshape(2, P, T).transpose(1, 0, 2).reshape(P, 2 * T)
    cst = np.concatenate([ident, ones, ones64, partner(P), partner(32), swap, np.cos(ang), np.sin(ang),
                          rows(bandB), rows(bandC)], 1).astype(np.float32)
    f = 10000.0 ** -((i % 64) / 64.0)
    ang = np.stack([row[None] * f[:, None], col[None] * f[:, None]], 1)
    rope = np.stack([np.cos(ang), np.sin(ang)], 1).astype(np.float32)
    j = np.concatenate([np.arange(T) - T, np.arange(T)]).reshape(4, P).T[:, :, None]
    ctx_key = (j < 0)
    l = j + T
    fwd = np.where(ctx_key, T + t - l, np.maximum(t - j, 0))
    bwd = np.where(ctx_key, T - t + l, np.maximum(j - t, 0))
    m_f = np.where(ctx_key, 1, t >= j)
    m_b = np.where(ctx_key, 1, t <= j)
    dist = np.stack([fwd, bwd, m_f, m_b], 1).astype(np.float32)
    a, b = np.arange(CH)[:, None], np.arange(CH)[None]
    masks = [a <= b, a > b, a < b]
    for lv in range(6):
        size = 2 << lv
        masks.append((a // size == b // size) & (a % size < size // 2) & (b % size >= size // 2))
    c64 = np.stack(masks, 1).astype(np.float32)
    return cst, rope, dist, c64


def kernel(**inp):
    import concourse.bacc as bacc
    from concourse.bass_utils import run_bass_kernel_spmd

    a = {k: np.asarray(v) for k, v in inp.items()}
    f32 = np.float32
    ada = np.concatenate([blocks1024(a["ada_w"][l]) for l in range(2)])
    parts = []
    rw = a["ret_w_in"][0]
    parts += [blocks1024(rw), deep_blocks(a["ret_w_out"][0])]
    fh = FFN_B * P

    def ffn(l):
        return [pairs1024(a["ffn_w_in"][l][:, :fh], a["ffn_w_in"][l][:, fh:]), ffn_out_blocks(a["ffn_w_out"][l])]
    parts += ffn(0)
    parts += [blocks1024(a["diff_w_in"][0]), blocks1024(a["diff_w_out"][0])]
    parts += ffn(1)
    hid = FF_B * P
    for l in range(LAYERS2):
        for k in ("1", "2"):
            if k == "2":
                w = a["w_in_2"][l]
                small = np.zeros((D, 2 * P), f32)
                small[:, 0:8] = w[:, 1536:1544]
                parts.append(blocks1024(np.concatenate([w[:, :1536], w[:, 1544:], small], 1)))
                parts.append(blocks1024(a["w_gate_2"][l]))
                parts += [branch_blocks(a[f"w_br_{x}_2"][l]) for x in "abc"]
                parts.append(blocks1024(a["w_out_2"][l]))
            w = a[f"w_ff{k}_in_2"][l]
            parts.append(pairs1024(w[:, :hid], w[:, hid:]))
            parts.append(deep_blocks(a[f"w_ff{k}_out_2"][l]))
    parts.append(np.zeros((SPLIT, P, 16, P), f32))
    ws = np.concatenate(parts)
    assert ws.shape == (TILES, P, 16, P), ws.shape

    def feature_major(x):
        return x[0].T.reshape(DC, P, T).transpose(1, 0, 2)
    xt = np.concatenate([feature_major(a["ctx"]), feature_major(a["x"])], 2)
    cond = np.stack([columns(a["c_ctx"]), columns(a["c"][0])], 2).reshape(P, 16)
    col1 = np.concatenate([columns(a["ada_b"]), columns(a["ret_norm_g"]),
                           np.tile(a["diff_q_norm_g"].reshape(64, 1), (2, 1)),
                           np.tile(a["diff_k_norm_g"].reshape(64, 1), (2, 1)),
                           columns(a["diff_subln_g"]), cond], 1)
    row1 = np.concatenate([spread(a["ret_decay_logit"]), spread(a["diff_lambda"])], 1)
    col2, row2, relb = [], [], []
    t = np.arange(T)
    rel = np.clip(t[:, None] - t[None], -63, 128) + 63
    for l in range(LAYERS2):
        bi = a["b_in_2"][l]
        fm = np.concatenate([bi[:1536], bi[1544:3080], bi[3592:4232]])
        col2.append(np.concatenate([columns(a[n][l]) for n in ("ln1_g_2", "ln1_b_2", "ln2_g_2", "ln2_b_2",
                                                               "ln3_g_2", "ln3_b_2")]
                                   + [columns(fm), columns(a["b_gate_2"][l]), columns(a["conv_w_2"][l]),
                                      columns(a["gdn_norm_g_2"][l])], 1))
        row2.append(np.concatenate([spread(v) for v in (bi[3080:3592], bi[4232:4360], bi[1536:1544],
                                                        a["a_log_2"][l], a["dt_bias_2"][l], a["sinks_2"][l])], 1))
        relb.append(a["rel_bias_2"][l][:, rel].reshape(4, 2, P, T).transpose(2, 0, 1, 3))
    cst, rope, dist, c64 = constants()
    arrays = dict(ada=ada, ws=ws, xt=xt, col1=col1, row1=row1, col2=np.stack(col2), row2=np.stack(row2),
                  relb=np.stack(relb), cst=cst, ret_cst=rope, ret_dist=dist, c64=c64)
    arrays = {f"in_{k}": np.ascontiguousarray(v) for k, v in arrays.items()}
    nc = bacc.Bacc("TRN2", target_bir_lowering=False, num_devices=1)
    args = [nc.dram_tensor(k, v.shape, mybir.dt.from_np(v.dtype), kind="ExternalInput").ap()
            for k, v in arrays.items()]
    args.append(nc.dram_tensor("out_0", (P, DC, T), F32, kind="ExternalOutput").ap())
    build(nc, *args)
    r = run_bass_kernel_spmd(nc, [arrays], core_ids=[0])
    got = r.results[0]["out_0"]
    return got.transpose(1, 0, 2).reshape(D, T).T[None]
```

```python
import math
from contextlib import ExitStack

import numpy as np

import concourse.bass as bass
from concourse import mybir

F32 = mybir.dt.float32
F32R = mybir.dt.float32r
ALU = mybir.AluOpType
ACT = mybir.ActivationFunctionType
AX = mybir.AxisListType.X

P = 128
D = 1024
DC = D // P
T = 256
TT = 2 * T
CTX, LAT = slice(0, T), slice(T, TT)
EPS = 1e-6
LN_EPS = 1e-5
RET_H, RET_VB = 4, 4
FFN_B = 22
FF_B = 32
LAMBDA_INIT = 0.8 - 0.6 * math.exp(-0.3)
ALPHA = 4.0 ** 0.25
LAYERS2 = 2
CH = 64
RAW, SPLIT = 4, 2

ADA_TILES = 48
FIRST = [("ada", ADA_TILES, ADA_TILES), ("ret_qkv", 16, 16), ("ret_g", 8, 8), ("ret_out", 8, 4), ("ffn_in0", 22, 22), ("ffn_out0", 11, 2),
         ("diff_in", 12, 12), ("diff_out", 4, 4), ("ffn_in1", 22, 22), ("ffn_out1", 11, 2)]
LAYER = [("ff1_in", 32, 32), ("ff1_out", 16, 4), ("w_in", 18, 18), ("w_gate", 12, 12), ("w_br", 6, 6),
         ("w_out", 4, 4), ("ff2_in", 32, 32), ("ff2_out", 16, 4)]
N1 = sum(t for _, t, _ in FIRST)
G1 = sum(g for _, _, g in FIRST)
NL = sum(t for _, t, _ in LAYER)
GL = sum(g for _, _, g in LAYER)
NORMS = 4 + 3 * LAYERS2
TILES = N1 + LAYERS2 * NL + SPLIT
assert NL % 4 == 0 and GL % 2 == 0 and G1 % 2 == 0 and TILES % 4 == 0


def starts(phases, n, g):
    out = {}
    for name, tiles, groups in phases:
        out[name] = (n, g, tiles)
        n, g = n + tiles, g + groups
    return out


PH = {**starts(FIRST, 0, 0), **starts(LAYER, N1, G1)}

C_ADAB, C_RETG, C_DQG, C_DKG, C_SUB, C_COND = 0, 96, 112, 113, 114, 115
NCOL1 = 131
C_LN = [(0, 8), (16, 24), (32, 40)]
C_BIN, C_BG, C_CONV, C_GDN = 48, 77, 101, 149
NCOL2 = 150
R_VB, R_VC, R_BETA, R_A, R_ALOG, R_DT, R_SINK = 0, 512, 640, 644, 648, 652, 656
NROW2 = 664


def build(nc, ws, xt, col1, row1, col2, row2, relb, cst, ret_cst, ret_dist, c64, out):
    KB = 1024
    base = -(-nc.sbuf_base // 64) * 64

    def at(name, shape, kb, dtype=F32):
        return nc.alloc_sbuf_tensor_at(name, shape, dtype, offset=base + int(kb * KB) // 32 * 32)

    raw = at("raw", [P, RAW, 16, P], 0)
    w_lo = at("w_lo", [P, RAW, 16, P], 0, F32R)
    w_hi = at("w_hi", [P, SPLIT, 16, P], 32, F32R)
    X = at("X", [P, DC, TT], 48)
    h_hi = at("h_hi", [P, DC, TT], 64, F32R)
    h_lo = at("h_lo", [P, DC, TT], 80, F32R)
    l_hi = at("l_hi", [P, DC, T], 64, F32R)
    l_lo = at("l_lo", [P, DC, T], 72, F32R)
    relB = at("relB", [P, 4, 2, T], 80)
    rows2 = at("rows2", [P, NROW2], 88)
    bandB = at("bandB", [P, 2, T], 91)
    bandC = at("bandC", [P, 2, T], 93)
    cs = at("cs", [P, 6, P], 96)
    ident, ones, ones64, rot_ret, rot_diff, swap64 = (cs[:, i, :] for i in range(6))
    rope_d = at("rope_d", [P, 2, T], 99)
    mod = at("mod", [P, 2, 48, 2], 101)
    cols1 = at("cols1", [P, NCOL1], 101.8)
    cols2 = at("cols2", [P, NCOL2], 102.4)
    silu_c = at("silu_c", [P, DC, 2], 103.1)
    parts_sum = at("parts_sum", [4, 2], 103.16)
    lgam = at("lgam", [P, 8], 103.2)
    lam = at("lam", [P, 4], 103.3)
    small = at("small", [P, 16], 103.4)
    softx = at("softx", [P, 2, 16], 103.5)
    rr = at("rr", [P, TT], 104)
    ada_row = at("ada_row", [4, 2, T], 104)
    AR = 106
    cond4 = at("cond4", [P, DC, 4], AR, F32R)
    SQ = at("SQ", [P, DC, TT], AR)
    QK = at("QK", [P, 16, TT], AR)
    V = at("V", [P, RET_H, 4, TT], AR + 32)
    DM = at("DM", [P, RET_H, 4, T], AR + 64)
    rope_r = at("rope_r", [P, 2, 2, T], AR + 80)
    dist = at("dist", [P, 4, 4, T], AR + 32)
    expd = at("expd", [P, 2, 4, T], AR + 48)
    rtmp = at("rtmp", [P, 2, 2, T], AR + 84)
    att = at("att", [P, 6, T], AR + 84)
    sqh = at("sqh", [P, 4, TT], AR + 90)
    y_hi = at("y_hi", [P, 16, TT], AR + 32, F32R)
    y_lo = at("y_lo", [P, 16, TT], AR, F32R)
    gs = at("gs", [P, 2, TT], AR + 84)
    gp = at("gp", [P, 2, TT], AR + 90)
    hid_hi = at("hid_hi", [P, FFN_B, TT], AR, F32R)
    hid_lo = at("hid_lo", [P, FFN_B, TT], AR + 44, F32R)
    fs = at("fs", [P, 2, TT], AR + 88)
    fp = at("fp", [P, 2, TT], AR + 92)
    QK1 = at("QK1", [P, 12, TT], AR)
    V1 = at("V1", [P, 4, D], AR + 24)
    R1 = at("R1", [P, 12, TT], AR + 40)
    SQ1 = at("SQ1", [P, 12, TT], AR + 64)
    lamv = at("lamv", [P, 4, 64], AR + 100)
    E1 = at("E1", [P, 2, 2, TT], AR + 40)
    P1 = at("P1", [P, 2, TT], AR + 48)
    PT1 = at("PT1", [P, 2, 4, T], AR + 52)
    O1 = at("O1", [P, 8, T], AR + 64)
    SO1 = at("SO1", [P, 8, T], AR + 72)
    RO1 = at("RO1", [P, 8, T], AR + 80)
    d_hi = at("d_hi", [P, DC, T], AR, F32R)
    d_lo = at("d_lo", [P, DC, T], AR + 8, F32R)
    fh_hi = at("fh_hi", [P, FF_B, T], AR, F32R)
    fh_lo = at("fh_lo", [P, FF_B, T], AR + 32, F32R)
    gs2 = at("gs2", [P, 2, T], AR + 88)
    gp2 = at("gp2", [P, 2, T], AR + 92)
    gate = at("gate", [P, 24, T], AR)
    o_hi = at("o_hi", [P, 12, T], AR + 24, F32R)
    o_lo = at("o_lo", [P, 12, T], AR + 36, F32R)
    CV = at("CV", [P, 12, T], AR + 48)
    za = at("za", [P, 4, T], AR + 60)
    QKVp = at("QKVp", [P, 12, T + 3], AR + 64)
    qkb = at("qkb", [P, 8, T], AR + 76.5)
    vb = at("vb", [P, 2, 512], AR + 84.5)
    qc = at("qc", [P, 4, T], AR + 88.5)
    kc = at("kc", [P, 2, T], AR + 92.5)
    vc = at("vc", [P, 2, 2, P], AR + 94.5)
    ba = at("ba", [64, 4, 8], AR + 96.5)
    beta = at("beta", [64, 4, 4], AR + 96.75)
    gdec = at("gdec", [64, 4, 4], AR + 97)
    gcum = at("gcum", [64, 4, 4], AR + 97.25)
    gsuf = at("gsuf", [64, 4, 4], AR + 97.5)
    gexp = at("gexp", [64, 4, 4], AR + 97.75)
    bt = at("bt", [64, 8, 16], AR + 98)
    m64 = at("m64", [64, 9, CH], AR + 99.5)
    NSQ = at("NSQ", [P, 8, T], AR + 64)
    NR = at("NR", [P, 8, T], AR + 64)
    TT2 = at("TT2", [P, 2, 2, T], AR + 64)
    PT2 = at("PT2", [P, 2, 2, T], AR + 68)
    kT = at("kT", [64, 8, P], AR + 64)
    vT = at("vT", [64, 8, P], AR + 68)
    kbg = at("kbg", [64, 8, P], AR + 72)
    kdec = at("kdec", [64, 8, P], AR + 76)
    DT = at("DT", [64, 8, CH], AR + 80)
    LT = at("LT", [64, 8, CH], AR + 82)
    qkT = at("qkT", [64, 8, CH], AR + 84)
    TU = at("TU", [64, 2, 2, 4, CH], AR + 86)
    Pm = at("Pm", [64, 8, CH], AR + 90)
    Mm = at("Mm", [64, 8, CH], AR + 92)
    gcb = at("gcb", [P, 8, CH], AR + 94)
    uu = at("uu", [64, 8, P], AR + 64)
    wT = at("wT", [P, 8, CH], AR + 90)
    qdec = at("qdec", [P, 8, CH], AR + 82)
    vnew = at("vnew", [64, 2, P], AR + 92)
    Sst = at("Sst", [P, 2, P], AR + 86)
    oraw = at("oraw", [P, 4, T], AR + 36)
    oA = at("oA", [P, 4, T], AR + 72)
    osq = at("osq", [P, 4, T], AR + 76)
    ostd = at("ostd", [P, 4, T], AR + 80)
    mrg = at("mrg", [P, DC, T], AR + 64)
    mrt = at("mrt", [P, 4, T], AR + 72)
    m_hi = at("m_hi", [P, DC, T], AR + 76, F32R)
    m_lo = at("m_lo", [P, DC, T], AR + 84, F32R)

    with ExitStack() as ctx:
        ps = ctx.enter_context(nc.psum_tensor("ps", [P, 8, 512], F32))

        def sem(name):
            return ctx.enter_context(nc.semaphore(name))

        raw_full = [sem(f"raw_full{s}") for s in range(RAW)]
        (hi_done, lo_done, tile_used, sums_taken, mod_ready, tables_in, params_in, layer_used,
         x_in, silu_c_ready, operand_ready, silu_ready, gate_ready) = map(sem, (
            "hi_done", "lo_done", "tile_used", "sums_taken", "mod_ready", "tables_in", "params_in",
            "layer_used", "x_in", "silu_c_ready", "operand_ready", "silu_ready", "gate_ready"))
        (mean_ready, sq_ready, square_sum, var_ready, std_ready, scaled, normed, lgam_exp, lgam_one,
         lgam_ln, decays_exp, decays_ready, lgam_ready) = map(sem, (
            "mean_ready", "sq_ready", "square_sum", "var_ready", "std_ready", "scaled", "normed",
            "lgam_exp", "lgam_one", "lgam_ln", "decays_exp", "decays_ready", "lgam_ready"))
        (rot_in, rot_ready, rot_taken, att_ready, att_decayed, ho_ready, ho_taken, ho_mean, ho_centred, ho_sq,
         ho_sqsum, ho_var, ho_std, heads_done) = map(sem, (
            "rot_in", "rot_ready", "rot_taken", "att_ready", "att_decayed", "ho_ready", "ho_taken", "ho_mean",
            "ho_centred", "ho_sq", "ho_sqsum", "ho_var", "ho_std", "heads_done"))
        (lam_dot, lam_exp, qk_ready, qk_sq, qk_sums, qk_sums_taken, qk_std, drot_in, drot_ready, drot_taken,
         s_ready, s_max, s_exp, s_prob, s_turned, s_copied, so_ready, so_taken, so_sq, so_sum, so_var,
         so_std) = map(sem, (
            "lam_dot", "lam_exp", "qk_ready", "qk_sq", "qk_sums", "qk_sums_taken", "qk_std", "drot_in",
            "drot_ready", "drot_taken", "s_ready", "s_max", "s_exp", "s_prob", "s_turned", "s_copied", "so_ready",
            "so_taken", "so_sq", "so_sum", "so_var", "so_std"))
        (m_in, kswap_ready, kswap_taken, conv_done, conv_silu, n_sq, n_sum, n_var, n_std, n_done, ba_ready,
         a_in, a_out, b_s, b_max, b_exp, b_prob, b_turned, b_copied, b_o, b_taken, bias_ready) = map(sem, (
            "m_in", "kswap_ready", "kswap_taken", "conv_done", "conv_silu", "n_sq", "n_sum", "n_var", "n_std",
            "n_done", "ba_ready", "a_in", "a_out", "b_s", "b_max", "b_exp", "b_prob", "b_turned", "b_copied",
            "b_o", "b_taken", "bias_ready"))
        (g_mid, g_lin, g_exp, g_ln, g_rate, gd_ready, gd_sums, gd_taken, gd_exp, gd_turn_k, gd_turned,
         gd_diff, gd_decay, gd_kk, gd_sys, inv_ready, inv_p, inv_pc, inv_done, inv_next, rhs_ready, uw_ready,
         uw_taken, sc_w, sc_v, sc_s, sc_next, go_sq, go_sum, go_var, go_std, out_done) = map(sem, (
            "g_mid", "g_lin", "g_exp", "g_ln", "g_rate", "gd_ready", "gd_sums", "gd_taken", "gd_exp",
            "gd_turn_k", "gd_turned", "gd_diff", "gd_decay", "gd_kk", "gd_sys", "inv_ready", "inv_p", "inv_pc",
            "inv_done", "inv_next", "rhs_ready", "uw_ready", "uw_taken", "sc_w", "sc_v", "sc_s", "sc_next",
            "go_sq", "go_sum", "go_var", "go_std", "out_done"))

        waits_passed, ada_turned, cond_ready, cols_in, tables_ready, consts_in = map(sem, ("waits_passed", "ada_turned", "cond_ready", "cols_in", "tables_ready", "consts_in"))
        go_copied, block_ready = map(sem, ("go_copied", "block_ready"))
        (logit_in, dist_in, lam_in, band_in, ada_ready, mod_scaled, lgam_abs, qk_in, za_ready, centred) = map(sem, (
            "logit_in", "dist_in", "lam_in", "band_in", "ada_ready", "mod_scaled", "lgam_abs", "qk_in", "za_ready",
            "centred"))

        block = ctx.enter_context(nc.Block())

        def tiles(phase, layer, eng, body, first=0, count=None, per=4):
            n0, _, total = PH[phase]
            count = total - first if count is None else count
            turns = count // per
            done = 0
            if turns > 1:
                with eng.Fori(0, turns) as i:
                    for u in range(per):
                        body(i, u, n0 + first + u, i * (per // 4) + layer * (NL // 4))
                done = turns * per
            for u in range(done, count):
                body(0, u, n0 + first + u, layer * (NL // 4))

        def group(phase, layer, g):
            return layer * GL + g + PH[phase][1]

        def after_norm_input(q, mean=None):
            if mean is None:
                phase, n = {1: ("ret_out", 4), 2: ("ffn_out0", 2), 3: ("diff_out", 4)}[q]
                return group(phase, 0, n) + 2
            layer, j = mean
            return group(("ff1_out", "w_out", "ff2_out")[j], layer, 4) + 2

        def raw_slot(s):
            return s % RAW

        def pair(phase, g):
            return 2 * ((PH[phase][1] + g) % 2)

        def bank(phase, g):
            g += PH[phase][1]
            return 2 * (g % 2) + g // 2 % 2

        @block.sync
        def _(sp):
            sp.dma_start(cols1[:], col1).then_inc(cols_in, 16)
            for n in range(RAW):
                sp.dma_start(raw[:, n], ws[n]).then_inc(raw_full[n], 16)
            sp.dma_start(X[:], xt).then_inc(x_in, 16)
            with sp.Fori(0, TILES // 4 - 1) as i:
                for u in range(4):
                    sp.wait_ge(tile_used, i * 4 + u + 1 + SPLIT)
                    sp.dma_start(raw[:, u], ws[bass.ds(i * 4 + u + 4, 1)].rearrange("a p b c -> (a p) b c")
                                 ).then_inc(raw_full[u], 16)
            sp.wait_ge(normed, DC * NORMS)
            sp.dma_start(out, X[:, :, LAT]).then_inc(out_done, 16)
            sp.wait_ge(out_done, 16)

        @block.gpsimd
        def _(pool):
            pool.dma_start(cs[:], cst[:, 0:768].rearrange("p (a b) -> p a b", b=P)).then_inc(consts_in, 16)
            pool.dma_start(lgam[:], row1[:, 0:8]).then_inc(logit_in, 16)
            pool.dma_start(dist[:], ret_dist).then_inc(dist_in, 16)
            pool.dma_start(rope_r[:], ret_cst).then_inc(tables_in, 16)
            pool.dma_start(rope_d[:], cst[:, 768:1280].rearrange("p (a b) -> p a b", b=T)).then_inc(tables_in, 16)
            for h in range(RET_H):
                pool.wait_ge(decays_exp, 2 * h + 2)
                pool.wait_ge(dist_in, 16)
                nc.gpsimd.tensor_tensor(expd[:], expd[:], dist[:, 2:4], ALU.mult)
                pool.drain()
                nc.gpsimd.tensor_tensor(DM[:, h], expd[:, 0], expd[:, 1], ALU.add).then_inc(decays_ready, 1)
            pool.wait_ge(sums_taken, group("ffn_out0", 0, 2) + 2)
            pool.dma_start(lamv[:], row1[:, 8:264].rearrange("p (a b) -> p a b", b=64)).then_inc(lam_in, 16)
            pool.wait_ge(sums_taken, group("ffn_out1", 0, 2) + 2)
            pool.dma_start(bandB[:], cst[:, 1280:1792].rearrange("p (a b) -> p a b", b=T)).then_inc(band_in, 16)
            pool.dma_start(bandC[:], cst[:, 1792:2304].rearrange("p (a b) -> p a b", b=T)).then_inc(band_in, 16)
            pool.dma_start(m64[:], c64).then_inc(band_in, 16)
            pool.wait_ge(band_in, 48)
            with pool.Fori(0, LAYERS2) as layer:
                pool.wait_ge(layer_used, layer + 1)
                pool.dma_start(cols2[:], col2[bass.ds(layer, 1)].rearrange("a p c -> (a p) c")
                               ).then_inc(params_in, 16)
                pool.dma_start(rows2[:], row2[bass.ds(layer, 1)].rearrange("a p c -> (a p) c")
                               ).then_inc(params_in, 16)
                pool.dma_start(relB[:], relb[bass.ds(layer, 1)].rearrange("a p h b k -> (a p) h b k")
                               ).then_inc(params_in, 16)
                pool.wait_ge(params_in, layer * 48 + 48)
                for h in range(4):
                    ins = nc.gpsimd.tensor_tensor(relB[:, h], relB[:, h], bandB[:], ALU.add)
                ins.then_inc(bias_ready, 1)

        @block.tensor
        def _(pe):
            mm = nc.tensor.matmul

            def pass_wait():
                pe.sem_inc(waits_passed)

            def product(out_, blk, s, rhs_hi, rhs_lo, start, stop):
                mm(out_, w_hi[:, s % SPLIT, blk], rhs_hi, start=start, stop=False)
                mm(out_, w_hi[:, s % SPLIT, blk], rhs_lo, start=False, stop=False)
                return mm(out_, w_lo[:, raw_slot(s), blk], rhs_hi, start=False, stop=stop)

            def product_rows(out_, blk, s, x_hi, x_lo, start, stop):
                mm(out_, x_hi, w_hi[:, s % SPLIT, blk], start=start, stop=False)
                mm(out_, x_hi, w_lo[:, raw_slot(s), blk], start=False, stop=False)
                return mm(out_, x_lo, w_hi[:, s % SPLIT, blk], start=False, stop=stop)

            def wait_tile(s, turn):
                pe.wait_ge(lo_done, turn * 4 + s + 1)

            def wide(phase, layer, rhs_hi, rhs_lo, width, first=0, count=None, ring=False, blocks=None):
                if width == T and not ring:
                    pe.wait_ge(sums_taken, group(phase, layer, first + 2))
                    pass_wait()

                def body(i, u, s, turn):
                    wait_tile(s, turn)
                    ahead = 1 if width == TT else -1
                    pe.wait_ge(sums_taken, group(phase, layer, i * 4 + first + u + ahead))
                    b = pair(phase, first + u) if width == TT else bank(phase, first + u)
                    for mi in range(2):
                        o = ps[:, b + mi, 0:TT] if width == TT else ps[:, b, mi * T:(mi + 1) * T]
                        for c in range(DC):
                            if blocks is not None and first + u == 0 and mi == 0:
                                pe.wait_ge(block_ready, blocks + c + 1)
                                pass_wait()
                            ins = product(o, mi * DC + c, s, rhs_hi[:, c, :], rhs_lo[:, c, :], c == 0, c == DC - 1)
                    ins.then_inc(tile_used, 1)
                tiles(phase, layer, pe, body, first, count)

            def values(phase, layer, x_hi, x_lo, nblk, first, count):
                def body(i, u, s, turn):
                    wait_tile(s, turn)
                    pe.wait_ge(sums_taken, group(phase, layer, i * 4 + first + u + (1 if nblk == 4 else -1)))
                    b = pair(phase, first + u) if nblk == 4 else bank(phase, first + u)
                    for kb in range(nblk):
                        o = ps[:, b + kb // 2, (kb % 2) * T:(kb % 2 + 1) * T].rearrange("p (a b) -> p a b", b=P)
                        for c in range(DC):
                            tok = slice(kb * P, kb * P + P)
                            ins = product_rows(o, slice(c, 16, DC), s, x_hi[:, c, tok], x_lo[:, c, tok],
                                               c == 0, c == DC - 1)
                    ins.then_inc(tile_used, 1)
                tiles(phase, layer, pe, body, first, count)

            def deep(phase, layer, rhs_hi, rhs_lo, width, parts):
                def body(i, u, s, turn):
                    wait_tile(s, turn)
                    q = u % parts
                    if q == 0:
                        pe.wait_ge(sums_taken, group(phase, layer, i * 2 + u // parts + 1))
                    b = pair(phase, u // parts)
                    for mi in range(2):
                        for c in range(DC):
                            ins = product(ps[:, b + mi, 0:width], mi * DC + c, s, rhs_hi[:, q * DC + c, :],
                                          rhs_lo[:, q * DC + c, :], q == 0 and c == 0, q == parts - 1 and c == DC - 1)
                    ins.then_inc(tile_used, 1)
                tiles(phase, layer, pe, body, per=2 * parts)

            def ffn_out(phase, cols):
                width = cols.stop - cols.start
                pe.wait_ge(sums_taken, group(phase, 0, 2))

                def body(first, last):
                    def run(i, u, s, turn):
                        wait_tile(s, turn)
                        for ci in range(2):
                            blk = bass.ds(i * 8 + 2 * (u + first) + ci, 1)
                            for m in range(DC):
                                ins = product(ps[:, m, 0:width], ci * DC + m, s,
                                              hid_hi[:, blk, cols], hid_lo[:, blk, cols],
                                              first == 0 and ci == 0, last and ci == 1)
                        ins.then_inc(tile_used, 1)
                    return run
                tiles(phase, 0, pe, body(0, False), 0, 1)
                tiles(phase, 0, pe, body(1, False), 1, 8)
                tiles(phase, 0, pe, body(9, False), 9, 1)
                tiles(phase, 0, pe, body(10, True), 10, 1)

            def norm(q, cols, mean=None):
                width = cols.stop - cols.start
                if mean is not None:
                    pe.wait_ge(sums_taken, after_norm_input(q, mean))
                    for c in range(DC):
                        ins = mm(ps[:, 4, 0:width], ones, X[:, c, cols], start=c == 0, stop=c == DC - 1)
                    ins.then_inc(mean_ready, 1)
                for c in range(DC):
                    pe.wait_ge(sq_ready, q * DC + c + 1)
                    ins = mm(ps[:, 5, 0:width], ones, SQ[:, c, 0:width], start=c == 0, stop=c == DC - 1)
                ins.then_inc(square_sum, 1)

            pe.sem_inc(tile_used, SPLIT)
            def ada_rows(i, u, s, turn):
                wait_tile(s, turn)
                pe.wait_ge(sums_taken, i * 4 + s + 1)
                o = ps[0:4, 4 + u % 2, 0:T].rearrange("p (a b) -> p a b", b=P)
                for c in range(DC):
                    mm(o, cond4[:, c, :], w_hi[:, s % SPLIT, c:16:DC, :], start=c == 0, stop=False)
                    ins = mm(o, cond4[:, c, :], w_lo[:, raw_slot(s), c:16:DC, :], start=False, stop=c == DC - 1)
                ins.then_inc(tile_used, 1)

            def ada_turn(t, u):
                pe.wait_ge(sums_taken, t + 3)
                for mi in range(2):
                    ins = mm(ps[:, 6 + u % 2, 2 * mi:2 * mi + 2], ada_row[:, u % 2, mi * P:mi * P + P],
                             parts_sum[:], start=True, stop=True)
                ins.then_inc(ada_turned, 1)

            pe.wait_ge(cond_ready, 1)

            def first_tiles(i, u, s, turn):
                ada_rows(i, u, s, turn)
                if u == 1:
                    pe.wait_ge(tables_ready, 1)
                if u:
                    ada_turn(u - 1, u - 1)

            def later_tiles(i, u, s, turn):
                ada_rows(i, u, s, turn)
                ada_turn(i * 4 + s - 1, (u - 1) % 4)
            tiles("ada", 0, pe, first_tiles, 0, 4)
            tiles("ada", 0, pe, later_tiles, 4)
            ada_turn(ADA_TILES - 1, 3)
            pe.wait_ge(consts_in, 16)
            pe.wait_ge(mod_ready, ADA_TILES)

            norm(0, slice(0, TT))
            wide("ret_qkv", 0, h_hi, h_lo, TT, 0, 4, blocks=0)
            pe.wait_ge(operand_ready, 1)
            wide("ret_qkv", 0, h_hi, h_lo, TT, 4, 4)
            values("ret_qkv", 0, h_hi, h_lo, 4, 8, 8)
            pe.wait_ge(sums_taken, group("ret_qkv", 0, 16) + 2)
            for r in range(8):
                if r >= 4:
                    pe.wait_ge(rot_taken, r - 3)
                mm(ps[:, 4 + r % 4, :].rearrange("p (a b) -> p a b", b=T), rot_ret, QK[:, 2 * r:2 * r + 2, LAT],
                   start=True, stop=True).then_inc(rot_ready, 1)
            pe.wait_ge(rot_taken, 8)
            for h in range(RET_H):
                if h:
                    pe.wait_ge(ho_var, h)
                for kb in range(4):
                    for c in range(2):
                        mm(ps[:, 4 + kb // 2, (kb % 2) * T:(kb % 2 + 1) * T], QK[:, 8 + 2 * h + c, kb * P:kb * P + P],
                           QK[:, 2 * h + c, LAT], start=c == 0, stop=c == 1)
                for kb in range(2):
                    for c in range(2):
                        ins = mm(ps[:, 6, kb * T:kb * T + T], QK[:, 8 + 2 * h + c, kb * P:kb * P + P],
                                 QK[:, 2 * h + c, CTX], start=c == 0, stop=c == 1)
                ins.then_inc(att_ready, 1)
                pe.wait_ge(att_decayed, h + 1)
                for b in range(4):
                    for kb in range(2):
                        mm(ps[:, b, CTX], V[:, h, kb, b * P:b * P + P], att[:, 4 + kb, :], start=kb == 0, stop=kb == 1)
                    for kb in range(4):
                        ins = mm(ps[:, b, LAT], V[:, h, kb, b * P:b * P + P], att[:, kb, :],
                                 start=kb == 0, stop=kb == 3)
                ins.then_inc(ho_ready, 1)
                pe.wait_ge(ho_taken, h + 1)
                for b in range(4):
                    ins = mm(ps[:, 7, :], ones, V[:, h, b, :], start=b == 0, stop=b == 3)
                ins.then_inc(ho_mean, 1)
                pe.wait_ge(ho_sq, h + 1)
                for b in range(4):
                    ins = mm(ps[:, 4, :], ones, sqh[:, b, :], start=b == 0, stop=b == 3)
                ins.then_inc(ho_sqsum, 1)
            wide("ret_g", 0, h_hi, h_lo, TT)
            pe.wait_ge(operand_ready, 2)
            deep("ret_out", 0, y_hi, y_lo, TT, 2)
            norm(1, slice(0, TT))
            wide("ffn_in0", 0, h_hi, h_lo, TT, 0, 4, blocks=DC)
            pe.wait_ge(operand_ready, 3)
            wide("ffn_in0", 0, h_hi, h_lo, TT, 4)
            pe.wait_ge(operand_ready, 4)
            ffn_out("ffn_out0", slice(0, TT))

            norm(2, slice(0, TT))
            wide("diff_in", 0, h_hi[:, :, LAT], h_lo[:, :, LAT], T, 0, 4, blocks=2 * DC)
            pe.wait_ge(operand_ready, 5)
            wide("diff_in", 0, h_hi, h_lo, TT, 4, 4)
            values("diff_in", 0, h_hi, h_lo, 4, 8, 4)
            for r in range(12):
                pe.wait_ge(qk_sq, r // 4 + 1)
                if r >= 4:
                    pe.wait_ge(qk_sums_taken, r - 3)
                mm(ps[:, 4 + r % 4, :], ones64, SQ1[:, r, :], start=True, stop=True).then_inc(qk_sums, 1)
            for r in range(8):
                pe.wait_ge(qk_ready, 1 if r < 4 else 2 if r < 6 else 3)
                pe.wait_ge(qk_sums_taken, 12) if r < 4 else pe.wait_ge(drot_taken, r - 3)
                src = (QK1[:, r, :].rearrange("p (a b) -> p a b", b=T) if r < 4
                       else QK1[:, 4 + 2 * (r - 4):6 + 2 * (r - 4), LAT])
                mm(ps[:, 4 + r % 4, :].rearrange("p (a b) -> p a b", b=T), rot_diff, src,
                   start=True, stop=True).then_inc(drot_ready, 1)
            pe.wait_ge(drot_taken, 8)
            pe.wait_ge(sums_taken, group("diff_in", 0, 12) + 2)

            def diff_scores(r):
                h, qb = r // 2, r % 2
                if r >= 2:
                    pe.wait_ge(s_exp, r - 1)
                for m in range(2):
                    rows = slice(64 * m, 64 * m + 64)
                    off = (h % 2) * T + qb * P
                    ins = mm(ps[:, 4 + 2 * (r % 2) + m, :], QK1[rows, h // 2, off:off + P], QK1[rows, 4 + h, :],
                             start=True, stop=True)
                ins.then_inc(s_ready, 1)

            def diff_turn(r):
                pe.wait_ge(s_prob, r + 1)
                if r >= 2:
                    pe.wait_ge(s_copied, r - 1)
                for kb in range(4):
                    ins = nc.tensor.transpose(ps[:, r % 2, kb * P:kb * P + P], P1[:, r % 2, kb * P:kb * P + P], ident)
                ins.then_inc(s_turned, 1)

            def diff_values(h):
                pe.wait_ge(s_copied, 2 * h + 2)
                if h >= 2:
                    pe.wait_ge(so_taken, h - 1)
                for kb in range(4):
                    ins = mm(ps[:, 2 + h % 2, 0:T], V1[:, kb, h * P:h * P + P], PT1[:, h % 2, kb, :],
                             start=kb == 0, stop=kb == 3)
                ins.then_inc(so_ready, 1)
            diff_scores(0)
            for r in range(18):
                if r < 15:
                    diff_scores(r + 1)
                if 1 <= r < 17:
                    diff_turn(r - 1)
                if r >= 3 and r % 2 == 1:
                    diff_values(r // 2 - 1)
            pe.wait_ge(so_sq, 1)
            for r in range(4):
                ins = mm(ps[:, 4 + r, :], ones, SO1[:, 2 * r:2 * r + 2, :], start=True, stop=True)
            ins.then_inc(so_sum, 1)
            pe.wait_ge(operand_ready, 6)
            wide("diff_out", 0, d_hi, d_lo, T)
            norm(3, LAT)
            wide("ffn_in1", 0, h_hi[:, :, LAT], h_lo[:, :, LAT], T, 0, 4, blocks=3 * DC)
            pe.wait_ge(operand_ready, 7)
            wide("ffn_in1", 0, h_hi[:, :, LAT], h_lo[:, :, LAT], T, 4, ring=True)
            pe.wait_ge(operand_ready, 8)
            ffn_out("ffn_out1", slice(0, T))

            with pe.Fori(0, LAYERS2) as layer:
                def have(k):
                    pe.wait_ge(operand_ready, layer * 7 + 9 + k)
                    pass_wait()
                wide("ff1_in", layer, l_hi, l_lo, T, 0, 4, blocks=layer * 3 * DC + 4 * DC)
                have(0)
                wide("ff1_in", layer, l_hi, l_lo, T, 4, ring=True)
                have(1)
                deep("ff1_out", layer, fh_hi, fh_lo, T, 4)
                norm(layer * 3 + 4, LAT, (layer, 0))
                wide("w_in", layer, l_hi, l_lo, T, 0, 4, blocks=layer * 3 * DC + 5 * DC)
                have(2)
                wide("w_in", layer, l_hi, l_lo, T, 4, 8, ring=True)
                values("w_in", layer, l_hi, l_lo, 2, 12, 2)
                wide("w_in", layer, l_hi, l_lo, T, 14, 2, ring=True)

                def key_value(i, u, s, turn):
                    wait_tile(s, turn)
                    pe.wait_ge(sums_taken, group("w_in", layer, 15))
                    b = bank("w_in", 16)
                    for c in range(DC):
                        product(ps[:, b, 0:T], c, s, l_hi[:, c, :], l_lo[:, c, :], c == 0, c == DC - 1)
                    for kb in range(2):
                        for c in range(DC):
                            tok = slice(kb * P, kb * P + P)
                            ins = product_rows(ps[:, b, T + kb * P:T + kb * P + P], DC + c, s, l_hi[:, c, tok],
                                               l_lo[:, c, tok], c == 0, c == DC - 1)
                    ins.then_inc(tile_used, 1)
                tiles("w_in", layer, pe, key_value, 16, 1)

                def rates(i, u, s, turn):
                    wait_tile(s, turn)
                    pe.wait_ge(sums_taken, group("w_in", layer, 16))
                    b = bank("w_in", 17)
                    for n in range(4):
                        tok = slice(n * CH, n * CH + CH)
                        o = ps[0:64, b, n * 8:n * 8 + 8]
                        for c in range(DC):
                            mm(o, l_hi[:, c, tok], w_hi[:, s % SPLIT, c, 0:8], start=c == 0, stop=False)
                            mm(o, l_hi[:, c, tok], w_lo[:, raw_slot(s), c, 0:8], start=False, stop=False)
                            ins = mm(o, l_lo[:, c, tok], w_hi[:, s % SPLIT, c, 0:8], start=False, stop=c == DC - 1)
                    ins.then_inc(tile_used, 1)
                tiles("w_in", layer, pe, rates, 17, 1)
                wide("w_gate", layer, l_hi, l_lo, T, 0, 8, ring=True)
                pe.wait_ge(m_in, layer + 1)
                pass_wait()
                mm(ps[:, 4, 0:T], swap64, kc[:, 0, :], start=True, stop=True).then_inc(kswap_ready, 1)
                wide("w_gate", layer, l_hi, l_lo, T, 8, 2, ring=True)
                pe.wait_ge(n_sq, layer + 1)
                pe.wait_ge(kswap_taken, layer + 1)
                pass_wait()
                for j in range(4):
                    ins = mm(ps[:, 4 + j, :], ones, NSQ[:, 2 * j:2 * j + 2, :], start=True, stop=True)
                ins.then_inc(n_sum, 1)
                wide("w_gate", layer, l_hi, l_lo, T, 10, 2, ring=True)
                pe.wait_ge(n_var, layer + 1)
                pe.wait_ge(sums_taken, group("w_gate", layer, 12) + 2)

                def scores(r):
                    if r >= 2:
                        pe.wait_ge(b_max, layer * 12 + r - 1)
                    for qb in range(2):
                        if r < 4:
                            q, k = qkb[:, r, qb * P:qb * P + P], qkb[:, 4 + r, :]
                        else:
                            h = r - 4
                            rows = slice(64 * (h % 2), 64 * (h % 2) + 64)
                            kv = h // 4
                            q, k = qc[rows, h // 2, qb * P:qb * P + P], kc[rows, 0 if kv == h % 2 else 1, :]
                        ins = mm(ps[:, 4 + r % 2, qb * T:qb * T + T], q, k, start=True, stop=True)
                    ins.then_inc(b_s, 1)

                def turn(r):
                    pe.wait_ge(b_prob, layer * 12 + r + 1)
                    if r >= 2:
                        pe.wait_ge(b_copied, layer * 12 + r - 1)
                    for kb in range(2):
                        for qb in range(2):
                            ins = nc.tensor.transpose(ps[:, 6 + r % 2, kb * T + qb * P:kb * T + qb * P + P],
                                                      TT2[:, r % 2, qb, kb * P:kb * P + P], ident)
                    ins.then_inc(b_turned, 1)

                def mix(r):
                    pe.wait_ge(b_copied, layer * 12 + r + 1)
                    if r >= 2:
                        pe.wait_ge(b_taken, layer * 12 + r - 1)
                    for kb in range(2):
                        if r < 4:
                            v = vb[:, kb, r * P:r * P + P]
                        else:
                            h = r - 4
                            v = vc[:, kb, 0 if h // 4 == h % 2 else 1, :]
                        ins = mm(ps[:, r % 2, 0:T], v, PT2[:, r % 2, kb, :], start=kb == 0, stop=kb == 1)
                    ins.then_inc(b_o, 1)
                scores(0)
                for r in range(14):
                    if r < 11:
                        scores(r + 1)
                    if 1 <= r < 13:
                        turn(r - 1)
                    if r >= 2:
                        mix(r - 2)
                pe.wait_ge(b_taken, layer * 12 + 12)
                pe.wait_ge(b_copied, layer * 12 + 12)

                pe.wait_ge(g_rate, layer + 1)
                pass_wait()
                mm(ps[0:64, 4, 0:16], m64[:, 0, :], gdec[:], start=True, stop=True)
                mm(ps[0:64, 4, 16:32], m64[:, 1, :], gdec[:], start=True, stop=True).then_inc(gd_sums, 1)
                for hp in range(2):
                    w = layer * 2 + hp
                    pe.wait_ge(gd_ready, w + 1)
                    mm(ps[:, 4, :], ones[0:64, :], Pm[:], start=True, stop=True)
                    mm(ps[0:64, 5, :], ones[0:64, 0:64], Mm[:], start=True, stop=True)
                    for y in range(8):
                        h, n = 2 * hp + y // 4, y % 4
                        q, k, v = (CV[:, 4 * j + h, n * CH:n * CH + CH] for j in range(3))
                        mm(ps[0:64, 6, y * CH:y * CH + CH], k, k, start=True, stop=True)
                        mm(ps[0:64, 7, y * CH:y * CH + CH], k, q, start=True, stop=True)
                        nc.tensor.transpose(ps[0:64, y // 4, (y % 4) * P:(y % 4) * P + P], k, ident)
                        ins = nc.tensor.transpose(ps[0:64, 2 + y // 4, (y % 4) * P:(y % 4) * P + P], v, ident)
                    ins.then_inc(gd_kk, 1)
                    for lv in range(6):
                        for g in range(2):
                            pe.wait_ge(inv_ready, w * 12 + lv * 2 + g + 1)
                            pass_wait()
                            for y in range(4):
                                rhs = TU[:, g, 0, y, :] if lv else ident[0:64, 0:64]
                                ins = mm(ps[0:64, 4 + 3 * g, y * CH:y * CH + CH], Mm[:, 4 * g + y, :], rhs,
                                         start=True, stop=True)
                            ins.then_inc(inv_p, 1)
                        for g in range(2):
                            if lv == 0:
                                break
                            pe.wait_ge(inv_pc, w * 10 + lv * 2 + g - 1)
                            pass_wait()
                            for y in range(4):
                                p, u = Pm[:, 4 * g + y, :], TU[:, g, 1, y, :]
                                if lv < 5:
                                    mm(ps[0:64, 5 + g, y * CH:y * CH + CH], u, p, start=True, stop=True)
                                ins = mm(ps[0:64, 5 + g, (4 + y) * CH:(5 + y) * CH], p, u, start=True, stop=True)
                            ins.then_inc(inv_done, 1)
                    pe.wait_ge(inv_next, w * 2 + 2)
                    pass_wait()
                    for y in range(8):
                        u = TU[:, y // 4, 1, y % 4, :]
                        mm(ps[0:64, y // 4, (y % 4) * P:(y % 4) * P + P], u, vT[:, y, :], start=True, stop=True)
                        ins = mm(ps[:, 4, y * CH:y * CH + CH], kbg[:, y, :], u, start=True, stop=True)
                    ins.then_inc(uw_ready, 1)
                    pe.wait_ge(uw_taken, w + 1)
                    for n in range(4):
                        x = w * 4 + n
                        outs = [ps[:, 2 + j, n * CH:n * CH + CH] for j in range(2)]
                        if n:
                            pe.wait_ge(sc_next, w * 3 + n)
                            for j in range(2):
                                ins = mm(ps[0:64, 5, j * P:j * P + P], wT[:, 4 * j + n, :], Sst[:, j, :],
                                         start=True, stop=True)
                            ins.then_inc(sc_w, 1)
                            for j in range(2):
                                mm(outs[j], Sst[:, j, :], qdec[:, 4 * j + n, :], start=True, stop=False)
                        pe.wait_ge(sc_v, x + 1)
                        pass_wait()
                        if n < 3:
                            for j in range(2):
                                ins = mm(ps[:, 7, j * P:j * P + P], kdec[:, 4 * j + n, :], vnew[:, j, :],
                                         start=True, stop=True)
                            ins.then_inc(sc_s, 1)
                        for j in range(2):
                            ins = mm(outs[j], vnew[:, j, :], qkT[:, 4 * j + n, :], start=n == 0, stop=True)
                        if n == 3:
                            ins.then_inc(sc_s, 1)
                def branch(first):
                    def body(i, u, s, turn):
                        u += first
                        br = (u // 2 + 1) % 3
                        wait_tile(s, turn)
                        pe.wait_ge(sums_taken, group("w_br", layer, u + 1))
                        b = pair("w_br", u)
                        for mi in range(4):
                            for c in range(4):
                                ins = product(ps[:, b + mi // 2, (mi % 2) * T:(mi % 2 + 1) * T], mi * 4 + c, s,
                                              o_hi[:, 4 * br + c, :], o_lo[:, 4 * br + c, :], c == 0, c == 3)
                        ins.then_inc(tile_used, 1)
                    return body
                tiles("w_br", layer, pe, branch(0), 0, 1)
                pe.wait_ge(go_sq, layer + 1)
                for j in range(2):
                    ins = mm(ps[:, 4 + j, :], ones, osq[:, 2 * j:2 * j + 2, :], start=True, stop=True)
                ins.then_inc(go_sum, 1)
                tiles("w_br", layer, pe, branch(1), 1, 3)
                have(3)
                tiles("w_br", layer, pe, branch(4), 4, 2)
                have(4)
                wide("w_out", layer, m_hi, m_lo, T)
                norm(layer * 3 + 5, LAT, (layer, 1))
                wide("ff2_in", layer, l_hi, l_lo, T, 0, 4, blocks=layer * 3 * DC + 6 * DC)
                have(5)
                wide("ff2_in", layer, l_hi, l_lo, T, 4, ring=True)
                have(6)
                deep("ff2_out", layer, fh_hi, fh_lo, T, 4)
                norm(layer * 3 + 6, LAT, (layer, 2))

        @block.scalar
        def _(act):
            fn = nc.scalar.activation

            def split_hi(s, turn):
                act.wait_ge(raw_full[raw_slot(s)], turn * 16 + 16 * (s // 4 + 1))
                act.wait_ge(tile_used, turn * 4 + s + 1)
                nc.scalar.copy(w_hi[:, s % SPLIT], raw[:, raw_slot(s)]).then_inc(hi_done, 1)

            def only_split(phase, layer, first=0, count=None, per=4):
                tiles(phase, layer, act, lambda i, u, s, turn: split_hi(s + SPLIT, turn), first, count, per)

            def inverse_root(v):
                fn(v, v, ACT.Ln)
                act.drain()
                return fn(v, v, ACT.Exp, scale=-0.5)

            def norm(q, cols, gains, hi, mean=None):
                width = cols.stop - cols.start
                if mean is None and q:
                    act.wait_ge(sums_taken, after_norm_input(q))
                for c in range(DC):
                    if mean is not None:
                        act.wait_ge(centred, mean * DC + c + 1)
                    fn(SQ[:, c, 0:width], X[:, c, cols], ACT.Square).then_inc(sq_ready, 1)
                act.wait_ge(var_ready, q + 1)
                inverse_root(rr[:, 0:width]).then_inc(std_ready, 1)
                for c in range(DC):
                    act.wait_ge(scaled, q * DC + c + 1)
                    v = SQ[:, c, 0:width] if mean is None else X[:, c, cols]
                    for part, (gain, shift) in gains(c):
                        fn(v[:, part], v[:, part], ACT.Identity, bias=shift, scale=gain)
                    act.drain()
                    nc.scalar.copy(hi[:, c, :], v).then_inc(normed, 1)

            def ada_gains(layer, which, parts):
                def of(c):
                    return [(part, (mod[:, layer, 8 * (which + 1) + c, j:j + 1], mod[:, layer, 8 * which + c, j:j + 1]))
                            for part, j in parts]
                return of

            def ln_gains(j):
                def of(c):
                    g, b = C_LN[j]
                    return [(slice(0, T), (cols2[:, g + c:g + c + 1], cols2[:, b + c:b + c + 1]))]
                return of

            def swiglu(phase, layer, dst, width, number):
                def body(i, u, s, turn):
                    if width == T:
                        split_hi(s + SPLIT, turn)
                    b = pair(phase, u) if width == TT else bank(phase, u)
                    act.wait_ge(tile_used, turn * 4 + s + 1 + SPLIT)
                    act.wait_ge(sums_taken, group(phase, layer, i * 4 + u + 1))
                    fn(dst[:, u % 2, 0:width], ps[:, b, 0:width], ACT.Silu).then_inc(silu_ready, 1)
                    if width == TT:
                        split_hi(s + SPLIT, turn)
                tiles(phase, layer, act, body)

            both = [(CTX, 0), (LAT, 1)]
            act.wait_ge(cols_in, 16)
            fn(silu_c[:], cols1[:, C_COND:C_COND + 16].rearrange("p (a b) -> p a b", b=2), ACT.Silu
               ).then_inc(silu_c_ready, 1)
            split_hi(0, 0)
            split_hi(1, 0)
            act.wait_ge(lgam_abs, 1)
            fn(small[:, 0:8], small[:, 0:8], ACT.Exp).then_inc(lgam_exp, 1)
            act.wait_ge(lgam_one, 1)
            fn(small[:, 8:16], rr[:, 0:8], ACT.Ln).then_inc(lgam_ln, 1)

            def ada_decays(i, u, s, turn):
                split_hi(s + SPLIT, turn)
                h = u // 3
                if u == 2:
                    act.wait_ge(lgam_ready, 1)
                    act.wait_ge(dist_in, 16)
                if u % 3 == 2:
                    if h:
                        act.wait_ge(decays_ready, h)
                    for d in range(2):
                        fn(expd[:, d], dist[:, d], ACT.Exp, scale=lgam[:, 4 * d + h:4 * d + h + 1]
                           ).then_inc(decays_exp, 1)
            tiles("ada", 0, act, ada_decays, 0, 3 * RET_H, per=3 * RET_H)
            only_split("ada", 0, 3 * RET_H)
            act.wait_ge(x_in, 16)
            act.wait_ge(mod_scaled, 1)
            norm(0, slice(0, TT), ada_gains(0, 0, both), h_hi)
            only_split("ret_qkv", 0)
            for h in range(RET_H):
                act.wait_ge(ho_centred, h + 1)
                fn(sqh[:], V[:, h], ACT.Square).then_inc(ho_sq, 1)
                act.wait_ge(ho_var, h + 1)
                inverse_root(rr[:]).then_inc(ho_std, 1)

            def gate_silu(i, u, s, turn):
                b = pair("ret_g", u)
                act.wait_ge(tile_used, turn * 4 + s + 1 + SPLIT)
                act.wait_ge(sums_taken, group("ret_g", 0, i * 4 + u + 2))
                fn(gs[:], ps[:, b:b + 2, :], ACT.Silu).then_inc(silu_ready, 1)
                split_hi(s + SPLIT, turn)
            tiles("ret_g", 0, act, gate_silu)
            only_split("ret_out", 0)
            norm(1, slice(0, TT), ada_gains(0, 3, both), h_hi)
            swiglu("ffn_in0", 0, fs, TT, 8)
            only_split("ffn_out0", 0, 0, 11)
            norm(2, slice(0, TT), ada_gains(1, 0, both), h_hi)
            only_split("diff_in", 0)
            act.wait_ge(lam_dot, 1)
            fn(lam[:, 0:2], lam[:, 0:2], ACT.Exp).then_inc(lam_exp, 1)
            act.wait_ge(qk_in, 1)
            for j in range(3):
                fn(SQ1[:, 4 * j:4 * j + 4], QK1[:, 4 * j:4 * j + 4], ACT.Square).then_inc(qk_sq, 1)
            for j in range(3):
                act.wait_ge(qk_sums_taken, 4 * j + 4)
                fn(R1[:, 4 * j:4 * j + 4], R1[:, 4 * j:4 * j + 4], ACT.Ln)
            act.drain()
            for j in range(3):
                fn(R1[:, 4 * j:4 * j + 4], R1[:, 4 * j:4 * j + 4], ACT.Exp, scale=-0.5).then_inc(qk_std, 1)

            def diff_copy(r):
                h, qb = r // 2, r % 2
                act.wait_ge(s_turned, r + 1)
                if h >= 2:
                    act.wait_ge(so_ready, h - 1)
                nc.scalar.copy(PT1[:, h % 2, :, qb * P:qb * P + P], ps[:, r % 2, :].rearrange("p (a b) -> p a b", b=P)
                               ).then_inc(s_copied, 1)
            for r in range(16):
                act.wait_ge(s_max, r + 1)
                for m in range(2):
                    ins = fn(E1[:, r % 2, m], ps[:, 4 + 2 * (r % 2) + m, :], ACT.Exp, bias=softx[:, r % 2, 2 + m:3 + m],
                             scale=0.125, accum_out=softx[:, r % 2, 4 + m:5 + m])
                ins.then_inc(s_exp, 1)
                if r:
                    diff_copy(r - 1)
            diff_copy(15)
            act.wait_ge(so_taken, 8)
            fn(SO1[:], O1[:], ACT.Square).then_inc(so_sq, 1)
            act.wait_ge(so_var, 1)
            inverse_root(RO1[:]).then_inc(so_std, 1)
            only_split("diff_out", 0)
            norm(3, LAT, ada_gains(1, 3, [(slice(0, T), 1)]), h_hi[:, :, LAT])
            swiglu("ffn_in1", 0, fs, T, 30)
            only_split("ffn_out1", 0, 0, 11)

            with act.Fori(0, LAYERS2) as layer:
                swiglu("ff1_in", layer, gs2, T, 52)
                only_split("ff1_out", layer)
                act.wait_ge(params_in, layer * 48 + 48)
                norm(layer * 3 + 4, LAT, ln_gains(0), l_hi, layer * 3)
                only_split("w_in", layer)

                def gates(i, u, s, turn):
                    split_hi(s + SPLIT, turn)
                    b = bank("w_gate", u)
                    act.wait_ge(tile_used, turn * 4 + s + 1 + SPLIT)
                    act.wait_ge(sums_taken, group("w_gate", layer, u + 2))
                    for mi in range(2):
                        blk = 2 * u + mi
                        ins = fn(gate[:, blk, :], ps[:, b, mi * T:mi * T + T], ACT.Sigmoid,
                                 bias=cols2[:, C_BG + blk:C_BG + blk + 1])
                    ins.then_inc(sums_taken, 1)
                    if u == 6:
                        act.wait_ge(conv_done, layer + 1)
                        fn(CV[:, 0:8], CV[:, 0:8], ACT.Silu)
                    elif u == 7:
                        act.drain()
                        fn(NSQ[:], CV[:, 0:8], ACT.Square).then_inc(n_sq, 1)
                    elif u == 8:
                        act.wait_ge(m_in, layer + 1)
                        fn(za[:], za[:], ACT.Silu).then_inc(za_ready, 1)
                    elif u == 9:
                        fn(CV[:, 8:12], CV[:, 8:12], ACT.Silu).then_inc(conv_silu, 1)
                tiles("w_gate", layer, act, gates, per=16)
                act.wait_ge(n_var, layer + 1)
                inverse_root(NR[:]).then_inc(n_std, 1)

                def turned_copy(r):
                    act.wait_ge(b_turned, layer * 12 + r + 1)
                    if r >= 2:
                        act.wait_ge(b_o, layer * 12 + r - 1)
                    nc.scalar.copy(PT2[:, r % 2], ps[:, 6 + r % 2, :].rearrange("p (a c) -> p a c", c=T)
                                   ).then_inc(b_copied, 1)
                for r in range(12):
                    act.wait_ge(b_max, layer * 12 + r + 1)
                    for qb in range(2):
                        ins = fn(TT2[:, r % 2, qb], TT2[:, r % 2, qb], ACT.Exp, bias=softx[:, r % 2, 2 + qb:3 + qb],
                                 scale=1.0 if r < 4 else 0.125, accum_out=softx[:, r % 2, 4 + qb:5 + qb])
                    if r >= 4:
                        ins = fn(softx[:, r % 2, 8:10], softx[:, r % 2, 8:10], ACT.Exp)
                    ins.then_inc(b_exp, 1)
                    if r:
                        turned_copy(r - 1)
                turned_copy(11)
                act.wait_ge(g_lin, layer + 1)
                fn(bt[:, 2], bt[:, 2], ACT.Exp)
                fn(bt[:, 3, 0:4], rows2[0:64, R_ALOG:R_ALOG + 4], ACT.Exp).then_inc(g_exp, 1)
                act.wait_ge(g_mid, layer + 1)
                fn(bt[:, 5], bt[:, 4], ACT.Ln)
                fn(bt[:, 0], bt[:, 0], ACT.Exp, scale=-1.0).then_inc(g_ln, 1)
                act.wait_ge(gd_taken, layer + 1)
                fn(gexp[:], gcum[:], ACT.Exp)
                fn(gsuf[:], gsuf[:], ACT.Exp).then_inc(gd_exp, 1)
                for hp in range(2):
                    w = layer * 2 + hp
                    act.wait_ge(gd_kk, w + 1)
                    act.wait_ge(gd_diff, w + 1)
                    fn(gcb[:], ps[:, 4, :].rearrange("p (a b) -> p a b", b=CH), ACT.Exp)
                    fn(DT[:], DT[:], ACT.Exp).then_inc(gd_decay, 1)
                act.wait_ge(go_copied, layer * 2 + 2)
                fn(osq[:], oraw[:], ACT.Square).then_inc(go_sq, 1)
                act.wait_ge(go_var, layer + 1)
                inverse_root(ostd[:]).then_inc(go_std, 1)
                only_split("w_br", layer)
                only_split("w_out", layer)
                norm(layer * 3 + 5, LAT, ln_gains(1), l_hi, layer * 3 + 1)
                swiglu("ff2_in", layer, gs2, T, 84)
                only_split("ff2_out", layer)
                norm(layer * 3 + 6, LAT, ln_gains(2), l_hi, layer * 3 + 2)

        @block.vector
        def _(dve):
            tt, ts, stt, copy = (nc.vector.tensor_tensor, nc.vector.tensor_scalar, nc.vector.scalar_tensor_tensor,
                                 nc.vector.tensor_copy)

            def split_lo(s, turn):
                dve.wait_ge(hi_done, turn * 4 + s + 1)
                tt(w_lo[:, raw_slot(s)], raw[:, raw_slot(s)], w_hi[:, s % SPLIT].bitcast(F32), ALU.subtract
                   ).then_inc(lo_done, 1)

            def each(phase, layer, take, first=0, count=None, per=4, split_first=False):
                def body(i, u, s, turn):
                    if split_first:
                        split_lo(s + SPLIT, turn)
                    dve.wait_ge(tile_used, turn * 4 + s + 1 + SPLIT)
                    take(i, u)
                    if not split_first:
                        split_lo(s + SPLIT, turn)
                tiles(phase, layer, dve, body, first, count, per)

            def halves(hi, lo, src):
                copy(hi, src)
                dve.drain()
                return tt(lo, src, hi.bitcast(F32), ALU.subtract)

            def norm(q, cols, hi, lo, mean=None, eps=EPS):
                width = cols.stop - cols.start
                r = rr[:, 0:width]
                if mean is not None:
                    dve.wait_ge(mean_ready, mean + 1)
                    ts(r, ps[:, 4, 0:width], 1.0 / D, None, ALU.mult)
                    dve.drain()
                    for c in range(DC):
                        tt(X[:, c, cols], X[:, c, cols], r, ALU.subtract).then_inc(centred, 1)
                    dve.drain()
                dve.wait_ge(square_sum, q + 1)
                ts(r, ps[:, 5, 0:width], 1.0 / D, eps, ALU.mult, ALU.add).then_inc(var_ready, 1)
                dve.wait_ge(std_ready, q + 1)
                for c in range(DC):
                    v = SQ[:, c, 0:width] if mean is None else X[:, c, cols]
                    tt(v, X[:, c, cols], r, ALU.mult).then_inc(scaled, 1)
                v = SQ[:, :, 0:width] if mean is None else X[:, :, cols]
                for c in range(DC):
                    dve.wait_ge(normed, q * DC + c + 1)
                    ins = tt(lo[:, c, :], v[:, c, :], hi[:, c, :].bitcast(F32), ALU.subtract)
                    ins.then_inc(block_ready, 1)
                dve.drain()
                copy(small[:, 15:16], small[:, 14:15]).then_inc(operand_ready, 1)

            def swiglu(phase, layer, gates, prods, hi, lo, width, number):
                def take(i, u):
                    b = pair(phase, u) if width == TT else bank(phase, u)
                    up = ps[:, b + 1, 0:TT] if width == TT else ps[:, b, T:TT]
                    dve.wait_ge(silu_ready, layer * 64 + i * 4 + u + number + 1)
                    tt(prods[:, u % 2, 0:width], gates[:, u % 2, 0:width], up, ALU.mult)
                    dve.drain()
                    blk = bass.ds(i * 4 + u, 1)
                    halves(hi[:, blk, 0:width], lo[:, blk, 0:width], prods[:, u % 2:u % 2 + 1, 0:width]
                           ).then_inc(sums_taken, 1)
                each(phase, layer, take, split_first=width == T)
                dve.drain()
                copy(small[:, 15:16], small[:, 14:15]).then_inc(operand_ready, 1)

            dve.sem_inc(sums_taken, 2)
            dve.sem_inc(layer_used, 1)
            nc.vector.memset(small[:], 0.0)
            dve.drain()
            dve.wait_ge(silu_c_ready, 1)
            halves(cond4[:, :, 0:2], cond4[:, :, 2:4], silu_c[:]).then_inc(cond_ready, 1)
            split_lo(0, 0)
            split_lo(1, 0)
            dve.wait_ge(logit_in, 16)
            stt(small[:, 0:8], lgam[:], -1.0, lgam[:], ALU.mult, ALU.min).then_inc(lgam_abs, 1)
            dve.wait_ge(lgam_exp, 1)
            ts(rr[:, 0:8], small[:, 0:8], 1.0, None, ALU.add).then_inc(lgam_one, 1)
            dve.wait_ge(lgam_ln, 1)
            ts(rr[:, 8:16], rr[:, 0:8], -1.0, 1e-30, ALU.add, ALU.max)
            dve.drain()
            nc.vector.reciprocal(rr[:, 8:16], rr[:, 8:16])
            dve.drain()
            tt(rr[:, 8:16], rr[:, 8:16], small[:, 0:8], ALU.mult)
            dve.drain()
            tt(small[:, 8:16], small[:, 8:16], rr[:, 8:16], ALU.mult)
            dve.drain()
            stt(lgam[:], lgam[:], 0.0, small[:, 8:16], ALU.min, ALU.subtract).then_inc(lgam_ready, 1)
            dve.wait_ge(consts_in, 16)
            tt(parts_sum[:], ident[0:4, 0:2], ident[0:4, 2:4], ALU.add).then_inc(tables_ready, 1)

            def ada_copy(u):
                copy(ada_row[:, u % 2], ps[0:4, 4 + u % 2, 0:T]).then_inc(sums_taken, 1)

            def ada_add(t, u):
                dve.wait_ge(ada_turned, t + 1)
                tt(mod[:].rearrange("p l c v -> p (l c) v")[:, bass.ds(t * 2, 2), :],
                   ps[:, 6 + u % 2, 0:4].rearrange("p (a b) -> p a b", b=2),
                   cols1[:, bass.ds(t * 2, 2)].unsqueeze(2).to_broadcast([P, 2, 2]), ALU.add).then_inc(mod_ready, 1)

            def first_ada(i, u):
                ada_copy(u)
                if u:
                    ada_add(u - 1, u - 1)

            def later_ada(i, u):
                ada_copy(u)
                ada_add(i * 4 + u + 3, (u - 1) % 4)
            each("ada", 0, first_ada, 0, 4)
            each("ada", 0, later_ada, 4)
            ada_add(ADA_TILES - 1, 3)
            dve.drain()
            for l in range(2):
                for w in (1, 4):
                    ins = ts(mod[:, l, 8 * w:8 * w + 8, :], mod[:, l, 8 * w:8 * w + 8, :], 1.0, None, ALU.add)
            ins.then_inc(mod_scaled, 1)
            dve.wait_ge(x_in, 16)

            norm(0, slice(0, TT), h_hi[:], h_lo[:])
            dve.wait_ge(decays_ready, RET_H)

            def take_qk(i, u):
                b = pair("ret_qkv", u)
                copy(QK[:, bass.ds(i * 8 + 2 * u, 2), :], ps[:, b:b + 2, :]).then_inc(sums_taken, 1)

            def take_v(i, u):
                b = pair("ret_qkv", u)
                dst = V[:, bass.ds(i * 2 + u // 2, 1), :, (u % 2) * T:(u % 2 + 1) * T]
                copy(dst.rearrange("p a b c -> p (a b) c"), ps[:, b:b + 2, :].rearrange("p b (a c) -> p (b a) c", c=T)
                     ).then_inc(sums_taken, 1)
            each("ret_qkv", 0, take_qk, 0, 8)
            each("ret_qkv", 0, take_v, 8, 8)
            dve.drain()

            def rotate(x, sums, cos, sin, tmp):
                tt(tmp[:, 0], x, cos, ALU.mult)
                tt(tmp[:, 1], sums, sin, ALU.mult)
                dve.drain()
                return tt(x, tmp[:, 0], tmp[:, 1], ALU.add)
            dve.wait_ge(tables_in, 32)
            for r in range(8):
                dve.wait_ge(rot_ready, r + 1)
                rotate(QK[:, 2 * r:2 * r + 2, LAT], ps[:, 4 + r % 4, :].rearrange("p (a b) -> p a b", b=T),
                       rope_r[:, 0], rope_r[:, 1], rtmp).then_inc(rot_taken, 1)
                dve.drain()
            for h in range(RET_H):
                dve.wait_ge(att_ready, h + 1)
                stt(att[:, 0:4, :], ps[:, 4:6, :].rearrange("p b (a c) -> p (b a) c", c=T), 0.0625, DM[:, h],
                    ALU.mult, ALU.mult)
                stt(att[:, 4:6, :], ps[:, 6, :].rearrange("p (a c) -> p a c", c=T), 0.0625, DM[:, h, 2:4],
                    ALU.mult, ALU.mult).then_inc(att_decayed, 1)
                dve.wait_ge(ho_ready, h + 1)
                copy(V[:, h], ps[:, 0:4, :]).then_inc(ho_taken, 1)
                dve.wait_ge(ho_mean, h + 1)
                ts(rr[:], ps[:, 7, :], 1.0 / TT, None, ALU.mult)
                dve.drain()
                tt(V[:, h], V[:, h], rr[:].unsqueeze(1).to_broadcast([P, 4, TT]), ALU.subtract).then_inc(ho_centred, 1)
                dve.wait_ge(ho_sqsum, h + 1)
                ts(rr[:], ps[:, 4, :], 1.0 / TT, EPS, ALU.mult, ALU.add).then_inc(ho_var, 1)
                dve.wait_ge(ho_std, h + 1)
                tt(V[:, h], V[:, h], rr[:].unsqueeze(1).to_broadcast([P, 4, TT]), ALU.mult)
                dve.drain()
            Vb = V[:].rearrange("p h b t -> p (h b) t")

            def take_g(i, u):
                dve.wait_ge(silu_ready, i * 4 + u + 1)
                for mi in range(2):
                    blk = i * 8 + 2 * u + mi
                    stt(gp[:, mi:mi + 1, :], Vb[:, bass.ds(blk, 1), :], cols1[:, bass.ds(blk + C_RETG, 1)],
                        gs[:, mi:mi + 1, :], ALU.mult, ALU.mult)
                dve.drain()
                two = bass.ds(i * 8 + 2 * u, 2)
                halves(y_hi[:, two, :], y_lo[:, two, :], gp[:]).then_inc(sums_taken, 1)
            each("ret_g", 0, take_g)
            dve.drain()
            copy(small[:, 15:16], small[:, 14:15]).then_inc(operand_ready, 1)

            def add_gated(layer, which, m, sums, parts):
                for part, cols, j in parts:
                    ins = stt(X[:, m, cols], sums[:, part], mod[:, layer, 8 * which + m, j:j + 1], X[:, m, cols],
                              ALU.mult, ALU.add)
                return ins
            both = [(CTX, CTX, 0), (LAT, LAT, 1)]
            lat = [(slice(0, T), LAT, 1)]

            def take_ret_out(i, u):
                if u % 2:
                    b = pair("ret_out", u // 2)
                    for mi in range(2):
                        ins = add_gated(0, 2, 2 * (u // 2) + mi, ps[:, b + mi, :], both)
                    ins.then_inc(sums_taken, 1)
            each("ret_out", 0, take_ret_out, per=16)
            dve.drain()
            norm(1, slice(0, TT), h_hi[:], h_lo[:])
            swiglu("ffn_in0", 0, fs, fp, hid_hi, hid_lo, TT, 8)

            def ffn_out(phase, layer, parts):
                each(phase, 0, lambda i, u: None, 0, 11)
                for m in range(DC):
                    ins = add_gated(layer, 5, m, ps[:, m, :], parts)
                    if m >= DC - 2:
                        ins.then_inc(sums_taken, 1)
                dve.drain()
            ffn_out("ffn_out0", 0, both)

            norm(2, slice(0, TT), h_hi[:], h_lo[:])

            def take_diff(i, u):
                b = pair("diff_in", u) if u >= 4 else bank("diff_in", u)
                if u < 4:
                    ins = copy(QK1[:, u, :], ps[:, b, :])
                elif u < 8:
                    ins = copy(QK1[:, 4 + 2 * (u - 4):6 + 2 * (u - 4), :], ps[:, b:b + 2, :])
                else:
                    ins = copy(V1[:, :, (u - 8) * T:(u - 7) * T], ps[:, b:b + 2, :].rearrange("p b (a c) -> p (b a) c", c=T))
                ins.then_inc(sums_taken, 1)
            each("diff_in", 0, take_diff, per=16)
            dve.wait_ge(lam_in, 16)
            tt(lamv[:, 0:4:2], lamv[:, 0:4:2], lamv[:, 1:4:2], ALU.mult)
            dve.drain()
            nc.vector.tensor_reduce(lam[:, 0:2], lamv[:, 0:4:2], AX, ALU.add).then_inc(lam_dot, 1)
            dve.drain()
            copy(small[:, 15:16], small[:, 14:15]).then_inc(qk_in, 1)
            dve.wait_ge(lam_exp, 1)
            stt(lam[:, 2:3], lam[:, 1:2], -LAMBDA_INIT, lam[:, 0:1], ALU.add, ALU.subtract)
            for r in range(12):
                dve.wait_ge(qk_sums, r + 1)
                ts(R1[:, r], ps[:, 4 + r % 4, :], 1.0 / 64, EPS, ALU.mult, ALU.add).then_inc(qk_sums_taken, 1)
            for j in range(3):
                some, gain = slice(4 * j, 4 * j + 4), C_DKG if j else C_DQG
                dve.wait_ge(qk_std, j + 1)
                stt(QK1[:, some], QK1[:, some], cols1[:, gain:gain + 1], R1[:, some], ALU.mult, ALU.mult
                    ).then_inc(qk_ready, 1)
            dtmp = SQ1[:, 0:2, :].rearrange("p t (a b) -> p t a b", b=T)
            dve.drain()
            for r in range(8):
                dve.wait_ge(drot_ready, r + 1)
                x = (QK1[:, r, :].rearrange("p (a b) -> p a b", b=T) if r < 4
                     else QK1[:, 4 + 2 * (r - 4):6 + 2 * (r - 4), LAT])
                cos, sin = (rope_d[:, j].unsqueeze(1).to_broadcast([P, 2, T]) for j in range(2))
                rotate(x, ps[:, 4 + r % 4, :].rearrange("p (a b) -> p a b", b=T), cos, sin, dtmp).then_inc(drot_taken, 1)
                dve.drain()

            def diff_max(r):
                dve.wait_ge(s_ready, r + 1)
                b = 4 + 2 * (r % 2)
                nc.vector.tensor_reduce(softx[:, r % 2, 0:2], ps[:, b:b + 2, :], AX, ALU.max)
                dve.drain()
                ts(softx[:, r % 2, 2:4], softx[:, r % 2, 0:2], -0.125, None, ALU.mult).then_inc(s_max, 1)

            def diff_prob(r):
                dve.wait_ge(s_exp, r + 1)
                sx = softx[:, r % 2]
                nc.vector.reciprocal(sx[:, 6:8], sx[:, 4:6])
                dve.drain()
                tt(sx[:, 7:8], sx[:, 7:8], lam[:, 2:3], ALU.mult)
                if r >= 2:
                    dve.wait_ge(s_turned, r - 1)
                ts(P1[:, r % 2], E1[:, r % 2, 0], sx[:, 6:7], None, ALU.mult)
                dve.drain()
                stt(P1[:, r % 2], E1[:, r % 2, 1], sx[:, 7:8], P1[:, r % 2], ALU.mult, ALU.add).then_inc(s_prob, 1)

            def diff_out_head(h):
                dve.wait_ge(so_ready, h + 1)
                copy(O1[:, h, :], ps[:, 2 + h % 2, 0:T]).then_inc(so_taken, 1)
            for r in range(20):
                if r < 16:
                    diff_max(r)
                if 1 <= r < 17:
                    diff_prob(r - 1)
                if r >= 5 and r % 2 == 1:
                    diff_out_head((r - 5) // 2)
            dve.wait_ge(so_sum, 1)
            for r in range(4):
                ins = ts(RO1[:, 2 * r:2 * r + 2, :], ps[:, 4 + r, :].rearrange("p (a b) -> p a b", b=T), 1.0 / P, EPS,
                         ALU.mult, ALU.add)
            ins.then_inc(so_var, 1)
            dve.wait_ge(so_std, 1)
            tt(O1[:], O1[:], RO1[:], ALU.mult)
            dve.drain()
            ts(O1[:], O1[:], cols1[:, C_SUB:C_SUB + 1], 1.0 - LAMBDA_INIT, ALU.mult, ALU.mult)
            dve.drain()
            halves(d_hi[:], d_lo[:], O1[:]).then_inc(operand_ready, 1)

            def take_diff_out(i, u):
                b = bank("diff_out", u)
                for mi in range(2):
                    ins = add_gated(1, 2, 2 * u + mi, ps[:, b, mi * T:mi * T + T], lat)
                ins.then_inc(sums_taken, 1)
            each("diff_out", 0, take_diff_out, per=8)
            dve.drain()
            norm(3, LAT, h_hi[:, :, LAT], h_lo[:, :, LAT])
            swiglu("ffn_in1", 0, fs, fp, hid_hi, hid_lo, T, 30)
            ffn_out("ffn_out1", 1, lat)
            for c in range(DC):
                copy(l_hi[:, c, :], X[:, c, LAT])
                dve.drain()
                tt(l_lo[:, c, :], X[:, c, LAT], l_hi[:, c, :].bitcast(F32), ALU.subtract).then_inc(block_ready, 1)
            dve.drain()
            copy(small[:, 15:16], small[:, 14:15]).then_inc(operand_ready, 1)

            with dve.Fori(0, LAYERS2) as layer:
                def scale_residual():
                    ts(X[:, :, LAT], X[:, :, LAT], ALPHA, None, ALU.mult)
                    dve.drain()

                def scaled_sum(phase, width_pair, factor):
                    def take(m, b):
                        x = X[:, m, LAT]
                        sums = (ps[:, b:b + 2, 0:T] if width_pair else ps[:, b, :].rearrange("p (a c) -> p a c", c=T))
                        stt(x, sums, factor, x, ALU.mult, ALU.add).then_inc(sums_taken, 1)
                    return take

                def ff_out(phase):
                    add = scaled_sum(phase, True, 0.5)

                    def take(i, u):
                        if u % 4 == 3:
                            add(bass.ds(i * 4 + 2 * (u // 4), 2), pair(phase, u // 4))
                    each(phase, layer, take, per=8)
                    dve.drain()

                scale_residual()
                swiglu("ff1_in", layer, gs2, gp2, fh_hi, fh_lo, T, 52)
                ff_out("ff1_out")
                norm(layer * 3 + 4, LAT, l_hi[:], l_lo[:], layer * 3, LN_EPS)
                scale_residual()

                def take_in(i, u):
                    b = bank("w_in", u)

                    def fm(dst, col):
                        for mi in range(2):
                            ins = ts(dst[mi], ps[:, b, mi * T:mi * T + T], cols2[:, C_BIN + col + mi:C_BIN + col + mi + 1],
                                     None, ALU.add)
                        return ins
                    if u < 6:
                        ins = fm([QKVp[:, 2 * u + mi, 3:T + 3] for mi in range(2)], 2 * u)
                    elif u < 8:
                        ins = fm([za[:, 2 * (u - 6) + mi, :] for mi in range(2)], 2 * u)
                    elif u < 12:
                        ins = fm([qkb[:, 2 * (u - 8) + mi, :] for mi in range(2)], 2 * u)
                    elif u < 14:
                        c0 = (u - 12) * T
                        ins = tt(vb[:, :, c0:c0 + T], ps[:, b, :].rearrange("p (a c) -> p a c", c=T),
                                 rows2[:, R_VB + c0:R_VB + c0 + T].unsqueeze(1).to_broadcast([P, 2, T]), ALU.add)
                    elif u < 16:
                        ins = fm([qc[:, 2 * (u - 14) + mi, :] for mi in range(2)], 24 + 2 * (u - 14))
                    elif u == 16:
                        ts(kc[:, 0, :], ps[:, b, 0:T], cols2[:, C_BIN + 28:C_BIN + 29], None, ALU.add)
                        vv = ps[:, b, T:TT].rearrange("p (a c) -> p a c", c=P)
                        bias = rows2[:, R_VC:R_VC + P].unsqueeze(1).to_broadcast([P, 2, P])
                        tt(vc[:, :, 0, :], vv, bias, ALU.add)
                        tt(vc[:, :, 1, 0:64], vv[:, :, 64:128], bias[:, :, 64:128], ALU.add)
                        ins = tt(vc[:, :, 1, 64:128], vv[:, :, 0:64], bias[:, :, 0:64], ALU.add)
                    else:
                        ins = tt(ba[:], ps[0:64, b, 0:32].rearrange("p (a c) -> p a c", c=8),
                                 rows2[0:64, R_BETA:R_BETA + 8].unsqueeze(1).to_broadcast([64, 4, 8]), ALU.add)
                    ins.then_inc(sums_taken, 1)
                each("w_in", layer, take_in, per=32)
                nc.vector.memset(QKVp[:, :, 0:3], 0.0)
                dve.drain()
                copy(small[:, 15:16], small[:, 14:15]).then_inc(m_in, 1)

                def gate_tile(i, u, s, turn):
                    split_lo(s + SPLIT, turn)
                    if u < 6:
                        for tap in range(4):
                            for blk in (2 * u, 2 * u + 1):
                                w = cols2[:, C_CONV + tap * 12 + blk:C_CONV + tap * 12 + blk + 1]
                                x = QKVp[:, blk, tap:tap + T]
                                if tap == 0:
                                    ins = ts(CV[:, blk, :], x, w, None, ALU.mult)
                                else:
                                    ins = stt(CV[:, blk, :], x, w, CV[:, blk, :], ALU.mult, ALU.add)
                            if tap == 3 and u == 5:
                                ins.then_inc(conv_done, 1)
                            else:
                                dve.drain()
                    elif u == 8:
                        dve.wait_ge(kswap_ready, layer + 1)
                        copy(kc[:, 1, :], ps[:, 4, 0:T]).then_inc(kswap_taken, 1)
                    elif u == 10:
                        dve.wait_ge(n_sum, layer + 1)
                        ts(NR[:], ps[:, 4:8, :].rearrange("p b (a c) -> p (b a) c", c=T), 1.0, EPS, ALU.mult, ALU.add
                           ).then_inc(n_var, 1)
                tiles("w_gate", layer, dve, gate_tile, per=16)
                dve.wait_ge(n_std, layer + 1)
                dve.wait_ge(conv_silu, layer + 1)
                stt(CV[:, 0:4], CV[:, 0:4], P ** -0.5, NR[:, 0:4], ALU.mult, ALU.mult)
                tt(CV[:, 4:8], CV[:, 4:8], NR[:, 4:8], ALU.mult)
                dve.drain()

                dve.wait_ge(bias_ready, layer + 1)
                dve.wait_ge(band_in, 48)

                def soft_max(r):
                    dve.wait_ge(b_s, layer * 12 + r + 1)
                    if r >= 2:
                        dve.wait_ge(b_turned, layer * 12 + r - 1)
                    sx = softx[:, r % 2]
                    s = ps[:, 4 + r % 2, :].rearrange("p (a c) -> p a c", c=T)
                    if r < 4:
                        stt(TT2[:, r % 2], s, P ** -0.5, relB[:, r], ALU.mult, ALU.add)
                    else:
                        stt(TT2[:, r % 2], bandC[:], 8.0 * 2.0 ** -(r - 3), s, ALU.mult, ALU.add)
                    dve.drain()
                    nc.vector.tensor_reduce(sx[:, 0:2], TT2[:, r % 2], AX, ALU.max)
                    dve.drain()
                    if r < 4:
                        ins = ts(sx[:, 2:4], sx[:, 0:2], -1.0, None, ALU.mult)
                    else:
                        sink = rows2[:, R_SINK + r - 4:R_SINK + r - 3]
                        ts(sx[:, 0:2], sx[:, 0:2], 0.125, sink, ALU.mult, ALU.max)
                        dve.drain()
                        ts(sx[:, 2:4], sx[:, 0:2], -1.0, None, ALU.mult)
                        dve.drain()
                        ins = ts(sx[:, 8:10], sx[:, 2:4], sink, None, ALU.add)
                    ins.then_inc(b_max, 1)

                def soft_prob(r):
                    dve.wait_ge(b_exp, layer * 12 + r + 1)
                    sx = softx[:, r % 2]
                    if r >= 4:
                        tt(sx[:, 4:6], sx[:, 4:6], sx[:, 8:10], ALU.add)
                        dve.drain()
                    nc.vector.reciprocal(sx[:, 6:8], sx[:, 4:6])
                    dve.drain()
                    for qb in range(2):
                        ins = ts(TT2[:, r % 2, qb], TT2[:, r % 2, qb], sx[:, 6 + qb:7 + qb], None, ALU.mult)
                    ins.then_inc(b_prob, 1)

                def soft_out(r):
                    dve.wait_ge(b_o, layer * 12 + r + 1)
                    if r < 4:
                        rows, blk = slice(0, P), 4 + r
                    else:
                        h = r - 4
                        rows, blk = slice(64 * (h % 2), 64 * (h % 2) + 64), 8 + h // 2
                    halves(o_hi[rows, blk, :], o_lo[rows, blk, :], ps[rows, r % 2, 0:T]).then_inc(b_taken, 1)
                for r in range(15):
                    if r < 12:
                        soft_max(r)
                    if 1 <= r < 13:
                        soft_prob(r - 1)
                    if r >= 3:
                        soft_out(r - 3)
                dve.drain()

                bh = ba[:, :, 0:4].rearrange("p n h -> p h n")
                ah = ba[:, :, 4:8].rearrange("p n h -> p h n")
                b4 = [bt[:, j, :].rearrange("p (h n) -> p h n", n=4) for j in range(8)]
                copy(b4[0], bh)
                tt(b4[1], ah, rows2[0:64, R_DT:R_DT + 4].unsqueeze(2).to_broadcast([64, 4, 4]), ALU.add)
                dve.drain()
                stt(bt[:, 2], bt[:, 1], -1.0, bt[:, 1], ALU.mult, ALU.min).then_inc(g_lin, 1)
                dve.wait_ge(g_exp, layer + 1)
                ts(bt[:, 4], bt[:, 2], 1.0, None, ALU.add).then_inc(g_mid, 1)
                dve.drain()
                ts(bt[:, 6], bt[:, 4], -1.0, 1e-30, ALU.add, ALU.max)
                dve.drain()
                nc.vector.reciprocal(bt[:, 6], bt[:, 6])
                dve.drain()
                tt(bt[:, 6], bt[:, 6], bt[:, 2], ALU.mult)
                ts(bt[:, 1], bt[:, 1], 0.0, None, ALU.max)
                dve.drain()
                dve.wait_ge(g_ln, layer + 1)
                tt(bt[:, 6], bt[:, 6], bt[:, 5], ALU.mult)
                ts(bt[:, 0], bt[:, 0], 1.0, None, ALU.add)
                dve.drain()
                tt(bt[:, 6], bt[:, 6], bt[:, 1], ALU.add)
                nc.vector.reciprocal(beta[:], b4[0])
                dve.drain()
                stt(gdec[:], b4[6], -1.0, bt[:, 3, 0:4].unsqueeze(2).to_broadcast([64, 4, 4]), ALU.mult, ALU.mult
                    ).then_inc(g_rate, 1)
                dve.wait_ge(gd_sums, layer + 1)
                copy(gcum[:], ps[0:64, 4, 0:16].rearrange("p (a b) -> p a b", b=4))
                copy(gsuf[:], ps[0:64, 4, 16:32].rearrange("p (a b) -> p a b", b=4)).then_inc(gd_taken, 1)
                dve.wait_ge(gd_exp, layer + 1)
                tt(gexp[:], gexp[:], beta[:], ALU.mult)
                dve.drain()
                dve.wait_ge(za_ready, layer + 1)

                def over_systems(m):
                    return m.unsqueeze(1).to_broadcast([64, 8, CH])

                def per_token(t, hp, width):
                    v = t[:, 2 * hp:2 * hp + 2, :].rearrange("p h n -> p (h n)")
                    return v.unsqueeze(2).to_broadcast([64, 8, width])
                for hp in range(2):
                    w = layer * 2 + hp
                    tt(Pm[:], over_systems(m64[:, 0, :]), per_token(gdec, hp, CH), ALU.mult)
                    tt(Mm[:], over_systems(ident[0:64, 0:64]), per_token(beta, hp, CH), ALU.mult).then_inc(gd_ready, 1)
                    dve.wait_ge(gd_kk, w + 1)

                    def sums64(b):
                        return ps[0:64, b, :].rearrange("p (a c) -> p a c", c=CH)
                    tt(DT[:], sums64(4), per_token(gcum, hp, CH), ALU.subtract)
                    dve.drain()
                    ts(DT[:], DT[:], 0.0, None, ALU.min).then_inc(gd_diff, 1)
                    tt(LT[:], sums64(6), over_systems(m64[:, 2, :]), ALU.mult)
                    tt(qkT[:], sums64(7), over_systems(m64[:, 0, :]), ALU.mult)
                    dve.drain()
                    tt(LT[:], sums64(5), LT[:], ALU.mult)
                    dve.drain()
                    dve.wait_ge(gd_decay, w + 1)
                    tt(LT[:], LT[:], DT[:], ALU.mult)
                    dve.drain()

                    def half(t, g):
                        return t[:, 4 * g:4 * g + 4, :]

                    def over_half(m):
                        return m.unsqueeze(1).to_broadcast([64, 4, CH])

                    def sums_half(b, at_=0):
                        return ps[0:64, b, at_:at_ + T].rearrange("p (a c) -> p a c", c=CH)

                    def mask(lv, g):
                        return tt(half(Mm, g), half(LT, g), over_half(m64[:, 3 + lv, :]), ALU.mult)
                    for g in range(2):
                        mask(0, g).then_inc(inv_ready, 1)
                    for g in range(2):
                        dve.wait_ge(inv_p, w * 12 + g + 1)
                        tt(TU[:, g, 0], over_half(ident[0:64, 0:64]), sums_half(4 + 3 * g), ALU.subtract)
                        tt(TU[:, g, 1], over_half(ident[0:64, 0:64]), half(Mm, g), ALU.subtract)
                        dve.drain()
                        mask(1, g).then_inc(inv_ready, 1)
                    for lv in range(1, 6):
                        for g in range(2):
                            dve.wait_ge(inv_p, w * 12 + lv * 2 + g + 1)
                            copy(half(Pm, g), sums_half(4 + 3 * g)).then_inc(inv_pc, 1)
                            if lv < 5:
                                mask(lv + 1, g)
                        if lv == 1:
                            copy(kT[:], ps[0:64, 0:2, :].rearrange("p b (a c) -> p (b a) c", c=P))
                        elif lv == 2:
                            tt(kbg[:], kT[:], per_token(gexp, hp, P), ALU.mult)
                        elif lv == 3:
                            tt(vT[:], ps[0:64, 2:4, :].rearrange("p b (a c) -> p (b a) c", c=P),
                               per_token(beta, hp, P), ALU.mult)
                        elif lv == 4:
                            tt(kdec[:], kT[:], per_token(gsuf, hp, P), ALU.mult)
                        else:
                            tt(qkT[:], qkT[:], DT[:], ALU.mult)
                        dve.drain()
                        for g in range(2):
                            dve.wait_ge(inv_done, w * 10 + lv * 2 + g - 1)
                            if lv < 5:
                                two = TU[:, g].rearrange("p t a c -> p (t a) c")
                                tt(two, two, ps[0:64, 5 + g, :].rearrange("p (a c) -> p a c", c=CH), ALU.subtract
                                   ).then_inc(inv_ready, 1)
                            else:
                                tt(TU[:, g, 1], TU[:, g, 1], sums_half(5 + g, T), ALU.subtract).then_inc(inv_next, 1)
                    dve.wait_ge(uw_ready, w + 1)
                    copy(uu[:], ps[0:64, 0:2, :].rearrange("p b (a c) -> p (b a) c", c=P))
                    copy(wT[:], ps[:, 4, :].rearrange("p (a c) -> p a c", c=CH))
                    tt(qdec[:], CV[:, 2 * hp:2 * hp + 2, :].rearrange("p h (n c) -> p (h n) c", c=CH), gcb[:],
                       ALU.mult).then_inc(uw_taken, 1)
                    dve.drain()
                    for n in range(4):
                        u_n = uu[:, n:8:4, :]
                        if n:
                            dve.wait_ge(sc_w, w * 3 + n)
                            tt(vnew[:], u_n, ps[0:64, 5, 0:T].rearrange("p (a c) -> p a c", c=P), ALU.subtract
                               ).then_inc(sc_v, 1)
                        else:
                            copy(vnew[:], u_n).then_inc(sc_v, 1)
                        dve.wait_ge(sc_s, w * 4 + n + 1)
                        if n < 3:
                            for j in range(2):
                                new = ps[:, 7, j * P:j * P + P]
                                if n:
                                    ins = stt(Sst[:, j, :], Sst[:, j, :], gcb[:, 4 * j + n, CH - 1:CH], new,
                                              ALU.mult, ALU.add)
                                else:
                                    ins = copy(Sst[:, j, :], new)
                            ins.then_inc(sc_next, 1)
                            dve.drain()
                    copy(oraw[:, 2 * hp:2 * hp + 2], ps[:, 2:4, 0:T]).then_inc(go_copied, 1)
                    dve.drain()
                dve.wait_ge(go_sum, layer + 1)
                ts(ostd[:], ps[:, 4:6, :].rearrange("p b (a c) -> p (b a) c", c=T), 1.0 / P, EPS, ALU.mult, ALU.add
                   ).then_inc(go_var, 1)
                stt(oA[:], oraw[:], cols2[:, C_GDN:C_GDN + 1], za[:], ALU.mult, ALU.mult)
                dve.drain()
                dve.wait_ge(go_std, layer + 1)
                tt(oA[:], oA[:], ostd[:], ALU.mult)
                dve.drain()
                halves(o_hi[:, 0:4, :], o_lo[:, 0:4, :], oA[:]).then_inc(operand_ready, 1)

                def take_branch(i, u):
                    b = pair("w_br", u)
                    first, br, m0 = u < 2, (u // 2 + 1) % 3, 4 * (u % 2)
                    if u == 0:
                        dve.wait_ge(sums_taken, group("w_gate", layer, 12) + 2)
                    sums = ps[:, b:b + 2, :].rearrange("p b (a c) -> p (b a) c", c=T)
                    g = gate[:, 8 * br + m0:8 * br + m0 + 4, :]
                    if first:
                        tt(mrg[:, m0:m0 + 4, :], g, sums, ALU.mult).then_inc(sums_taken, 1)
                    else:
                        tt(mrt[:], g, sums, ALU.mult).then_inc(sums_taken, 1)
                        dve.drain()
                        tt(mrg[:, m0:m0 + 4, :], mrg[:, m0:m0 + 4, :], mrt[:], ALU.add)
                    dve.drain()
                    if u >= 4:
                        ins = halves(m_hi[:, m0:m0 + 4, :], m_lo[:, m0:m0 + 4, :], mrg[:, m0:m0 + 4, :])
                    if u == 5:
                        ins.then_inc(operand_ready, 1)
                each("w_br", layer, take_branch, per=8)
                add_mix = scaled_sum("w_out", False, 1.0)
                each("w_out", layer, lambda i, u: add_mix(slice(2 * u, 2 * u + 2), bank("w_out", u)), per=8)
                dve.drain()
                norm(layer * 3 + 5, LAT, l_hi[:], l_lo[:], layer * 3 + 1, LN_EPS)
                scale_residual()
                swiglu("ff2_in", layer, gs2, gp2, fh_hi, fh_lo, T, 84)
                ff_out("ff2_out")
                norm(layer * 3 + 6, LAT, l_hi[:], l_lo[:], layer * 3 + 2, LN_EPS)
                dve.drain()
                copy(small[:, 15:16], small[:, 14:15]).then_inc(layer_used, 1)


def blocks1024(w):
    return w.reshape(8, P, -1, 2, P).transpose(2, 1, 3, 0, 4).reshape(-1, P, 16, P)


def pairs1024(a, b):
    both = np.stack([a.reshape(8, P, -1, P), b.reshape(8, P, -1, P)], 0)
    return both.transpose(3, 2, 0, 1, 4).reshape(-1, P, 16, P)


def deep_blocks(w):
    return w.reshape(-1, 8, P, 4, 2, P).transpose(3, 0, 2, 4, 1, 5).reshape(-1, P, 16, P)


def ffn_out_blocks(w):
    return w.reshape(-1, 2, P, 8, P).transpose(0, 2, 1, 3, 4).reshape(-1, P, 16, P)


def branch_blocks(w):
    return w.reshape(4, P, 2, 4, P).transpose(2, 1, 3, 0, 4).reshape(-1, P, 16, P)


def columns(v):
    return v.reshape(-1, P).T


def spread(v):
    return np.broadcast_to(v.reshape(1, -1), (P, v.size))


def constants():
    i = np.arange(P)
    ident = np.eye(P)
    ones = np.ones((P, P))
    ones64 = (i[:, None] // 64 == i[None] // 64) * 1.0

    def partner(size):
        half = size // 2
        r = np.zeros((P, P))
        for m in range(P):
            if m % size < half:
                r[m + half, m] = -1.0
            else:
                r[m - half, m] = 1.0
        return r
    swap = np.zeros((P, P))
    swap[(i + 64) % P, i] = 1.0
    t = np.arange(T)
    row, col = t // 64, t % 64
    f = 10000.0 ** -((i % 16) / 16.0)
    pos = np.where((i[:, None] % 64) < 32, row[None], col[None])
    ang = pos * f[:, None]
    q, k = t[:, None], t[None]
    bandB = np.where(k // CH <= q // CH, 0.0, -1e30)
    inside = (k // CH <= q // CH) & (k // CH >= q // CH - 2)
    bandC = np.where(inside, -np.abs(q - k), -1e30)

    def rows(m):
        return m.reshape(2, P, T).transpose(1, 0, 2).reshape(P, 2 * T)
    cst = np.concatenate([ident, ones, ones64, partner(P), partner(32), swap, np.cos(ang), np.sin(ang),
                          rows(bandB), rows(bandC)], 1).astype(np.float32)
    f = 10000.0 ** -((i % 64) / 64.0)
    ang = np.stack([row[None] * f[:, None], col[None] * f[:, None]], 1)
    rope = np.stack([np.cos(ang), np.sin(ang)], 1).astype(np.float32)
    j = np.concatenate([np.arange(T) - T, np.arange(T)]).reshape(4, P).T[:, :, None]
    ctx_key = (j < 0)
    l = j + T
    fwd = np.where(ctx_key, T + t - l, np.maximum(t - j, 0))
    bwd = np.where(ctx_key, T - t + l, np.maximum(j - t, 0))
    m_f = np.where(ctx_key, 1, t >= j)
    m_b = np.where(ctx_key, 1, t <= j)
    dist = np.stack([fwd, bwd, m_f, m_b], 1).astype(np.float32)
    a, b = np.arange(CH)[:, None], np.arange(CH)[None]
    masks = [a <= b, a > b, a < b]
    for lv in range(6):
        size = 2 << lv
        masks.append((a // size == b // size) & (a % size < size // 2) & (b % size >= size // 2))
    c64 = np.stack(masks, 1).astype(np.float32)
    return cst, rope, dist, c64


def kernel(**inp):
    import concourse.bacc as bacc
    from concourse.bass_utils import run_bass_kernel_spmd

    a = {k: np.asarray(v) for k, v in inp.items()}
    f32 = np.float32
    parts = [blocks1024(a["ada_w"][l]) for l in range(2)]
    rw = a["ret_w_in"][0]
    parts += [blocks1024(rw), deep_blocks(a["ret_w_out"][0])]
    fh = FFN_B * P

    def ffn(l):
        return [pairs1024(a["ffn_w_in"][l][:, :fh], a["ffn_w_in"][l][:, fh:]), ffn_out_blocks(a["ffn_w_out"][l])]
    parts += ffn(0)
    parts += [blocks1024(a["diff_w_in"][0]), blocks1024(a["diff_w_out"][0])]
    parts += ffn(1)
    hid = FF_B * P
    for l in range(LAYERS2):
        for k in ("1", "2"):
            if k == "2":
                w = a["w_in_2"][l]
                small = np.zeros((D, 2 * P), f32)
                small[:, 0:8] = w[:, 1536:1544]
                parts.append(blocks1024(np.concatenate([w[:, :1536], w[:, 1544:], small], 1)))
                parts.append(blocks1024(a["w_gate_2"][l]))
                parts += [branch_blocks(a[f"w_br_{x}_2"][l]) for x in "bca"]
                parts.append(blocks1024(a["w_out_2"][l]))
            w = a[f"w_ff{k}_in_2"][l]
            parts.append(pairs1024(w[:, :hid], w[:, hid:]))
            parts.append(deep_blocks(a[f"w_ff{k}_out_2"][l]))
    parts.append(np.zeros((SPLIT, P, 16, P), f32))
    ws = np.concatenate(parts)
    assert ws.shape == (TILES, P, 16, P), ws.shape

    def feature_major(x):
        return x[0].T.reshape(DC, P, T).transpose(1, 0, 2)
    xt = np.concatenate([feature_major(a["ctx"]), feature_major(a["x"])], 2)
    cond = np.stack([columns(a["c_ctx"]), columns(a["c"][0])], 2).reshape(P, 16)
    col1 = np.concatenate([columns(a["ada_b"]), columns(a["ret_norm_g"]),
                           np.tile(a["diff_q_norm_g"].reshape(64, 1), (2, 1)),
                           np.tile(a["diff_k_norm_g"].reshape(64, 1), (2, 1)),
                           columns(a["diff_subln_g"]), cond], 1)
    row1 = np.concatenate([spread(a["ret_decay_logit"]), spread(a["diff_lambda"])], 1)
    col2, row2, relb = [], [], []
    t = np.arange(T)
    rel = np.clip(t[:, None] - t[None], -63, 128) + 63
    for l in range(LAYERS2):
        bi = a["b_in_2"][l]
        fm = np.concatenate([bi[:1536], bi[1544:3080], bi[3592:4232]])
        col2.append(np.concatenate([columns(a[n][l]) for n in ("ln1_g_2", "ln1_b_2", "ln2_g_2", "ln2_b_2",
                                                               "ln3_g_2", "ln3_b_2")]
                                   + [columns(fm), columns(a["b_gate_2"][l]), columns(a["conv_w_2"][l]),
                                      columns(a["gdn_norm_g_2"][l])], 1))
        row2.append(np.concatenate([spread(v) for v in (bi[3080:3592], bi[4232:4360], bi[1536:1544],
                                                        a["a_log_2"][l], a["dt_bias_2"][l], a["sinks_2"][l])], 1))
        relb.append(a["rel_bias_2"][l][:, rel].reshape(4, 2, P, T).transpose(2, 0, 1, 3))
    cst, rope, dist, c64 = constants()
    arrays = dict(ws=ws, xt=xt, col1=col1, row1=row1, col2=np.stack(col2), row2=np.stack(row2),
                  relb=np.stack(relb), cst=cst, ret_cst=rope, ret_dist=dist, c64=c64)
    arrays = {f"in_{k}": np.ascontiguousarray(v) for k, v in arrays.items()}
    nc = bacc.Bacc("TRN2", target_bir_lowering=False, num_devices=1)
    args = [nc.dram_tensor(k, v.shape, mybir.dt.from_np(v.dtype), kind="ExternalInput").ap()
            for k, v in arrays.items()]
    args.append(nc.dram_tensor("out_0", (P, DC, T), F32, kind="ExternalOutput").ap())
    build(nc, *args)
    r = run_bass_kernel_spmd(nc, [arrays], core_ids=[0])
    got = r.results[0]["out_0"]
    return got.transpose(1, 0, 2).reshape(D, T).T[None]
```
